# Optimizing a Trainium2 kernel written in Bass

```python
import jax, jax.numpy as jnp
from jax import lax
import numpy as np

D_MODEL = 1024
BATCH = 1
SEQ = 512
DEPTH = 1

CHUNK = 64
EPS = 1e-6
N_Q_HEADS = 16
N_KV_HEADS = 2
HEAD_DIM = 64
ATTN_WIDTH = N_Q_HEADS * HEAD_DIM
KV_WIDTH = N_KV_HEADS * HEAD_DIM
Q_PER_KV = N_Q_HEADS // N_KV_HEADS
WINDOW = 128
WINDOW_CHUNKS = WINDOW // CHUNK
BAND = WINDOW_CHUNKS * CHUNK
N_BUCKETS = 32
MAX_DISTANCE = 128
RWKV_HEAD = 64
RWKV_HEADS = D_MODEL // RWKV_HEAD
RWKV_WIDTH = RWKV_HEADS * RWKV_HEAD
DECAY_LORA = 64
AAA_LORA = 64
GATE_LORA = 160
GN_EPS = 64e-5
N_BRANCH = 2
BRANCH_WIDTH = ATTN_WIDTH
D_FF = 4 * D_MODEL

IN_SIZES = [ATTN_WIDTH, KV_WIDTH, KV_WIDTH,
            RWKV_WIDTH, RWKV_WIDTH, RWKV_WIDTH,
            DECAY_LORA, AAA_LORA, GATE_LORA,
            N_BRANCH * D_MODEL]
IN_COLS = sum(IN_SIZES)
SHIFT_COLS = 3 * RWKV_WIDTH + DECAY_LORA + AAA_LORA + GATE_LORA

kernel_name = "hybrid_swa_sink_rwkv7_gated_block"

def rms_norm(x, g):
    x32 = x.astype(jnp.float32)
    y = x32 * lax.rsqrt(jnp.mean(x32 * x32, axis=-1, keepdims=True) + EPS)
    return (y * g.astype(jnp.float32)).astype(x.dtype)

def t5_buckets(q_len, k_len, offset):
    q = np.arange(q_len)[:, None]
    k = np.arange(k_len)[None, :]
    rel = k - offset - q
    nb = N_BUCKETS // 2
    max_exact = nb // 2
    ret = (rel > 0).astype(np.int32) * nb
    n = np.abs(rel)
    ratio = np.maximum(n, 1).astype(np.float32) / np.float32(max_exact)
    large = max_exact + (np.log(ratio) / np.float32(np.log(MAX_DISTANCE / max_exact))
                         * (nb - max_exact)).astype(np.int32)
    large = np.minimum(large, nb - 1)
    return (ret + np.where(n < max_exact, n, large)).astype(np.int32)

def band_keys(z, n_chunks):
    pad = [(0, 0)] * z.ndim
    parts = []
    for j in range(WINDOW_CHUNKS - 1, -1, -1):
        pad[1] = (j, 0)
        parts.append(jnp.pad(z, pad)[:, :n_chunks])
    return jnp.concatenate(parts, axis=2)

def sink_window_attention(q, k, v, sinks, rel_bias):
    B, T, _ = q.shape
    nc = T // CHUNK
    qc = q.reshape(B, nc, CHUNK, N_KV_HEADS, Q_PER_KV, HEAD_DIM)
    kb = band_keys(k.reshape(B, nc, CHUNK, N_KV_HEADS, HEAD_DIM), nc)
    vb = band_keys(v.reshape(B, nc, CHUNK, N_KV_HEADS, HEAD_DIM), nc)
    logits = jnp.einsum('bcqhgd,bcshd->bchgqs', qc, kb).astype(jnp.float32) * (HEAD_DIM ** -0.5)
    bucket = t5_buckets(CHUNK, BAND, (WINDOW_CHUNKS - 1) * CHUNK)
    bias = rel_bias.astype(jnp.float32)[bucket]
    bias = bias.transpose(2, 0, 1).reshape(N_KV_HEADS, Q_PER_KV, CHUNK, BAND)
    chunk_idx = jnp.arange(nc)[:, None]
    slot = jnp.arange(BAND)[None, :] // CHUNK
    valid = (chunk_idx - (WINDOW_CHUNKS - 1) + slot) >= 0
    logits = jnp.where(valid[None, :, None, None, None, :], logits + bias, -1e30)
    sink = sinks.astype(jnp.float32).reshape(N_KV_HEADS, Q_PER_KV)[None, None, :, :, None, None]
    m = jnp.maximum(jnp.max(logits, axis=-1, keepdims=True), sink)
    p = jnp.exp(logits - m)
    probs = p / (jnp.sum(p, axis=-1, keepdims=True) + jnp.exp(sink - m))
    out = jnp.einsum('bchgqs,bcshd->bcqhgd', probs.astype(vb.dtype), vb)
    return out.reshape(B, T, ATTN_WIDTH)

def rwkv7_time_mix(r, k, v, wd, ad, gd, w0, w_decay_up, a0, w_aaa_up, w_gate_up,
                   k_k, k_a, r_k, ln_x_w, ln_x_b):
    f32 = jnp.float32
    r, k, v, wd, ad, gd = (z.astype(f32) for z in (r, k, v, wd, ad, gd))
    B, T, _ = r.shape
    heads = lambda z: z.reshape(B, T, RWKV_HEADS, RWKV_HEAD)
    w_log = -jax.nn.softplus(-(w0 + jnp.tanh(wd) @ w_decay_up)) - 0.5
    decay = jnp.exp(-jnp.exp(w_log))
    a = jax.nn.sigmoid(a0 + ad @ w_aaa_up)
    g = jax.nn.sigmoid(gd) @ w_gate_up
    kk = heads(k * k_k)
    kk = kk / jnp.maximum(jnp.sqrt(jnp.sum(kk * kk, axis=-1, keepdims=True)), 1e-12)
    k = k * (1.0 + (a - 1.0) * k_a)

    def step(S, inp):
        r_t, w_t, k_t, v_t, kk_t, a_t = inp
        s_kk = jnp.einsum('bhij,bhj->bhi', S, -kk_t)
        S = (S * w_t[:, :, None, :]
             + s_kk[..., :, None] * (kk_t * a_t)[:, :, None, :]
             + v_t[..., :, None] * k_t[:, :, None, :])
        return S, jnp.einsum('bhij,bhj->bhi', S, r_t)

    tm = lambda z: jnp.moveaxis(z, 1, 0)
    xs = (tm(heads(r)), tm(heads(decay)), tm(heads(k)), tm(heads(v)), tm(kk), tm(heads(a)))
    S0 = jnp.zeros((B, RWKV_HEADS, RWKV_HEAD, RWKV_HEAD), f32)
    _, y = lax.scan(step, S0, xs)
    y = jnp.moveaxis(y, 0, 1)
    mu = jnp.mean(y, axis=-1, keepdims=True)
    var = jnp.mean(jnp.square(y - mu), axis=-1, keepdims=True)
    y = ((y - mu) * lax.rsqrt(var + GN_EPS)).reshape(B, T, RWKV_WIDTH) * ln_x_w + ln_x_b
    bonus = jnp.sum(heads(r) * heads(k) * r_k, axis=-1, keepdims=True) * heads(v)
    return (y + bonus.reshape(B, T, RWKV_WIDTH)) * g

def hybrid_layer(x, w_in, rwkv_shift, pre_mix_g, post_mix_g, pre_ffn_g, post_ffn_g,
                 attn_sinks, rel_bias, w0, w_decay_up, a0, w_aaa_up, w_gate_up,
                 k_k, k_a, r_k, ln_x_w, ln_x_b, gate_bias, w_branch, w_out,
                 w_ff_up, w_ff_down):
    B, T, _ = x.shape
    h = rms_norm(x, pre_mix_g)
    proj = h @ w_in
    split_at = np.cumsum(IN_SIZES)[:-1].tolist()
    attn_cols = split_at[2]
    gate_col = split_at[-1]
    q, k, v = jnp.split(proj[..., :attn_cols], [ATTN_WIDTH, ATTN_WIDTH + KV_WIDTH], axis=-1)
    z = proj[..., attn_cols:gate_col]
    z_prev = jnp.pad(z, ((0, 0), (1, 0), (0, 0)))[:, :-1]
    z = z + (z_prev - z) * rwkv_shift
    rr, kr, vr, wd, ad, gd = jnp.split(
        z, np.cumsum([RWKV_WIDTH, RWKV_WIDTH, RWKV_WIDTH, DECAY_LORA, AAA_LORA]).tolist(), axis=-1)
    gates = jax.nn.sigmoid(proj[..., gate_col:].reshape(B, T, N_BRANCH, D_MODEL) + gate_bias)

    y_attn = sink_window_attention(q, k, v, attn_sinks, rel_bias)
    y_rwkv = rwkv7_time_mix(rr, kr, vr, wd, ad, gd, w0, w_decay_up, a0, w_aaa_up, w_gate_up,
                            k_k, k_a, r_k, ln_x_w, ln_x_b).astype(y_attn.dtype)
    merged = (gates[:, :, 0] * (y_attn @ w_branch[0])
              + gates[:, :, 1] * (y_rwkv @ w_branch[1]))
    x = x + rms_norm((merged @ w_out).astype(x.dtype), post_mix_g)

    hf = rms_norm(x, pre_ffn_g)
    ff = jnp.square(jax.nn.relu(hf @ w_ff_up)) @ w_ff_down
    return x + rms_norm(ff.astype(x.dtype), post_ffn_g)

def setup_inputs(seed: int = 0) -> dict:
    key = jax.random.key(seed)
    ks = iter(jax.random.split(key, 32))
    L = DEPTH
    nrm = lambda shape, s: jax.random.normal(next(ks), shape, jnp.float32) * s
    gain = lambda shape: 1.0 + nrm(shape, 0.1)
    uni = lambda shape, lo, hi: jax.random.uniform(next(ks), shape, jnp.float32, lo, hi)
    return {
        "x": nrm((BATCH, SEQ, D_MODEL), 1.0),
        "w_in": nrm((L, D_MODEL, IN_COLS), D_MODEL ** -0.5),
        "rwkv_shift": uni((L, SHIFT_COLS), 0.0, 1.0),
        "pre_mix_g": gain((L, D_MODEL)),
        "post_mix_g": gain((L, D_MODEL)),
        "pre_ffn_g": gain((L, D_MODEL)),
        "post_ffn_g": gain((L, D_MODEL)),
        "attn_sinks": nrm((L, N_Q_HEADS), 0.5),
        "rel_bias": nrm((N_BUCKETS, N_Q_HEADS), 0.5),
        "w0": uni((L, RWKV_WIDTH), -6.0, 1.0),
        "w_decay_up": nrm((L, DECAY_LORA, RWKV_WIDTH), 0.5 * DECAY_LORA ** -0.5),
        "a0": nrm((L, RWKV_WIDTH), 0.5),
        "w_aaa_up": nrm((L, AAA_LORA, RWKV_WIDTH), 0.5 * AAA_LORA ** -0.5),
        "w_gate_up": nrm((L, GATE_LORA, RWKV_WIDTH), GATE_LORA ** -0.5),
        "k_k": 0.85 + nrm((L, RWKV_WIDTH), 0.05),
        "k_a": 1.0 + nrm((L, RWKV_WIDTH), 0.05),
        "r_k": nrm((L, RWKV_HEADS, RWKV_HEAD), 0.1),
        "ln_x_w": gain((L, RWKV_WIDTH)),
        "ln_x_b": nrm((L, RWKV_WIDTH), 0.01),
        "gate_bias": nrm((L, N_BRANCH, D_MODEL), 0.1),
        "w_branch": nrm((L, N_BRANCH, BRANCH_WIDTH, D_MODEL), BRANCH_WIDTH ** -0.5),
        "w_out": nrm((L, D_MODEL, D_MODEL), D_MODEL ** -0.5),
        "w_ff_up": nrm((L, D_MODEL, D_FF), D_MODEL ** -0.5),
        "w_ff_down": nrm((L, D_FF, D_MODEL), D_FF ** -0.5),
    }

def reference(x, w_in, rwkv_shift, pre_mix_g, post_mix_g, pre_ffn_g, post_ffn_g,
              attn_sinks, rel_bias, w0, w_decay_up, a0, w_aaa_up, w_gate_up,
              k_k, k_a, r_k, ln_x_w, ln_x_b, gate_bias, w_branch, w_out,
              w_ff_up, w_ff_down):
    for l in range(DEPTH):
        x = hybrid_layer(x, w_in[l], rwkv_shift[l], pre_mix_g[l], post_mix_g[l],
                         pre_ffn_g[l], post_ffn_g[l], attn_sinks[l], rel_bias,
                         w0[l], w_decay_up[l], a0[l], w_aaa_up[l], w_gate_up[l],
                         k_k[l], k_a[l], r_k[l], ln_x_w[l], ln_x_b[l], gate_bias[l],
                         w_branch[l], w_out[l], w_ff_up[l], w_ff_down[l])
    return x


_drawn_inputs = setup_inputs


def setup_inputs(seed=0):
    import zlib

    import numpy as np

    out = dict(_drawn_inputs(seed))
    spreads = {}
    factors = {'attn_sinks': 31.565, 'w_decay_up': 3.261, 'ln_x_b': 8.0}
    for name, (base, spread) in spreads.items():
        noise = np.random.default_rng([zlib.crc32(name.encode()), seed]).standard_normal(out[name].shape)
        drawn = base * np.exp(spread * noise) if base else spread * noise
        out[name] = __import__('jax').numpy.asarray(drawn.astype(out[name].dtype))
    for name, factor in factors.items():
        out[name] = (out[name] * factor).astype(out[name].dtype)
    return out
```

```python
import math

import concourse.bass as bass
import numpy as np
from concourse import mybir
from concourse.alu_op_type import AluOpType as ALU

F32 = mybir.dt.float32
F32R = mybir.dt.float32r
ACT = mybir.ActivationFunctionType
AX = mybir.AxisListType.X

P = 128
T = 512
D = 1024
KC = D // P
CH = 64
NCH = T // CH
HD = 64
DFF = 4 * D
KB = DFF // D
EPS = 1e-6
GN_EPS = 64e-5
BETA = 192
C_DEC = 0.5 * math.exp(-0.5)

Q0, K0, V0 = 0, D, D + P
R0, RK0, RV0 = D + 2 * P, 2 * D + 2 * P, 3 * D + 2 * P
L0 = 4 * D + 2 * P
G0 = L0 + 64 + 64 + 160

NAMES = ["pre_mix", "post_mix", "pre_ffn", "post_ffn", "mu_r", "mu_k", "mu_v", "w0", "a0",
         "k_k", "k_a", "r_k", "ln_w", "ln_b", "gb0", "gb1"]
COL = {n: 8 * i for i, n in enumerate(NAMES)}
MU_L = 8 * len(NAMES)
NCOL = MU_L + 3
OM_R, OM_K, OM_V, OM_L = NCOL, NCOL + 8, NCOL + 16, NCOL + 24
H_W0, H_A0, H_KA, OH_KA, N_KK, H_GB0, H_GB1 = (NCOL + 27 + 8 * i for i in range(7))
NCOLS = NCOL + 27 + 56

N_L, N_K, N_V, N_Q = 0, 3, 4, 5
N_G0 = 13
N_B0 = 21
N_PAIR = 29
N_G1 = 53
N_B1 = 61
N_OUT = 69
N_UP = 77
N_DOWN = 109
N_SLABS = 141
LEVELS = [2, 4, 8, 16, 32]
E_G0, E_B0, E_G1, E_B1, E_OUT, E_UP, E_DOWN, E_ALL = 10, 18, 26, 34, 42, 50, 82, 90
N1, N2, N3, N4 = 0, 8, 16, 24
SP_H, SP_Y, SP_M, SP_F = 0, 8, 16, 24


def build(nc, xT, w_in, cols, sinks, onehot, rel_bias, wdec, waaa, wgate, w_br, w_out, w_up, w_down, out):
    sems = {}

    def S(name):
        if name not in sems:
            sems[name] = nc.alloc_semaphore(name)
        return sems[name]

    base = (nc.sbuf_base + 63) // 64 * 64

    def at(name, shape, kib, dt=F32):
        kib = kib if kib < 10 else kib - 0.5
        return nc.alloc_sbuf_tensor_at(name, [P] + shape, dt, offset=base + int(kib * 1024))

    ident = at("ident", [P], 0)
    ones = at("ones", [P], 0.5)
    bdones = at("bdones", [P], 1)
    m_strict = at("m_strict", [P], 1.5)
    m_incl = at("m_incl", [P], 2)
    m_1 = at("m_1", [P], 2.5)
    m_1t = at("m_1t", [P], 3)
    m_lev = [at(f"m_lev{b}", [P], 3.5 + 0.5 * i) for i, b in enumerate(LEVELS)]
    scanm = at("scanm", [T], 6)
    par = at("par", [NCOLS], 8)
    sinkT = at("sinkT", [8], 9)
    lnw_bc = None
    wc = at("wc", [KC, NCH], 9.25)
    raw = at("raw", [2, KC, P], 10)
    whi = at("whi", [2, KC, P], 18, F32R)
    wlo = at("wlo", [2, KC, P], 26, F32R)
    r1h, r1l = at("r1h", [KC, T], 34, F32R), at("r1l", [KC, T], 50, F32R)
    r2h, r2l = at("r2h", [KC, T], 66, F32R), at("r2l", [KC, T], 82, F32R)
    xs = at("xs", [KC, T], 98)
    q = at("q", [4, NCH, 2, CH], 98)
    kb = at("kb", [2, 2, 2, 4, P], 114)
    v1 = at("v1", [4, P], 130)
    v2 = at("v2", [4, P], 132)
    bias = at("bias", [8, 192], 134)
    lg = at("lg", [2, 8, P], 146)
    pT = at("pT", [2, 8, P], 154)
    kT = at("kT", [T], 162)
    vT = at("vT", [T], 164)
    m0 = at("m0", [KC, T], 166)
    beta = at("beta", [BETA], 182)
    oneh = at("oneh", [BETA], 183)
    relb = at("relb", [16], 184)
    asm = at("asm", [2, 5, 8], 185)
    sqt = at("sqt", [2, T], 194)
    hx = at("hx", [2, T], 198)
    rst = at("rst", [2, T], 202)
    tl = at("tl", [T], 202)
    sg = at("sg", [2, T], 204)
    ar = at("ar", [2, KC, T], 66)
    bt = at("bt", [KC, T], 98)
    kt = at("kt", [KC, T], 114)
    vb = at("vb", [KC, T], 130)
    bv = at("bv", [KC, T], 146)
    wl = at("wl", [2, 2, P], 162)
    tmp = {n: at("t_" + n, [T], 164 + 2 * i) for i, n in enumerate(
        ["kS", "rS", "tw", "ld", "cum", "cx", "ta", "t", "kp", "aa", "eW", "eWi", "eWx", "b0",
         "sq", "ssm", "nrm", "inv", "p"])}
    t1 = at("t1", [KC, T], 164)
    U2 = {}
    for i, n in enumerate(["aab", "aak", "arb", "ark", "X", "XT", "Qs", "AI"]):
        U2[n] = [at(f"u_{n}{h}", [4, P], 34 + 2 * (2 * i + h)) for h in range(2)]
    for i, n in enumerate(["BDa", "BDr", "BDb", "BDk", "VD", "btok", "ktok"]):
        U2[n] = [at(f"u_{n}{h}", [4, P], 164 + 2 * (2 * i + h)) for h in range(2)]
    for i, n in enumerate(["Vc", "G", "U", "Y", "Yt", "St"]):
        U2[n] = [at(f"u_{n}{h}", [4, HD], 192 + 2 * i + h) for h in range(2)]
    gn = at("gn", [2, 4, 4], 162)
    wg = at("wg", [2, D], 98)
    m0b = at("m0b", [KC, T], 106)
    t1b = at("t1b", [KC, T], 122)
    mix = at("mix", [KC, T], 162)
    xr = at("xr", [KC, T], 138)
    fh = at("fh", [KB * KC, T], 66, F32R)
    fl = at("fl", [KB * KC, T], 130, F32R)
    ob = at("ob", [KC, T], 34)
    x1 = at("x1", [KC, T], 50)

    m0_d = nc.dram_tensor("m0_d", [P, KC * T], F32, kind="Internal").ap()
    t1_d = nc.dram_tensor("t1_d", [P, KC * T], F32, kind="Internal").ap()
    x1_d = nc.dram_tensor("x1_d", [P, KC * T], F32, kind="Internal").ap()
    beta_t = nc.dram_tensor("beta_d", [16, CH, BETA], F32, kind="Internal")
    beta_d = beta_t.ap()

    B = [nc.alloc_psum_tensor(f"bank{i}", [P, T], F32) for i in range(8)]

    def slabs(w):
        return w.rearrange("(kc p) n -> p kc n", p=P)

    win_s, wout_s, wup_s = slabs(w_in), slabs(w_out), slabs(w_up)
    wbr_s = [slabs(w_br[0]), slabs(w_br[1])]
    wdn_s = [slabs(w_down[D * b:D * (b + 1), :]) for b in range(KB)]

    def col(name, m):
        c = COL[name] if name in COL else name
        return par[:, c + m:c + m + 1] if isinstance(m, int) else par[:, bass.ds(c + m, 1)]

    def pcol(c0, m):
        return par[:, c0 + m:c0 + m + 1] if isinstance(m, int) else par[:, bass.ds(c0 + m, 1)]

    def flat(t):
        return t[:].rearrange("p a b -> p (a b)")

    def bc2(ap):
        return ap.unsqueeze(2).to_broadcast([P, 4, 2, CH])

    def mask4(t):
        return t[:].rearrange("p (e t) -> p e t", e=2).unsqueeze(1).to_broadcast([P, 4, 2, CH])

    def mask4f(t):
        return t[:].unsqueeze(1).to_broadcast([P, 4, P])

    def v4(bank):
        return bank[:].rearrange("p (m n) -> p m n", m=4)

    block = nc.Block()
    block.__enter__()

    @block.sync
    def _(sp):
        def slab(n, slot, count, src):
            if not isinstance(n, int) or n >= 2:
                sp.wait_ge(S("w_split"), n - 1)
            sp.dma_start(raw[:, slot, :, :], src).then_inc(S(f"w_raw{slot}"), 16)

        sp.dma_start(xs[:], xT).then_inc(S("x_in"), 16)
        sp.dma_start(par[:, 0:NCOL], cols).then_inc(S("par_in"), 16)
        for n in range(13):
            c0 = ([L0, L0 + P, L0 + 2 * P, K0, V0] + [Q0 + P * j for j in range(8)])[n]
            slab(n, n % 2, n // 2, win_s[:, :, c0:c0 + P])
            if n == 1:
                sp.dma_start(sinkT[:], sinks).then_inc(S("tab_in"), 16)
                sp.dma_start(oneh[0:32, :], onehot).then_inc(S("tab_in"), 16)
                sp.dma_start(relb[0:32, :], rel_bias).then_inc(S("tab_in"), 16)

        def tiles(n0, src, c0):
            with sp.Fori(0, 4) as i:
                for h in range(2):
                    slab(2 * i + (n0 + h), (n0 + h) % 2, None, src[:, :, bass.ds(i * (2 * P) + (c0 + P * h), P)])

        tiles(N_G0, win_s, G0)
        tiles(N_B0, wbr_s[0], 0)
        sp.wait_ge(S("wl_zero"), 1)
        sp.wait_ge(S("tile_ev"), E_G1)
        with sp.Fori(0, 4) as i:
            for h in range(2):
                sp.wait_ge(S("a_mm"), 2 * i + (h + 1))
                sp.dma_start(wl[0:64, h, 0, :], wdec[:, bass.ds(i * (2 * P) + P * h, P)]).then_inc(S(f"wl{h}"), 16)
                sp.dma_start(wl[64:128, h, 1, :], waaa[:, bass.ds(i * (2 * P) + P * h, P)]).then_inc(S(f"wl{h}"), 16)
                for j, c0 in enumerate((RK0, R0, RV0)):
                    slab(6 * i + (N_PAIR + 3 * h + j), (N_PAIR + 3 * h + j) % 2, None,
                         win_s[:, :, bass.ds(i * (2 * P) + (c0 + P * h), P)])
        tiles(N_G1, win_s, G0 + D)
        tiles(N_B1, wbr_s[1], 0)
        tiles(N_OUT, wout_s, 0)
        with sp.Fori(0, 16) as i:
            for h in range(2):
                slab(2 * i + (N_UP + h), (N_UP + h) % 2, None, wup_s[:, :, bass.ds(i * (2 * P) + P * h, P)])
        with sp.Fori(0, 8) as j:
            for b in range(KB):
                slab(4 * j + (N_DOWN + b), (N_DOWN + b) % 2, None, wdn_s[b][:, :, bass.ds(j * P, P)])
        sp.wait_ge(S("o_ready"), 8)
        sp.dma_start(out, ob[:]).then_inc(S("out_done"), 16)
        sp.wait_ge(S("out_done"), 16)

    @block.gpsimd
    def _(pool):
        ms = nc.gpsimd.memset
        for t, v in ((ident, 0.0), (ones, 1.0), (bdones, 1.0), (m_strict, 1.0), (m_incl, 1.0), (scanm, 1.0),
                     (m_1, 1.0), (m_1t, 1.0), *((m, 1.0) for m in m_lev)):
            ms(t[:], v).then_inc(S("set"), 1)
        pool.wait_ge(S("set"), 8 + len(LEVELS))

        def split(n, slot, count):
            pool.wait_ge(S(f"w_raw{slot}"), count)
            if not isinstance(n, int) or n >= 2:
                pool.wait_ge(S("slab_mm"), n - 1)
            pool.sem_inc(S("slab_go"), 1)
            nc.gpsimd.tensor_copy(whi[:, slot, :, :], raw[:, slot, :, :]).then_inc(S("w_hi"), 1)
            pool.wait_ge(S("w_hi"), n + 1)
            nc.gpsimd.tensor_tensor(wlo[:, slot, :, :], raw[:, slot, :, :], whi[:, slot, :, :].bitcast(F32),
                                    ALU.subtract).then_inc(S("w_split"), 1)

        sel = nc.gpsimd.affine_select

        def keep(view, base_, pattern, mult, op=ALU.is_ge, fill=0.0):
            return sel(out=view, in_=view, compare_op=op, fill=fill, base=base_, pattern=pattern,
                       channel_multiplier=mult)

        keep(ident[:], 0, [[-1, P]], 1, ALU.not_equal, 1.0).then_inc(S("ident"), 1)
        keep(scanm[:].rearrange("p (c t) -> p c t", c=NCH), 0, [[0, NCH], [1, CH]], 0,
             ALU.not_equal, 0.0).then_inc(S("masks"), 1)
        nm = [1]

        def step(ins):
            ins.then_inc(S("masks"), 1)
            nm[0] += 1
            pool.wait_ge(S("masks"), nm[0])

        def blocks(m, b):
            v = m[:].rearrange("p (n r) -> p n r", r=b)
            step(keep(v, 0, [[-b, P // b], [0, b]], 1))
            step(keep(v, b - 1, [[b, P // b], [0, b]], -1))

        blocks(bdones, CH)
        blocks(m_strict, CH)
        step(keep(m_strict[:], -1, [[1, P]], -1))
        blocks(m_incl, CH)
        step(keep(m_incl[:], 0, [[1, P]], -1))
        blocks(m_1, 2)
        step(keep(m_1[:], 0, [[-1, P]], 1))
        blocks(m_1t, 2)
        step(keep(m_1t[:], 0, [[1, P]], -1))
        for m, b in zip(m_lev, LEVELS):
            blocks(m, 2 * b)
            v = m[:].rearrange("p (n r) -> p n r", r=2 * b)
            step(keep(v, -b, [[-2 * b, P // (2 * b)], [0, 2 * b]], 1))
            step(keep(v, b - 1, [[0, P // (2 * b)], [-1, 2 * b]], 0))

        for n in range(3):
            split(n, n % 2, 16 * (n // 2 + 1))
        with pool.Fori(0, 30) as i:
            for h in range(2):
                split(2 * i + (3 + h), (3 + h) % 2, i * 16 + 16 * ((3 + h) // 2 + 1))

        pool.wait_ge(S("tile_ev"), E_B1)
        pool.wait_ge(S("spilled"), 32)
        with pool.Fori(0, NCH) as c:
            for h in range(2):
                pool.wait_ge(S(f"dS_mm{h}"), c + 1)
                pool.sem_inc(S("bd_go"), 1)
                tk = bass.ds(c * CH, CH)
                for n, src in (("BDb", bt), ("BDk", kt), ("BDa", ar[:, 0]), ("BDr", ar[:, 1])):
                    nc.gpsimd.tensor_tensor(U2[n][h][:].rearrange("p m (e t) -> p m e t", e=2),
                                            bc2(src[:, 4 * h:4 * h + 4, tk]), mask4(bdones), ALU.mult) \
                        .then_inc(S(f"bd{h}"), 1)
                nc.gpsimd.tensor_copy(U2["VD"][h][:].rearrange("p m (e t) -> p m e t", e=2),
                                      bc2(vb[:, 4 * h:4 * h + 4, tk])).then_inc(S(f"bd{h}"), 1)
        with pool.Fori(0, 39) as i:
            for h in range(2):
                split(2 * i + (63 + h), (63 + h) % 2, i * 16 + 16 * ((63 + h) // 2 + 1))

    @block.tensor
    def _(pe):
        mm = nc.tensor.matmul

        for n_ in ("w_mm", "a_mm", "ss_mm", "bon_mm", "dS_mm0", "dS_mm1"):
            pe.sem_inc(S(n_), 1)

        def slab_mm(n, slot, bank, hi, lo, M=P, first=True, last=True, kc0=0):
            pe.wait_ge(S("w_split"), n + 1)
            for kc in range(KC):
                for k, (w, x) in enumerate(((whi, hi), (whi, lo), (wlo, hi))):
                    r = mm(bank[0:M, :], w[:, slot, kc, 0:M], x[:, kc0 + kc, :],
                           start=(first and kc == 0 and k == 0), stop=(last and kc == KC - 1 and k == 2))
            return r

        def rms(norm, bank):
            for kc in range(KC):
                pe.wait_ge(S("rms_sq"), norm + kc + 1)
                mm(bank[:], ones[:], sqt[:, kc % 2, :], start=(kc == 0), stop=(kc == KC - 1)) \
                    .then_inc(S("rms_mm"), 1)

        pe.wait_ge(S("set"), 8 + len(LEVELS))
        rms(N1, B[7])

        pe.wait_ge(S("tab_in"), 48)
        mm(B[6][0:16, 0:BETA], relb[0:32, :], oneh[0:32, :], start=True, stop=True).then_inc(S("small_mm"), 1)
        pe.wait_ge(S("x_lo"), SP_H + 8)
        for n in range(13):
            if 2 <= n < 5:
                pe.wait_ge(S("lo_sh"), n - 1)
            elif n >= 5:
                pe.wait_ge(S("tile_ev"), n - 4)
            slab_mm(n, n % 2, B[n % 2], r1h, r1l, M=32 if n == 2 else P).then_inc(S("slab_mm"), 1)
            if n == 5:
                pe.wait_ge(S("vT"), 1)
                pe.wait_ge(S("ident"), 1)
                for t in range(4):
                    r = nc.tensor.transpose(B[2][:, P * t:P * t + P], vT[:, P * t:P * t + P], ident[:])
                r.then_inc(S("small_mm"), 1)

        def tiles(n0, hi, lo, ev):
            with pe.Fori(0, 4) as i:
                for h in range(2):
                    pe.wait_ge(S("tile_ev"), 2 * i + (ev + h - 1))
                    slab_mm(2 * i + (n0 + h), (n0 + h) % 2, B[h], hi, lo).then_inc(S("slab_mm"), 1)

        pe.wait_ge(S("tile_ev"), 10)
        tiles(N_G0, r1h, r1l, E_G0)

        def scores(c):
            o, t = c % 2, c // 2
            if c == 0:
                pe.wait_ge(S("kb_in"), 16 * 12)
                pe.wait_ge(S("tile_ev"), 10)
            b0 = 2 + 2 * (c % 2)
            if c >= 2:
                pe.wait_ge(S("at_lg"), 2 * (c - 1))
            for j in range(4):
                r = mm(B[b0 + j // 2][:].rearrange("p (a n) -> p a n", a=2)[:, j % 2, :],
                       q[:, j, c, :, :].rearrange("p e t -> p (e t)"),
                       kb[:, o, j // 2, :, t, :], start=True, stop=True)
            r.then_inc(S("at_sc"), 1)

        def probs_values(c):
            pe.wait_ge(S("at_p"), c + 1)
            for g in range(8):
                r = nc.tensor.transpose(B[6 + g // 4][:, P * (g % 4):P * (g % 4) + P], lg[:, c % 2, g, :], ident[:])
            r.then_inc(S("at_tr"), 1)
            pe.wait_ge(S("at_pT"), 2 * c + 2)
            if c >= 1:
                pe.wait_ge(S("at_lo"), c)
            vv = (v2, v1)[c % 2]
            for g in range(2):
                for p in range(2):
                    r = mm(B[0][64 * p:64 * p + 64, 256 * g:256 * g + 256],
                           vv[:, c // 2, 64 * g:64 * g + 64],
                           pT[:, c % 2, :, :].rearrange("k (j p) q -> k j p q", p=2)[:, 2 * g:2 * g + 2, p, :],
                           start=True, stop=True)
            r.then_inc(S("at_o"), 1)

        pe.wait_ge(S("tile_ev"), E_B0)
        pe.wait_ge(S("v_ready"), 3)
        pe.wait_ge(S("beta_ev"), 1)
        scores(0)
        for c in range(NCH):
            if c + 1 < NCH:
                scores(c + 1)
            probs_values(c)
        pe.wait_ge(S("at_lo"), NCH)
        tiles(N_B0, r2h, r2l, E_B0)

        pe.wait_ge(S("tile_ev"), E_G1)
        pe.wait_ge(S("masks"), 1 + 2 + 3 + 3 + 3 + 3 + 4 * len(LEVELS))
        with pe.Fori(0, 4) as i:
            for h in range(2):
                m = 2 * i + h
                n = 6 * i + (N_PAIR + 3 * h)
                s0 = (N_PAIR + 3 * h) % 2
                pe.wait_ge(S("k_sh"), m + 1)
                slab_mm(n, s0, B[0], r1h, r1l).then_inc(S("slab_mm"), 1)
                pe.wait_ge(S(f"wl{h}"), i * 32 + 32)
                pe.wait_ge(S("tw"), m + 1)
                mm(B[1][:], wl[:, h, 0, :], tl[:], start=True, stop=True).then_inc(S("w_mm"), 1)
                pe.wait_ge(S("ta"), m + 1)
                mm(B[2][:], wl[:, h, 1, :], tl[:], start=True, stop=True).then_inc(S("a_mm"), 1)
                pe.wait_ge(S("r_sh"), m + 1)
                slab_mm(n + 1, (s0 + 1) % 2, B[3], r1h, r1l).then_inc(S("slab_mm"), 1)
                pe.wait_ge(S("sq"), m + 2)
                pe.wait_ge(S("ssm"), m + 1)
                mm(B[4][:], bdones[:], tmp["sq"][:], start=True, stop=True).then_inc(S("ss_mm"), 1)
                pe.wait_ge(S("v_sh"), m + 1)
                slab_mm(n + 2, s0, B[5], r1h, r1l).then_inc(S("slab_mm"), 1)
                pe.wait_ge(S("p"), m + 2)
                pe.wait_ge(S("bv"), m + 1)
                mm(B[6][:], bdones[:], tmp["p"][:], start=True, stop=True).then_inc(S("bon_mm"), 1)

        pe.wait_ge(S("k_sh"), 9)
        pe.wait_ge(S("tw"), 9)
        tiles(N_G1, r1h, r1l, E_G1)

        pe.wait_ge(S("tile_ev"), E_B1)
        pe.wait_ge(S("bv"), 9)
        pe.wait_ge(S("st_zero"), 2)
        with pe.Fori(0, NCH) as c:
            tk = bass.ds(c * CH, CH)
            tr = nc.tensor.transpose

            def each(h, body):
                for m in range(4):
                    r = body(m)
                return r

            def out4(bank, m):
                return v4(bank)[:, m, :]

            for h in range(2):
                b = B[4 * h:4 * h + 4]
                pe.wait_ge(S(f"bd{h}"), c * 5 + 5)
                pe.wait_ge(S(f"y_read{h}"), c + 1)
                for n, k in (("BDb", 0), ("BDk", 1)):
                    for m in range(4):
                        r = mm(v4(b[k])[:, m, :].rearrange("p (x t) -> p x t", x=2), U2[n][h][:, m, :],
                               ar[:, :, 4 * h + m, tk], start=True, stop=True)
                    r.then_inc(S(f"sc_mm{h}"), 1)
            for h in range(2):
                b = B[4 * h:4 * h + 4]
                pe.wait_ge(S(f"sc_ev{h}"), c * 5 + 2)
                each(h, lambda m: tr(out4(b[0], m), U2["BDb"][h][:, m, :], ident[:])).then_inc(S(f"tok_mm{h}"), 1)
                pe.wait_ge(S(f"sc_ev{h}"), c * 5 + 5)
                each(h, lambda m: tr(out4(b[2], m), U2["AI"][h][:, m, :], ident[:])).then_inc(S(f"ai_mm{h}"), 1)
                each(h, lambda m: tr(out4(b[1], m), U2["BDk"][h][:, m, :], ident[:])).then_inc(S(f"tok_mm{h}"), 1)
                each(h, lambda m: tr(out4(b[3], m), U2["VD"][h][:, m, :], ident[:])).then_inc(S(f"tok_mm{h}"), 1)
            for k in range(len(LEVELS)):
                for h in range(2):
                    b = B[4 * h:4 * h + 4]
                    pe.wait_ge(S(f"x_ready{h}"), c * 5 + (k + 1))
                    each(h, lambda m: mm(out4(b[2], m), U2["aab"][h][:, m, :], U2["X"][h][:, m, :],
                                         start=True, stop=True)).then_inc(S(f"q_mm{h}"), 1)
                for h in range(2):
                    b = B[4 * h:4 * h + 4]
                    pe.wait_ge(S(f"q_ev{h}"), c * 5 + (k + 1))
                    pe.wait_ge(S(f"xt_ready{h}"), c * 5 + (k + 1))
                    if k == 0:
                        pe.wait_ge(S(f"tok_ev{h}"), c * 4 + 4)
                    if k < len(LEVELS) - 1:
                        each(h, lambda m: mm(out4(b[3], m), U2["XT"][h][:, m, :], U2["Qs"][h][:, m, :],
                                             start=True, stop=True)).then_inc(S(f"d_mm{h}"), 1)
                    else:
                        each(h, lambda m: mm(out4(b[3], m), U2["Qs"][h][:, m, :], U2["XT"][h][:, m, :],
                                             start=True, stop=True)).then_inc(S(f"d_mm{h}"), 1)
                if k < len(LEVELS) - 1:
                    for h in range(2):
                        b = B[4 * h:4 * h + 4]
                        pe.wait_ge(S(f"x_ready{h}"), c * 5 + (k + 2))
                        each(h, lambda m: tr(out4(b[0], m), U2["X"][h][:, m, :], ident[:])) \
                            .then_inc(S(f"xt_mm{h}"), 1)

            def o64(bank, m):
                return bank[:].rearrange("p (m n) -> p m n", n=CH)[:, m, :]

            for h in range(2):
                pe.wait_ge(S(f"st{h}"), c + 1)
                for m in range(4):
                    mm(o64(B[4 * h + 1], m), U2["BDa"][h][:, m, :], U2["St"][h][:, m, :], start=True, stop=False)
                    r = mm(o64(B[4 * h + 1], m), U2["aak"][h][:, m, :], U2["Vc"][h][:, m, :],
                           start=False, stop=True)
                r.then_inc(S(f"g_mm{h}"), 1)
            for h in range(2):
                pe.wait_ge(S(f"g_ev{h}"), c + 1)
                pe.wait_ge(S(f"xt_last{h}"), c + 1)
                for m in range(4):
                    r = mm(o64(B[4 * h + 2], m), U2["XT"][h][:, m, :], U2["G"][h][:, m, :], start=True, stop=True)
                r.then_inc(S(f"u_mm{h}"), 1)
            for h in range(2):
                pe.wait_ge(S(f"u_ev{h}"), c + 1)
                for m in range(4):
                    mm(o64(B[4 * h + 3], m), U2["BDr"][h][:, m, :], U2["St"][h][:, m, :], start=True, stop=False)
                    mm(o64(B[4 * h + 3], m), U2["arb"][h][:, m, :], U2["U"][h][:, m, :], start=False, stop=False)
                    r = mm(o64(B[4 * h + 3], m), U2["ark"][h][:, m, :], U2["Vc"][h][:, m, :],
                           start=False, stop=True)
                r.then_inc(S(f"y_mm{h}"), 1)
                for m in range(4):
                    mm(o64(B[4 * h], m), U2["btok"][h][:, m, :], U2["U"][h][:, m, :], start=True, stop=False)
                    r = mm(o64(B[4 * h], m), U2["ktok"][h][:, m, :], U2["Vc"][h][:, m, :], start=False, stop=True)
                r.then_inc(S(f"dS_mm{h}"), 1)
            for h in range(2):
                pe.wait_ge(S(f"yn{h}"), c + 1)
                for m in range(4):
                    for e in range(2):
                        r = mm(B[4 * h + 1][64 * e:64 * e + 64, CH * m:CH * m + CH], U2["Y"][h][:, m, :],
                               ident[:, 64 * e:64 * e + 64], start=True, stop=True)
                r.then_inc(S(f"yt_mm{h}"), 1)

        pe.wait_ge(S("y_read0"), 9)
        pe.wait_ge(S("y_read1"), 9)
        pe.wait_ge(S("back_in"), 64)
        for m in range(KC):
            if m >= 2:
                pe.wait_ge(S("x_f"), SP_Y + m - 1)
            mm(B[m % 2][:], wg[:, 0, P * m:P * m + P], sg[:, 0, :], start=True, stop=False)
            mm(B[m % 2][:], wg[0:32, 1, P * m:P * m + P], sg[0:32, 1, :], start=False, stop=True) \
                .then_inc(S("g_mm"), 1)
        pe.wait_ge(S("x_lo"), SP_Y + 8)
        tiles(N_B1, r1h, r1l, E_B1)
        pe.wait_ge(S("x_lo"), SP_M + 8)
        tiles(N_OUT, r2h, r2l, E_OUT)
        rms(N2, B[7])
        rms(N3, B[6])
        pe.wait_ge(S("x_lo"), SP_F + 8)
        with pe.Fori(0, 16) as i:
            for h in range(2):
                pe.wait_ge(S("tile_ev"), 2 * i + (E_UP + h - 1))
                slab_mm(2 * i + (N_UP + h), (N_UP + h) % 2, B[h], r1h, r1l).then_inc(S("slab_mm"), 1)
        pe.wait_ge(S("f_lo"), 32)
        with pe.Fori(0, 4) as i:
            for h in range(2):
                pe.wait_ge(S("tile_ev"), 2 * i + (E_DOWN + h - 1))
                for b in range(KB):
                    slab_mm(8 * i + (N_DOWN + 4 * h + b), (N_DOWN + b) % 2, B[2 + h], fh, fl,
                            first=(b == 0), last=(b == KB - 1), kc0=KC * b).then_inc(S("slab_mm"), 1)
        rms(N4, B[7])

    @block.scalar
    def _(act):
        A = nc.scalar.activation

        for n_ in ("k_sc", "tw", "ta", "sq", "eW", "eWi", "eWx", "r_sc", "nrm", "v_sc"):
            act.sem_inc(S(n_), 1)

        def rms_sq(norm, src, ready):
            for kc in range(KC):
                if ready:
                    act.wait_ge(S(ready), kc + 1)
                if kc >= 2:
                    act.wait_ge(S("rms_mm"), norm + kc - 1)
                A(sqt[:, kc % 2, :], src[:, kc, :], ACT.Square).then_inc(S("rms_sq"), 1)

        def rms_root(norm):
            act.wait_ge(S("rms_rec"), norm // 8 + 1)
            A(rst[:, 1, :], rst[:, 0, :], ACT.Sqrt).then_inc(S("rms_root"), 1)

        def split_hi(sp_, hi):
            for kc in range(KC):
                act.wait_ge(S("x_f"), sp_ + kc + 1)
                A(hi[:, kc, :], hx[:, kc % 2, :], ACT.Copy).then_inc(S("x_hi"), 1)

        act.wait_ge(S("x_in"), 16)
        rms_sq(N1, xs, None)
        rms_root(N1)
        split_hi(SP_H, r1h)
        act.wait_ge(S("beta_ev"), 1)
        act.dma_start(beta_d, beta[0:16, :].unsqueeze(1).to_broadcast([16, CH, BETA])).then_inc(S("beta_out"), 16)
        act.wait_ge(S("beta_out"), 16)
        for e in range(2):
            for p in range(2):
                hstep = CH * BETA
                for lo_, dst0 in ((0, 0), (1, 128)):
                    n = 128 if lo_ == 0 else 64
                    src = bass.AP(tensor=beta_t, offset=(2 * e + p) * hstep + CH - 1,
                                  ap=[[BETA - 1, CH], [4 * hstep, 4], [1, n]])
                    act.dma_start(bias[64 * e:64 * e + 64, p:8:2, dst0:dst0 + n], src).then_inc(S("bias_in"), 16)

        for n in range(13):
            act.wait_ge(S("slab_mm"), n + 1)
            b = B[n % 2]
            if n < 3:
                M = 32 if n == 2 else P
                dst = (tl, sg[:, 0, :], sg[:, 1, :])[n]
                dst = dst[0:M, :]
                A(dst, b[0:M, :], ACT.Copy, scale=par[0:M, OM_L + n:OM_L + n + 1]).then_inc(S("lo_sc"), 1)
                act.wait_ge(S("lo_sh"), n + 1)
                if n == 0:
                    A(tl[0:64, :], tl[0:64, :], ACT.Tanh).then_inc(S("lo_th"), 1)
                else:
                    A(dst, dst, ACT.Tanh, scale=0.5).then_inc(S("lo_th"), 1)
            elif n == 3:
                A(kT[:], b[:], ACT.Copy).then_inc(S("tile_ev"), 1)
                act.wait_ge(S("tile_ev"), 1)
                act.wait_ge(S("kb_zero"), 1)
                for o in range(2):
                    for g in range(2):
                        for p in range(2):
                            ksrc = kT[64 * g:64 * g + 64, :].rearrange("d (t x) -> d t x", x=P)
                            kdst = kb[64 * p:64 * p + 64, o, g, p, :, :]
                            if o == 1:
                                act.dma_start(kdst, ksrc).then_inc(S("kb_in"), 16)
                            else:
                                act.dma_start(kdst[:, :, 0:64], ksrc[:, :, 0:64]).then_inc(S("kb_in"), 16)
                                act.dma_start(kdst[:, 1:4, 64:128], ksrc[:, 0:3, 64:128]).then_inc(S("kb_in"), 16)
            elif n == 4:
                A(vT[:], b[:], ACT.Copy).then_inc(S("vT"), 1)
                act.wait_ge(S("vT"), 1)
                act.sem_inc(S("tile_ev"), 1)
            else:
                A(q[:, (n - 5) // 2, :, (n - 5) % 2, :], b[:].rearrange("p (c t) -> p c t", c=NCH), ACT.Copy) \
                    .then_inc(S("tile_ev"), 1)

        def tanh_tiles(dst, n0, hgb):
            with act.Fori(0, 4) as i:
                for h in range(2):
                    act.wait_ge(S("slab_mm"), 2 * i + (n0 + h + 1))
                    A(dst[:, 2 * i + h, :], B[h][:], ACT.Tanh, scale=0.5, bias=pcol(hgb, 2 * i + h)) \
                        .then_inc(S("tile_ev"), 1)

        tanh_tiles(m0, N_G0, H_GB0)

        for c in range(NCH):
            act.wait_ge(S("at_sub"), c + 1)
            A(lg[:, c % 2, :, :], lg[:, c % 2, :, :], ACT.Exp).then_inc(S("at_exp"), 1)
            A(asm[:, c % 2, 1, :], asm[:, c % 2, 1, :], ACT.Exp).then_inc(S("at_exs"), 1)
            act.wait_ge(S("at_tr"), c + 1)
            for k in range(2):
                A(pT[:, c % 2, 4 * k:4 * k + 4, :], v4(B[6 + k]), ACT.Copy).then_inc(S("at_pT"), 1)
            act.wait_ge(S("at_o"), c + 1)
            A(r2h[:, :, CH * c:CH * c + CH], B[0][:].rearrange("p (m t) -> p m t", m=KC), ACT.Copy) \
                .then_inc(S("at_hi"), 1)
        act.wait_ge(S("tile_ev"), E_G1)
        act.dma_start(m0_d, flat(m0)).then_inc(S("spilled"), 16)
        act.wait_ge(S("spilled"), 16)

        with act.Fori(0, 4) as i:
            for h in range(2):
                m = 2 * i + h
                n = 6 * i + (N_PAIR + 3 * h)
                act.wait_ge(S("slab_mm"), n + 1)
                act.wait_ge(S("ax"), m + 1)
                A(tmp["kS"][:], B[0][:], ACT.Copy, scale=pcol(OM_K, m)).then_inc(S("k_sc"), 1)
                act.wait_ge(S("w_mm"), m + 2)
                act.wait_ge(S("ld"), m + 1)
                A(tmp["tw"][:], B[1][:], ACT.Tanh, scale=0.5, bias=pcol(H_W0, m)).then_inc(S("tw"), 1)
                act.wait_ge(S("a_mm"), m + 2)
                act.wait_ge(S("aa"), m + 1)
                A(tmp["ta"][:], B[2][:], ACT.Tanh, scale=0.5, bias=pcol(H_A0, m)).then_inc(S("ta"), 1)
                act.wait_ge(S("k_sh"), m + 2)
                act.wait_ge(S("ss_mm"), m + 1)
                A(tmp["sq"][:], tmp["kS"][:], ACT.Square, scale=pcol(COL["k_k"], m)).then_inc(S("sq"), 1)
                act.wait_ge(S("cum"), m + 2)
                act.wait_ge(S("wc"), m + 1)
                A(tmp["eW"][:], tmp["cum"][:], ACT.Exp).then_inc(S("eW"), 1)
                act.wait_ge(S("bt"), m + 1)
                A(tmp["eWi"][:], tmp["cum"][:], ACT.Exp, scale=-1.0).then_inc(S("eWi"), 1)
                act.wait_ge(S("cx"), m + 2)
                act.wait_ge(S("at"), m + 1)
                A(tmp["eWx"][:], tmp["cx"][:], ACT.Exp).then_inc(S("eWx"), 1)
                act.wait_ge(S("slab_mm"), n + 2)
                act.wait_ge(S("p"), m + 1)
                A(tmp["rS"][:], B[3][:], ACT.Copy, scale=pcol(OM_R, m)).then_inc(S("r_sc"), 1)
                act.wait_ge(S("ssm"), m + 2)
                act.wait_ge(S("inv"), m + 1)
                A(tmp["nrm"][:], tmp["ssm"][:], ACT.Sqrt).then_inc(S("nrm"), 1)
                act.wait_ge(S("slab_mm"), n + 3)
                A(vb[:, m, :], B[5][:], ACT.Copy, scale=pcol(OM_V, m)).then_inc(S("v_sc"), 1)

        act.wait_ge(S("bv"), 9)
        tanh_tiles(t1, N_G1, H_GB1)
        act.wait_ge(S("tile_ev"), E_B1)
        act.dma_start(t1_d, flat(t1)).then_inc(S("spilled"), 16)
        act.wait_ge(S("spilled"), 32)

        with act.Fori(0, NCH) as c:
            for h in range(2):
                b = B[4 * h:4 * h + 4]
                act.wait_ge(S(f"tok_mm{h}"), c * 3 + 1)
                A(U2["btok"][h][:], v4(b[0]), ACT.Copy).then_inc(S(f"tok_ev{h}"), 1)
                act.wait_ge(S(f"tok_mm{h}"), c * 3 + 2)
                A(U2["ktok"][h][:], v4(b[1]), ACT.Copy).then_inc(S(f"tok_ev{h}"), 1)
                act.wait_ge(S(f"tok_mm{h}"), c * 3 + 3)
                for e in range(2):
                    A(U2["Vc"][h][64 * e:64 * e + 64, :, :], v4(b[3])[64 * e:64 * e + 64, :, 64 * e:64 * e + 64],
                      ACT.Copy).then_inc(S(f"tok_ev{h}"), 1)
            for k in range(len(LEVELS) - 1):
                for h in range(2):
                    act.wait_ge(S(f"xt_mm{h}"), c * 4 + (k + 1))
                    A(U2["XT"][h][:], v4(B[4 * h]), ACT.Copy).then_inc(S(f"xt_ready{h}"), 1)
            for h in range(2):
                act.wait_ge(S(f"g_mm{h}"), c + 1)
                A(U2["G"][h][:], B[4 * h + 1][:, 0:256].rearrange("p (m i) -> p m i", m=4), ACT.Copy) \
                    .then_inc(S(f"g_ev{h}"), 1)
            for h in range(2):
                act.wait_ge(S(f"u_mm{h}"), c + 1)
                A(U2["U"][h][:], B[4 * h + 2][:, 0:256].rearrange("p (m i) -> p m i", m=4), ACT.Copy) \
                    .then_inc(S(f"u_ev{h}"), 1)
            for h in range(2):
                act.wait_ge(S(f"yc{h}"), c + 1)
                A(U2["Yt"][h][:], U2["Y"][h][:], ACT.Square).then_inc(S(f"ysq{h}"), 1)
            for h in range(2):
                act.wait_ge(S(f"yv{h}"), c + 1)
                A(gn[:, h, 3, :], gn[:, h, 2, :], ACT.Sqrt).then_inc(S(f"yr{h}"), 1)

        act.wait_ge(S("y_read0"), 9)
        act.wait_ge(S("y_read1"), 9)
        act.wait_ge(S("spilled"), 16)
        act.dma_start(wg[:, 0, :], wgate[0:P, :]).then_inc(S("back_in"), 16)
        act.dma_start(wg[0:32, 1, :], wgate[P:P + 32, :]).then_inc(S("back_in"), 16)
        act.dma_start(flat(m0b), m0_d).then_inc(S("back_in"), 16)
        act.dma_start(flat(t1b), t1_d).then_inc(S("back_in"), 16)
        split_hi(SP_Y, r1h)
        split_hi(SP_M, r2h)
        act.wait_ge(S("x_f"), SP_Y + 8)
        act.dma_start(xr[:], xT).then_inc(S("x_in"), 16)
        with act.Fori(0, 4) as i:
            for h in range(2):
                act.wait_ge(S("slab_mm"), 2 * i + (N_OUT + h + 1))
                A(mix[:, 2 * i + h, :], B[h][:], ACT.Copy, scale=0.5).then_inc(S("tile_ev"), 1)
        act.wait_ge(S("tile_ev"), E_UP)
        rms_sq(N2, mix, None)
        rms_root(N2)
        rms_sq(N3, xr, "x1_f")
        act.dma_start(x1_d, flat(xr)).then_inc(S("spilled"), 16)
        rms_root(N3)
        split_hi(SP_F, r1h)
        with act.Fori(0, 16) as i:
            for h in range(2):
                j = 2 * i + h
                act.wait_ge(S("slab_mm"), 2 * i + (N_UP + h + 1))
                act.wait_ge(S(f"f_lo{h}"), i + 1)
                A(sqt[:, h, :], B[h][:], ACT.Relu).then_inc(S(f"f_relu{h}"), 1)
                act.wait_ge(S("tile_ev"), 2 * i + (E_UP + h + 1))
                A(fh[:, j, :], hx[:, h, :], ACT.Copy).then_inc(S(f"f_hi{h}"), 1)
        act.wait_ge(S("spilled"), 48)
        act.wait_ge(S("slab_mm"), N_DOWN)
        act.dma_start(flat(x1), x1_d).then_inc(S("x_in"), 16)
        with act.Fori(0, 4) as i:
            for h in range(2):
                act.wait_ge(S("slab_mm"), 8 * i + (N_DOWN + 4 * h + 4))
                A(ob[:, 2 * i + h, :], B[2 + h][:], ACT.Copy).then_inc(S("tile_ev"), 1)
        act.wait_ge(S("tile_ev"), E_ALL)
        rms_sq(N4, ob, None)
        rms_root(N4)

    @block.vector
    def _(dve):
        TT = nc.vector.tensor_tensor
        TS = nc.vector.tensor_scalar
        STT = nc.vector.scalar_tensor_tensor
        A_, M_, SUB = ALU.add, ALU.mult, ALU.subtract

        for n_ in ("k_sh", "ld", "cum", "cx", "aa", "kp", "r_sh", "wc", "p", "ssm", "inv", "ax", "be", "at", "bt", "v_sh", "bv", "y_read0", "y_read1", "f_lo0", "f_lo1"):
            dve.sem_inc(S(n_), 1)

        def rms_rec(norm, bank):
            dve.wait_ge(S("rms_mm"), norm + KC)
            TS(rst[:, 0, :], bank[:], 1.0 / D, EPS, M_, A_).then_inc(S("rms_ms"), 1)
            dve.wait_ge(S("rms_ms"), norm // 8 + 1)
            nc.vector.reciprocal(rst[:, 0, :], rst[:, 0, :]).then_inc(S("rms_rec"), 1)
            dve.wait_ge(S("rms_root"), norm // 8 + 1)

        def norm_split(src, gain, sp_, hi, lo):
            for kc in range(KC + 1):
                if kc < KC:
                    if kc >= 2:
                        dve.wait_ge(S("x_lo"), sp_ + kc - 1)
                    STT(hx[:, kc % 2, :], src[:, kc, :], col(gain, kc), rst[:, 1, :], M_, M_).then_inc(S("x_f"), 1)
                if kc >= 1:
                    remainder(kc - 1, sp_, hi, lo)

        def remainder(kc, sp_, hi, lo):
            dve.wait_ge(S("x_f"), sp_ + kc + 1)
            dve.wait_ge(S("x_hi"), sp_ + kc + 1)
            TT(lo[:, kc, :], hx[:, kc % 2, :], hi[:, kc, :].bitcast(F32), SUB).then_inc(S("x_lo"), 1)

        dve.wait_ge(S("par_in"), 16)
        for n_, (o, s_, w_, a, b) in enumerate((
                (OM_R, COL["mu_r"], 24, -1.0, 1.0), (OM_L, MU_L, 3, -1.0, 1.0), (H_W0, COL["w0"], 16, 0.5, 0.0),
                (H_KA, COL["k_a"], 8, 0.5, 0.0), (OH_KA, COL["k_a"], 8, -0.5, 1.0),
                (N_KK, COL["k_k"], 8, -1.0, 0.0), (H_GB0, COL["gb0"], 16, 0.5, 0.0))):
            TS(par[:, o:o + w_], par[:, s_:s_ + w_], a, b, M_, A_).then_inc(S("par_done"), 1)
        dve.wait_ge(S("par_done"), 7)

        nc.vector.memset(kb[:].rearrange("p a b c d e -> p (a b c d e)"), 0.0).then_inc(S("kb_zero"), 1)
        nc.vector.memset(v2[:], 0.0).then_inc(S("kb_zero"), 1)
        rms_rec(N1, B[7])
        norm_split(xs, "pre_mix", SP_H, r1h, r1l)
        dve.wait_ge(S("small_mm"), 1)
        nc.vector.tensor_copy(beta[0:16, :], B[6][0:16, 0:BETA]).then_inc(S("beta_ev"), 1)

        for n in range(3):
            M = 32 if n == 2 else P
            dst = (tl[:], sg[:, 0, :], sg[:, 1, :])[n][0:M]
            dve.wait_ge(S("lo_sc"), n + 1)
            STT(dst[:, 1:T], B[n % 2][0:M, 0:T - 1], par[0:M, MU_L + n:MU_L + n + 1], dst[:, 1:T], M_, A_) \
                .then_inc(S("lo_sh"), 1)
        for n in (1, 2):
            M = 32 if n == 2 else P
            dve.wait_ge(S("lo_th"), n + 1)
            TS(sg[0:M, n - 1, :], sg[0:M, n - 1, :], 0.5, 0.5, M_, A_)
        dve.wait_ge(S("small_mm"), 2)
        dve.wait_ge(S("kb_zero"), 2)
        nc.vector.tensor_copy(v1[:], v4(B[2])).then_inc(S("v_ready"), 1)
        nc.vector.tensor_copy(v2[0:64], v4(B[2])[0:64]).then_inc(S("v_ready"), 1)
        nc.vector.tensor_copy(v2[64:128, 1:4, :], v4(B[2])[64:128, 0:3, :]).then_inc(S("v_ready"), 1)

        dve.wait_ge(S("bias_in"), 16 * 8)
        dve.wait_ge(S("tab_in"), 48)

        def logits(c):
            dve.wait_ge(S("at_sc"), c + 1)
            if c >= 2:
                dve.wait_ge(S("at_tr"), c - 1)
            L = lg[:, c % 2].rearrange("p (k g) n -> p k g n", k=2)
            bs = bias[:, :, 0:128] if c % 2 else bias[:, :, 64:192]
            bs = bs.rearrange("p (k g) n -> p k g n", k=2)
            for k in range(2):
                ps = v4(B[2 + 2 * (c % 2) + k])
                if c == 0:
                    STT(L[:, k, :, 0:64], ps[:, :, 0:64], HD ** -0.5, bs[:, k, :, 0:64], M_, A_) \
                        .then_inc(S("at_lg"), 1)
                    nc.vector.memset(L[:, k, :, 64:128], -1e30).then_inc(S("at_no"), 1)
                else:
                    STT(L[:, k], ps, HD ** -0.5, bs[:, k], M_, A_).then_inc(S("at_lg"), 1)
            if c == 0:
                dve.wait_ge(S("at_no"), 2)
            dve.wait_ge(S("at_lg"), 2 * c + 2)
            a = asm[:, c % 2]
            L = lg[:, c % 2]
            nc.vector.tensor_reduce(a[:, 0, :], L, AX, ALU.max).then_inc(S("at_soft"), 1)
            dve.wait_ge(S("at_soft"), 6 * c + 1)
            TT(a[:, 0, :], a[:, 0, :], sinkT[:], ALU.max).then_inc(S("at_soft"), 1)
            dve.wait_ge(S("at_soft"), 6 * c + 2)
            TT(a[:, 1, :], sinkT[:], a[:, 0, :], SUB).then_inc(S("at_soft"), 1)
            dve.wait_ge(S("at_soft"), 6 * c + 3)
            TT(L, L, a[:, 0, :].unsqueeze(2).to_broadcast([P, 8, P]), SUB).then_inc(S("at_sub"), 1)

        def normalise(c):
            a = asm[:, c % 2]
            L = lg[:, c % 2]
            dve.wait_ge(S("at_exp"), c + 1)
            nc.vector.tensor_reduce(a[:, 2, :], L, AX, A_).then_inc(S("at_soft"), 1)
            dve.wait_ge(S("at_soft"), 6 * c + 4)
            dve.wait_ge(S("at_exs"), c + 1)
            TT(a[:, 3, :], a[:, 2, :], a[:, 1, :], A_).then_inc(S("at_soft"), 1)
            dve.wait_ge(S("at_soft"), 6 * c + 5)
            nc.vector.reciprocal(a[:, 4, :], a[:, 3, :]).then_inc(S("at_soft"), 1)
            dve.wait_ge(S("at_soft"), 6 * c + 6)
            TT(L, L, a[:, 4, :].unsqueeze(2).to_broadcast([P, 8, P]), M_).then_inc(S("at_p"), 1)

        def attn_lo(c):
            dve.wait_ge(S("at_hi"), c + 1)
            cs = slice(CH * c, CH * c + CH)
            TT(r2l[:, :, cs], B[0][:].rearrange("p (m t) -> p m t", m=KC), r2h[:, :, cs].bitcast(F32), SUB) \
                .then_inc(S("at_lo"), 1)

        logits(0)
        for c in range(NCH):
            normalise(c)
            if c + 1 < NCH:
                logits(c + 1)
            attn_lo(c)

        dve.wait_ge(S("tile_ev"), E_B0)
        with dve.Fori(0, 4) as i:
            for h in range(2):
                dve.wait_ge(S("slab_mm"), 2 * i + (N_B0 + h + 1))
                STT(m0[:, 2 * i + h, :], m0[:, 2 * i + h, :], 1.0, B[h][:], A_, M_).then_inc(S("tile_ev"), 1)
        nc.vector.memset(wl[:].rearrange("p a b c -> p (a b c)"), 0.0).then_inc(S("wl_zero"), 1)

        dve.wait_ge(S("masks"), 1 + 2 + 3 + 3 + 3 + 3 + 4 * len(LEVELS))
        dve.wait_ge(S("spilled"), 16)
        with dve.Fori(0, 4) as i:
            for h in range(2):
                m = 2 * i + h
                t = {k_: v_[:] for k_, v_ in tmp.items()}

                def need(*names):
                    for n_ in names:
                        dve.wait_ge(S(n_), m + 2)

                def read(*names):
                    for n_ in names:
                        dve.wait_ge(S(n_), m + 1)

                need("k_sc")
                STT(t["kS"][:, 1:T], B[0][:, 0:T - 1], col("mu_k", m), t["kS"][:, 1:T], M_, A_) \
                    .then_inc(S("k_sh"), 1)
                need("tw")
                TS(t["ld"], t["tw"], -C_DEC, -C_DEC, M_, A_).then_inc(S("ld"), 1)
                need("ld")
                read("eWi")
                nc.vector.tensor_tensor_scan(t["cum"], scanm[:], t["ld"], 0.0, M_, A_).then_inc(S("cum"), 1)
                need("cum")
                read("eWx")
                TT(t["cx"], t["cum"], t["ld"], SUB).then_inc(S("cx"), 1)
                need("ta")
                TS(t["t"], t["ta"], pcol(H_KA, m), pcol(OH_KA, m), M_, A_)
                TS(t["aa"], t["ta"], 0.5, 0.5, M_, A_).then_inc(S("aa"), 1)
                need("aa", "k_sh")
                TT(t["kp"], t["kS"], t["t"], M_).then_inc(S("kp"), 1)
                STT(t["b0"], t["kS"], col("k_k", m), t["aa"], M_, M_)
                need("kp", "eWi")
                TT(kt[:, m, :], t["kp"], t["eWi"], M_)
                need("r_sc")
                STT(t["rS"][:, 1:T], B[3][:, 0:T - 1], col("mu_r", m), t["rS"][:, 1:T], M_, A_) \
                    .then_inc(S("r_sh"), 1)
                need("r_sh", "eW")
                TT(ar[:, 1, m, :], t["rS"], t["eW"], M_)
                nc.vector.tensor_copy(wc[:, m, :], t["eW"][:, CH - 1:T:CH]).then_inc(S("wc"), 1)
                read("bon_mm")
                STT(t["p"], t["rS"], col("r_k", m), t["kp"], M_, M_).then_inc(S("p"), 1)
                need("ss_mm")
                read("nrm")
                TS(t["ssm"], B[4][:], 1e-24, None, ALU.max).then_inc(S("ssm"), 1)
                need("nrm")
                nc.vector.reciprocal(t["inv"], t["nrm"]).then_inc(S("inv"), 1)
                need("inv")
                STT(t["ssm"], t["kS"], pcol(N_KK, m), t["inv"], M_, M_).then_inc(S("ax"), 1)
                TT(t["b0"], t["b0"], t["inv"], M_).then_inc(S("be"), 1)
                need("ax", "eWx")
                TT(ar[:, 0, m, :], t["ssm"], t["eWx"], M_).then_inc(S("at"), 1)
                need("be")
                TT(bt[:, m, :], t["b0"], t["eWi"], M_).then_inc(S("bt"), 1)
                need("v_sc")
                STT(vb[:, m, 1:T], B[5][:, 0:T - 1], col("mu_v", m), vb[:, m, 1:T], M_, A_) \
                    .then_inc(S("v_sh"), 1)
                need("v_sh", "bon_mm")
                TT(bv[:, m, :], B[6][:], vb[:, m, :], M_).then_inc(S("bv"), 1)

        dve.wait_ge(S("spilled"), 32)
        for h in range(2):
            nc.vector.memset(U2["St"][h][:], 0.0).then_inc(S("st_zero"), 1)
        dve.wait_ge(S("st_zero"), 2)
        for h in range(2):
            dve.sem_inc(S(f"st{h}"), 1)
        with dve.Fori(0, NCH) as c:
            def m2(t_):
                return t_[:].rearrange("p m (e t) -> p m e t", e=2)

            for h in range(2):
                b = B[4 * h:4 * h + 4]
                dve.wait_ge(S(f"sc_mm{h}"), c * 2 + 1)
                TT(m2(U2["aab"][h]), bc2(v4(b[0])[:, :, 0:64]), mask4(m_strict), M_).then_inc(S(f"sc_ev{h}"), 1)
                TT(m2(U2["arb"][h]), bc2(v4(b[0])[:, :, 64:128]), mask4(m_incl), M_).then_inc(S(f"sc_ev{h}"), 1)
                dve.wait_ge(S(f"sc_mm{h}"), c * 2 + 2)
                TT(m2(U2["aak"][h]), bc2(v4(b[1])[:, :, 0:64]), mask4(m_strict), M_).then_inc(S(f"sc_ev{h}"), 1)
                TT(m2(U2["ark"][h]), bc2(v4(b[1])[:, :, 64:128]), mask4(m_incl), M_).then_inc(S(f"sc_ev{h}"), 1)
                dve.wait_ge(S(f"sc_ev{h}"), c * 5 + 1)
                TT(U2["AI"][h][:], U2["aab"][h][:], mask4f(ident), A_).then_inc(S(f"sc_ev{h}"), 1)
            for h in range(2):
                b = B[4 * h:4 * h + 4]
                dve.wait_ge(S(f"sc_ev{h}"), c * 5 + 5)
                TT(U2["XT"][h][:], U2["AI"][h][:], mask4f(m_1t), M_).then_inc(S(f"xt_ready{h}"), 1)
                dve.wait_ge(S(f"ai_mm{h}"), c + 1)
                TT(U2["X"][h][:], v4(b[2]), mask4f(m_1), M_).then_inc(S(f"x_ready{h}"), 1)
            for k in range(len(LEVELS)):
                for h in range(2):
                    dve.wait_ge(S(f"q_mm{h}"), c * 5 + (k + 1))
                    TT(U2["Qs"][h][:], v4(B[4 * h + 2]), mask4f(m_lev[k]), M_).then_inc(S(f"q_ev{h}"), 1)
                for h in range(2):
                    dve.wait_ge(S(f"d_mm{h}"), c * 5 + (k + 1))
                    if k < len(LEVELS) - 1:
                        TT(U2["X"][h][:], v4(B[4 * h + 3]), U2["X"][h][:], A_).then_inc(S(f"x_ready{h}"), 1)
                    else:
                        TT(U2["XT"][h][:], v4(B[4 * h + 3]), U2["XT"][h][:], A_).then_inc(S(f"xt_last{h}"), 1)

            def r4(t_):
                return t_.unsqueeze(2).to_broadcast([P, 4, CH])

            for h in range(2):
                ps = B[4 * h + 3][:, 0:256].rearrange("p (m i) -> p m i", m=4)
                dve.wait_ge(S(f"y_mm{h}"), c + 1)
                nc.vector.tensor_reduce(gn[:, h, 0, :], ps, AX, A_).then_inc(S(f"gn{h}"), 1)
                dve.wait_ge(S(f"gn{h}"), c * 5 + 1)
                TS(gn[:, h, 1, :], gn[:, h, 0, :], 1.0 / HD, None, M_).then_inc(S(f"gn{h}"), 1)
                dve.wait_ge(S(f"gn{h}"), c * 5 + 2)
                TT(U2["Y"][h][:], ps, r4(gn[:, h, 1, :]), SUB).then_inc(S(f"yc{h}"), 1)
                ds = B[4 * h][:, 0:256].rearrange("p (m i) -> p m i", m=4)
                dve.wait_ge(S(f"dS_mm{h}"), c + 2)
                TT(U2["St"][h][:], ds, U2["St"][h][:], A_).then_inc(S(f"gn{h}"), 1)
                dve.wait_ge(S(f"gn{h}"), c * 5 + 3)
                TT(U2["St"][h][:], U2["St"][h][:],
                   wc[:, 4 * h:4 * h + 4, bass.ds(c, 1)].to_broadcast([P, 4, CH]), M_).then_inc(S(f"st{h}"), 1)
            for h in range(2):
                dve.wait_ge(S(f"ysq{h}"), c + 1)
                nc.vector.tensor_reduce(gn[:, h, 0, :], U2["Yt"][h][:], AX, A_).then_inc(S(f"gn{h}"), 1)
                dve.wait_ge(S(f"gn{h}"), c * 5 + 4)
                TS(gn[:, h, 1, :], gn[:, h, 0, :], 1.0 / HD, GN_EPS, M_, A_).then_inc(S(f"gn{h}"), 1)
                dve.wait_ge(S(f"gn{h}"), c * 5 + 5)
                nc.vector.reciprocal(gn[:, h, 2, :], gn[:, h, 1, :]).then_inc(S(f"yv{h}"), 1)
            for h in range(2):
                dve.wait_ge(S(f"yr{h}"), c + 1)
                TT(U2["Y"][h][:], U2["Y"][h][:], r4(gn[:, h, 3, :]), M_).then_inc(S(f"yn{h}"), 1)
            for h in range(2):
                tk = bass.ds(c * CH, CH)
                dve.wait_ge(S(f"yt_mm{h}"), c + 1)
                TT(U2["Yt"][h][:], B[4 * h + 1][:, 0:256].rearrange("p (m i) -> p m i", m=4),
                   r4(par[:, COL["ln_w"] + 4 * h:COL["ln_w"] + 4 * h + 4]), M_).then_inc(S(f"y_read{h}"), 1)
                dve.wait_ge(S(f"y_read{h}"), c + 2)
                TT(bv[:, 4 * h:4 * h + 4, tk], U2["Yt"][h][:], bv[:, 4 * h:4 * h + 4, tk], A_) \
                    .then_inc(S("y_sum"), 1)

        dve.wait_ge(S("y_sum"), 16)
        for m in range(KC + 1):
            if m < KC:
                dve.wait_ge(S("g_mm"), m + 1)
                if m >= 2:
                    dve.wait_ge(S("x_lo"), SP_Y + m - 1)
                STT(hx[:, m % 2, :], bv[:, m, :], col("ln_b", m), B[m % 2][:], A_, M_).then_inc(S("x_f"), 1)
            if m >= 1:
                remainder(m - 1, SP_Y, r1h, r1l)
        dve.wait_ge(S("back_in"), 64)
        for m in range(KC):
            dve.wait_ge(S("slab_mm"), N_B1 + m + 1)
            STT(t1b[:, m, :], t1b[:, m, :], 1.0, B[m % 2][:], A_, M_).then_inc(S("tile_ev"), 1)
            dve.wait_ge(S("tile_ev"), E_B1 + m + 1)
            if m >= 2:
                dve.wait_ge(S("x_lo"), SP_M + m - 1)
            TT(hx[:, m % 2, :], t1b[:, m, :], m0b[:, m, :], A_).then_inc(S("x_f"), 1)
            remainder(m, SP_M, r2h, r2l)

        rms_rec(N2, B[7])
        dve.wait_ge(S("x_in"), 32)
        for kc in range(KC):
            STT(mix[:, kc, :], mix[:, kc, :], col("post_mix", kc), rst[:, 1, :], M_, M_).then_inc(S("scaled"), 1)
            dve.wait_ge(S("scaled"), kc + 1)
            TT(xr[:, kc, :], xr[:, kc, :], mix[:, kc, :], A_).then_inc(S("x1_f"), 1)
        dve.wait_ge(S("x1_f"), 8)
        rms_rec(N3, B[6])
        norm_split(xr, "pre_ffn", SP_F, r1h, r1l)
        dve.wait_ge(S("spilled"), 48)
        with dve.Fori(0, 16) as i:
            for h in range(2):
                j = 2 * i + h
                dve.wait_ge(S(f"f_relu{h}"), i + 1)
                STT(hx[:, h, :], B[h][:], 0.0, sqt[:, h, :], ALU.max, M_).then_inc(S("tile_ev"), 1)
                dve.wait_ge(S("tile_ev"), 2 * i + (E_UP + h + 1))
                dve.wait_ge(S(f"f_hi{h}"), i + 1)
                TT(fl[:, j, :], hx[:, h, :], fh[:, j, :].bitcast(F32), SUB).then_inc(S(f"f_lo{h}"), 1)
                dve.wait_ge(S(f"f_lo{h}"), i + 2)
                dve.sem_inc(S("f_lo"), 1)
        rms_rec(N4, B[7])
        dve.wait_ge(S("x_in"), 48)
        for kc in range(KC):
            STT(ob[:, kc, :], ob[:, kc, :], col("post_ffn", kc), rst[:, 1, :], M_, M_).then_inc(S("scaled"), 1)
            dve.wait_ge(S("scaled"), KC + kc + 1)
            TT(ob[:, kc, :], ob[:, kc, :], x1[:, kc, :], A_).then_inc(S("o_ready"), 1)

    block.__exit__(None, None, None)


def relative_buckets():
    rel = np.arange(-(CH * 2 - 1), CH)
    nb, max_exact = 16, 8
    ret = (rel > 0).astype(np.int32) * nb
    n = np.abs(rel)
    ratio = np.maximum(n, 1).astype(np.float32) / np.float32(max_exact)
    large = max_exact + (np.log(ratio) / np.float32(np.log(128 / max_exact)) * (nb - max_exact)).astype(np.int32)
    return ret + np.where(n < max_exact, n, np.minimum(large, nb - 1))


def kernel(x, w_in, rwkv_shift, pre_mix_g, post_mix_g, pre_ffn_g, post_ffn_g, attn_sinks, rel_bias, w0,
           w_decay_up, a0, w_aaa_up, w_gate_up, k_k, k_a, r_k, ln_x_w, ln_x_b, gate_bias, w_branch, w_out,
           w_ff_up, w_ff_down):
    import concourse.bacc as bacc
    from concourse.bass_utils import run_bass_kernel_spmd

    def tab(v):
        return np.asarray(v).reshape(KC, P).T

    mu = np.asarray(rwkv_shift)[0]
    lmu = np.zeros((3 * P,), np.float32)
    lmu[:288] = mu[3 * D:]
    gb = np.asarray(gate_bias)[0]
    cols = np.concatenate([tab(v) for v in (
        pre_mix_g[0], post_mix_g[0], pre_ffn_g[0], post_ffn_g[0], mu[0:D], mu[D:2 * D], mu[2 * D:3 * D],
        w0[0], a0[0], k_k[0], k_a[0], r_k[0], ln_x_w[0], ln_x_b[0], gb[0], gb[1])] + [lmu.reshape(3, P).T], axis=1)
    head = np.arange(8)
    hmap = np.stack([4 * (head // 2) + 2 * e + head % 2 for e in range(2)])
    sinks = np.repeat(np.asarray(attn_sinks)[0][hmap], CH, axis=0)
    onehot = np.zeros((32, BETA), np.float32)
    onehot[relative_buckets(), np.arange(BETA - 1)] = 1.0
    arrays = {
        "xT": np.asarray(x)[0].T.reshape(KC, P, T).transpose(1, 0, 2),
        "w_in": w_in[0], "cols": cols, "sinks": sinks, "onehot": onehot, "rel_bias": rel_bias,
        "wdec": w_decay_up[0], "waaa": w_aaa_up[0], "wgate": w_gate_up[0], "w_br": w_branch[0],
        "w_out": w_out[0], "w_up": w_ff_up[0], "w_down": w_ff_down[0],
    }
    arrays = {k: np.ascontiguousarray(v) for k, v in arrays.items()}
    nc = bacc.Bacc("TRN2", target_bir_lowering=False, num_devices=1)
    args = [nc.dram_tensor(k, list(v.shape), F32, kind="ExternalInput").ap() for k, v in arrays.items()]
    out = nc.dram_tensor("out", [P, KC, T], F32, kind="ExternalOutput").ap()
    build(nc, *args, out)
    r = run_bass_kernel_spmd(nc, [arrays], core_ids=[0])
    y = r.results[0]["out"]
    return y.transpose(1, 0, 2).reshape(D, T).T[None]
```

```python
import math

import concourse.bass as bass
import numpy as np
from concourse import mybir
from concourse.alu_op_type import AluOpType as ALU

F32 = mybir.dt.float32
F32R = mybir.dt.float32r
ACT = mybir.ActivationFunctionType
AX = mybir.AxisListType.X

P = 128
T = 512
D = 1024
KC = D // P
CH = 64
NCH = T // CH
HD = 64
DFF = 4 * D
KB = DFF // D
EPS = 1e-6
GN_EPS = 64e-5
BETA = 192
C_DEC = 0.5 * math.exp(-0.5)

Q0, K0, V0 = 0, D, D + P
R0, RK0, RV0 = D + 2 * P, 2 * D + 2 * P, 3 * D + 2 * P
L0 = 4 * D + 2 * P
G0 = L0 + 64 + 64 + 160

NAMES = ["pre_mix", "post_mix", "pre_ffn", "post_ffn", "mu_r", "mu_k", "mu_v", "w0", "a0",
         "k_k", "k_a", "r_k", "ln_w", "ln_b", "gb0", "gb1"]
COL = {n: 8 * i for i, n in enumerate(NAMES)}
MU_L = 8 * len(NAMES)
NCOL = MU_L + 3
OM_R, OM_K, OM_V, OM_L = NCOL, NCOL + 8, NCOL + 16, NCOL + 24
H_W0, H_A0, H_KA, OH_KA, N_KK, H_GB0, H_GB1 = (NCOL + 27 + 8 * i for i in range(7))
NCOLS = NCOL + 27 + 56

N_L, N_K, N_V, N_Q = 0, 3, 4, 5
N_B0 = 13
N_PAIR = 21
N_GATE = 45
N_B1 = 61
N_OUT = 69
N_UP = 77
N_DOWN = 109
N_SLABS = 141
LEVELS = [2, 4, 8, 16, 32]
E_B0, E_GATE, E_B1, E_OUT, E_UP, E_DOWN, E_ALL = 10, 18, 34, 42, 50, 82, 90
N1, N2, N3, N4 = 0, 8, 16, 24
SP_H, SP_Y, SP_M, SP_F = 0, 8, 16, 24


def build(nc, xT, w_in, cols, sinks, onehot, rel_bias, wdec, waaa, wgate, w_br, w_out, w_up, w_down, out):
    sems = {}

    def S(name):
        if name not in sems:
            sems[name] = nc.alloc_semaphore(name)
        return sems[name]

    base = (nc.sbuf_base + 63) // 64 * 64

    def at(name, shape, kib, dt=F32):
        kib = kib if kib < 10 else kib - 0.5
        return nc.alloc_sbuf_tensor_at(name, [P] + shape, dt, offset=base + int(kib * 1024))

    ident = at("ident", [P], 0)
    ones = at("ones", [P], 0.5)
    bdones = at("bdones", [P], 1)
    m_strict = at("m_strict", [P], 1.5)
    m_incl = at("m_incl", [P], 2)
    m_1 = at("m_1", [P], 2.5)
    m_1t = at("m_1t", [P], 3)
    m_lev = [at(f"m_lev{b}", [P], 3.5 + 0.5 * i) for i, b in enumerate(LEVELS)]
    scanm = at("scanm", [T], 6)
    par = at("par", [NCOLS], 8)
    sinkT = at("sinkT", [8], 9)
    lnw_bc = None
    wc = at("wc", [KC, NCH], 9.25)
    raw = at("raw", [2, KC, P], 10)
    whi = at("whi", [2, KC, P], 18, F32R)
    wlo = at("wlo", [2, KC, P], 26, F32R)
    r1h, r1l = at("r1h", [KC, T], 34, F32R), at("r1l", [KC, T], 50, F32R)
    r2h, r2l = at("r2h", [KC, T], 66, F32R), at("r2l", [KC, T], 82, F32R)
    xs = at("xs", [KC, T], 98)
    q = at("q", [4, NCH, 2, CH], 98)
    kb = at("kb", [2, 2, 2, 4, P], 114)
    v1 = at("v1", [4, P], 130)
    v2 = at("v2", [4, P], 132)
    bias = at("bias", [8, 192], 134)
    lg = at("lg", [2, 8, P], 146)
    pT = at("pT", [2, 8, P], 154)
    kT = at("kT", [T], 162)
    vT = at("vT", [T], 164)
    b0 = at("b0", [KC, T], 166)
    beta = at("beta", [BETA], 182)
    oneh = at("oneh", [BETA], 183)
    relb = at("relb", [16], 184)
    asm = at("asm", [2, 5, 8], 185)
    sqt = at("sqt", [2, T], 194)
    hx = at("hx", [2, T], 198)
    rst = at("rst", [2, T], 202)
    tl = at("tl", [T], 202)
    sg = at("sg", [2, T], 204)
    ar = at("ar", [2, KC, T], 66)
    bt = at("bt", [KC, T], 98)
    kt = at("kt", [KC, T], 114)
    vb = at("vb", [KC, T], 130)
    bv = at("bv", [KC, T], 146)
    wl = at("wl", [2, 2, P], 162)
    tmp = {n: at("t_" + n, [T], 164 + 2 * i) for i, n in enumerate(
        ["kS", "rS", "tw", "ld", "cum", "cx", "ta", "t", "kp", "aa", "eW", "eWi", "eWx", "b0",
         "sq", "ssm", "nrm", "inv", "p"])}
    U2 = {}
    for i, n in enumerate(["aab", "aak", "arb", "ark", "X", "XT", "Qs", "BDa", "BDr", "BDb", "BDk", "VD"]):
        U2[n] = [at(f"u_{n}{h}", [4, P], 146 + 2 * (2 * i + h)) for h in range(2)]
    U2["AI"] = U2["Qs"]
    U2["btok"], U2["ktok"] = U2["BDb"], U2["BDk"]
    for i, n in enumerate(["Vc", "Y", "Yt", "St"]):
        U2[n] = [at(f"u_{n}{h}", [4, HD], 194 + 2 * i + h) for h in range(2)]
    for i, n in enumerate(["G", "U"]):
        U2[n] = [at(f"u_{n}{h}", [4, HD], 190 + 2 * h + i) for h in range(2)]
    gs = at("gs", [2, T], 202)
    gn = at("gn", [2, 4, 4], 206)
    wg = at("wg", [2, D], 98)
    bvb = at("bvb", [KC, T], 106)
    sgb = at("sgb", [2, T], 122)
    b0b, t0b, t1b = (at(n, [KC, T], 146 + 16 * i) for i, n in enumerate(("b0b", "t0b", "t1b")))
    mix = at("mix", [KC, T], 98)
    xr = at("xr", [KC, T], 114)
    fh = at("fh", [KB * KC, T], 66, F32R)
    fl = at("fl", [KB * KC, T], 130, F32R)
    ob = at("ob", [KC, T], 34)
    x1 = at("x1", [KC, T], 50)

    b0_d, bv_d, t0_d, t1_d = (nc.dram_tensor(n, [P, KC, T], F32, kind="Internal").ap()
                              for n in ("b0_d", "bv_d", "t0_d", "t1_d"))
    sg_d = nc.dram_tensor("sg_d", [P, 2 * T], F32, kind="Internal").ap()
    x1_d = nc.dram_tensor("x1_d", [P, KC * T], F32, kind="Internal").ap()
    beta_t = nc.dram_tensor("beta_d", [16, CH, BETA], F32, kind="Internal")
    beta_d = beta_t.ap()

    B = [nc.alloc_psum_tensor(f"bank{i}", [P, T], F32) for i in range(8)]

    def slabs(w):
        return w.rearrange("(kc p) n -> p kc n", p=P)

    win_s, wout_s, wup_s = slabs(w_in), slabs(w_out), slabs(w_up)
    wbr_s = [slabs(w_br[0]), slabs(w_br[1])]
    wdn_s = [slabs(w_down[D * b:D * (b + 1), :]) for b in range(KB)]

    def col(name, m):
        c = COL[name] if name in COL else name
        return par[:, c + m:c + m + 1] if isinstance(m, int) else par[:, bass.ds(c + m, 1)]

    def pcol(c0, m):
        return par[:, c0 + m:c0 + m + 1] if isinstance(m, int) else par[:, bass.ds(c0 + m, 1)]

    def flat(t):
        return t[:].rearrange("p a b -> p (a b)")

    def bc2(ap):
        return ap.unsqueeze(2).to_broadcast([P, 4, 2, CH])

    def mask4(t):
        return t[:].rearrange("p (e t) -> p e t", e=2).unsqueeze(1).to_broadcast([P, 4, 2, CH])

    def mask4f(t):
        return t[:].unsqueeze(1).to_broadcast([P, 4, P])

    def v4(bank):
        return bank[:].rearrange("p (m n) -> p m n", m=4)

    block = nc.Block()
    block.__enter__()

    @block.sync
    def _(sp):
        def slab(n, slot, count, src):
            if not isinstance(n, int) or n >= 2:
                sp.wait_ge(S("w_split"), n - 1)
            sp.dma_start(raw[:, slot, :, :], src).then_inc(S(f"w_raw{slot}"), 16)

        sp.dma_start(xs[:], xT).then_inc(S("x_in"), 16)
        sp.dma_start(par[:, 0:NCOL], cols).then_inc(S("par_in"), 16)
        for n in range(13):
            c0 = ([L0, L0 + P, L0 + 2 * P, K0, V0] + [Q0 + P * j for j in range(8)])[n]
            slab(n, n % 2, n // 2, win_s[:, :, c0:c0 + P])
            if n == 1:
                sp.dma_start(sinkT[:], sinks).then_inc(S("tab_in"), 16)
                sp.dma_start(oneh[0:32, :], onehot).then_inc(S("tab_in"), 16)
                sp.dma_start(relb[0:32, :], rel_bias).then_inc(S("tab_in"), 16)

        def tiles(n0, src, c0):
            with sp.Fori(0, 4) as i:
                for h in range(2):
                    slab(2 * i + (n0 + h), (n0 + h) % 2, None, src[:, :, bass.ds(i * (2 * P) + (c0 + P * h), P)])

        tiles(N_B0, wbr_s[0], 0)
        sp.wait_ge(S("wl_zero"), 1)
        sp.wait_ge(S("tile_ev"), E_GATE)
        with sp.Fori(0, 4) as i:
            for h in range(2):
                sp.wait_ge(S("a_mm"), 2 * i + (h + 1))
                sp.dma_start(wl[0:64, h, 0, :], wdec[:, bass.ds(i * (2 * P) + P * h, P)]).then_inc(S(f"wl{h}"), 16)
                sp.dma_start(wl[64:128, h, 1, :], waaa[:, bass.ds(i * (2 * P) + P * h, P)]).then_inc(S(f"wl{h}"), 16)
                for j, c0 in enumerate((RK0, R0, RV0)):
                    slab(6 * i + (N_PAIR + 3 * h + j), (N_PAIR + 3 * h + j) % 2, None,
                         win_s[:, :, bass.ds(i * (2 * P) + (c0 + P * h), P)])
        with sp.Fori(0, NCH) as c:
            for h in range(2):
                slab(2 * c + (N_GATE + h), (N_GATE + h) % 2, None, win_s[:, :, bass.ds(c * P + (G0 + D * h), P)])
        tiles(N_B1, wbr_s[1], 0)
        tiles(N_OUT, wout_s, 0)
        with sp.Fori(0, 16) as i:
            for h in range(2):
                slab(2 * i + (N_UP + h), (N_UP + h) % 2, None, wup_s[:, :, bass.ds(i * (2 * P) + P * h, P)])
        with sp.Fori(0, 8) as j:
            for b in range(KB):
                slab(4 * j + (N_DOWN + b), (N_DOWN + b) % 2, None, wdn_s[b][:, :, bass.ds(j * P, P)])
        sp.wait_ge(S("o_ready"), 8)
        sp.dma_start(out, ob[:]).then_inc(S("out_done"), 16)
        sp.wait_ge(S("out_done"), 16)

    @block.gpsimd
    def _(pool):
        ms = nc.gpsimd.memset
        for t, v in ((ident, 0.0), (ones, 1.0), (bdones, 1.0), (m_strict, 1.0), (m_incl, 1.0), (scanm, 1.0),
                     (m_1, 1.0), (m_1t, 1.0), *((m, 1.0) for m in m_lev)):
            ms(t[:], v).then_inc(S("set"), 1)
        pool.wait_ge(S("set"), 8 + len(LEVELS))

        def split(n, slot):
            pool.wait_ge(S("w_hi"), n + 1)
            nc.gpsimd.tensor_tensor(wlo[:, slot, :, :], raw[:, slot, :, :], whi[:, slot, :, :].bitcast(F32),
                                    ALU.subtract).then_inc(S("w_split"), 1)

        sel = nc.gpsimd.affine_select

        def keep(view, base_, pattern, mult, op=ALU.is_ge, fill=0.0):
            return sel(out=view, in_=view, compare_op=op, fill=fill, base=base_, pattern=pattern,
                       channel_multiplier=mult)

        keep(ident[:], 0, [[-1, P]], 1, ALU.not_equal, 1.0).then_inc(S("ident"), 1)
        keep(scanm[:].rearrange("p (c t) -> p c t", c=NCH), 0, [[0, NCH], [1, CH]], 0,
             ALU.not_equal, 0.0).then_inc(S("masks"), 1)
        nm = [1]

        def step(ins):
            ins.then_inc(S("masks"), 1)
            nm[0] += 1
            pool.wait_ge(S("masks"), nm[0])

        def blocks(m, b):
            v = m[:].rearrange("p (n r) -> p n r", r=b)
            step(keep(v, 0, [[-b, P // b], [0, b]], 1))
            step(keep(v, b - 1, [[b, P // b], [0, b]], -1))

        blocks(bdones, CH)
        blocks(m_strict, CH)
        step(keep(m_strict[:], -1, [[1, P]], -1))
        blocks(m_incl, CH)
        step(keep(m_incl[:], 0, [[1, P]], -1))
        blocks(m_1, 2)
        step(keep(m_1[:], 0, [[-1, P]], 1))
        blocks(m_1t, 2)
        step(keep(m_1t[:], 0, [[1, P]], -1))
        for m, b in zip(m_lev, LEVELS):
            blocks(m, 2 * b)
            v = m[:].rearrange("p (n r) -> p n r", r=2 * b)
            step(keep(v, -b, [[-2 * b, P // (2 * b)], [0, 2 * b]], 1))
            step(keep(v, b - 1, [[0, P // (2 * b)], [-1, 2 * b]], 0))

        split(0, 0)
        with pool.Fori(0, 23) as i:
            for h in range(2):
                split(2 * i + (1 + h), (1 + h) % 2)

        pool.wait_ge(S("bv"), 9)
        with pool.Fori(0, NCH) as c:
            for h in range(2):
                pool.wait_ge(S(f"dS_mm{h}"), c + 1)
                pool.sem_inc(S("bd_go"), 1)
                tk = bass.ds(c * CH, CH)
                for n, src in (("BDb", bt), ("BDk", kt), ("BDa", ar[:, 0]), ("BDr", ar[:, 1])):
                    nc.gpsimd.tensor_tensor(U2[n][h][:].rearrange("p m (e t) -> p m e t", e=2),
                                            bc2(src[:, 4 * h:4 * h + 4, tk]), mask4(bdones), ALU.mult) \
                        .then_inc(S(f"bd{h}"), 1)
                nc.gpsimd.tensor_copy(U2["VD"][h][:].rearrange("p m (e t) -> p m e t", e=2),
                                      bc2(vb[:, 4 * h:4 * h + 4, tk])).then_inc(S(f"bd{h}"), 1)
            for h in range(2):
                split(2 * c + (N_GATE + 2 + h), (N_GATE + h) % 2)
        with pool.Fori(0, 39) as i:
            for h in range(2):
                split(2 * i + (63 + h), (63 + h) % 2)

    @block.tensor
    def _(pe):
        mm = nc.tensor.matmul

        for n_ in ("w_mm", "a_mm", "ss_mm", "bon_mm", "dS_mm0", "dS_mm1"):
            pe.sem_inc(S(n_), 1)

        def slab_mm(n, slot, bank, hi, lo, M=P, first=True, last=True, kc0=0, fresh=None):
            pe.wait_ge(S("w_split"), n + 1)
            for kc in range(KC):
                if fresh is not None:
                    pe.wait_ge(S("x_lo"), fresh + kc + 1)
                for k, (w, x) in enumerate(((whi, hi), (whi, lo), (wlo, hi))):
                    r = mm(bank[0:M, :], w[:, slot, kc, 0:M], x[:, kc0 + kc, :],
                           start=(first and kc == 0 and k == 0), stop=(last and kc == KC - 1 and k == 2))
            return r

        def rms(norm, bank):
            for kc in range(KC):
                pe.wait_ge(S("rms_sq"), norm + kc + 1)
                mm(bank[:], ones[:], sqt[:, kc % 2, :], start=(kc == 0), stop=(kc == KC - 1)) \
                    .then_inc(S("rms_mm"), 1)

        pe.wait_ge(S("set"), 8 + len(LEVELS))
        rms(N1, B[7])

        pe.wait_ge(S("tab_in"), 48)
        mm(B[6][0:16, 0:BETA], relb[0:32, :], oneh[0:32, :], start=True, stop=True).then_inc(S("small_mm"), 1)
        for n in range(13):
            if 2 <= n < 5:
                pe.wait_ge(S("lo_sh"), n - 1)
            elif n >= 5:
                pe.wait_ge(S("tile_ev"), n - 4)
            slab_mm(n, n % 2, B[n % 2], r1h, r1l, M=32 if n == 2 else P,
                    fresh=SP_H if n == 0 else None).then_inc(S("slab_mm"), 1)
            if n == 5:
                pe.wait_ge(S("vT"), 1)
                pe.wait_ge(S("ident"), 1)
                for t in range(4):
                    r = nc.tensor.transpose(B[2][:, P * t:P * t + P], vT[:, P * t:P * t + P], ident[:])
                r.then_inc(S("small_mm"), 1)

        def tiles(n0, hi, lo, ev):
            with pe.Fori(0, 4) as i:
                for h in range(2):
                    pe.wait_ge(S("tile_ev"), 2 * i + (ev + h - 1))
                    slab_mm(2 * i + (n0 + h), (n0 + h) % 2, B[h], hi, lo).then_inc(S("slab_mm"), 1)

        pe.wait_ge(S("tile_ev"), 10)

        def scores(c):
            o, t = c % 2, c // 2
            if c == 0:
                pe.wait_ge(S("kb_in"), 16 * 12)
                pe.wait_ge(S("tile_ev"), 10)
            b0 = 2 + 2 * (c % 2)
            if c >= 2:
                pe.wait_ge(S("at_lg"), 2 * (c - 1))
            for j in range(4):
                r = mm(B[b0 + j // 2][:].rearrange("p (a n) -> p a n", a=2)[:, j % 2, :],
                       q[:, j, c, :, :].rearrange("p e t -> p (e t)"),
                       kb[:, o, j // 2, :, t, :], start=True, stop=True)
            r.then_inc(S("at_sc"), 1)

        def probs_values(c):
            pe.wait_ge(S("at_p"), c + 1)
            for g in range(8):
                r = nc.tensor.transpose(B[6 + g // 4][:, P * (g % 4):P * (g % 4) + P], lg[:, c % 2, g, :], ident[:])
            r.then_inc(S("at_tr"), 1)
            pe.wait_ge(S("at_pT"), 2 * c + 2)
            if c >= 1:
                pe.wait_ge(S("at_lo"), c)
            vv = (v2, v1)[c % 2]
            for g in range(2):
                for p in range(2):
                    r = mm(B[0][64 * p:64 * p + 64, 256 * g:256 * g + 256],
                           vv[:, c // 2, 64 * g:64 * g + 64],
                           pT[:, c % 2, :, :].rearrange("k (j p) q -> k j p q", p=2)[:, 2 * g:2 * g + 2, p, :],
                           start=True, stop=True)
            r.then_inc(S("at_o"), 1)

        pe.wait_ge(S("v_ready"), 3)
        pe.wait_ge(S("beta_ev"), 1)
        scores(0)
        for c in range(NCH):
            if c + 1 < NCH:
                scores(c + 1)
            probs_values(c)
        pe.wait_ge(S("at_lo"), NCH)
        tiles(N_B0, r2h, r2l, E_B0)

        pe.wait_ge(S("tile_ev"), E_GATE)
        pe.wait_ge(S("masks"), 1 + 2 + 3 + 3 + 3 + 3 + 4 * len(LEVELS))
        with pe.Fori(0, 4) as i:
            for h in range(2):
                m = 2 * i + h
                n = 6 * i + (N_PAIR + 3 * h)
                s0 = (N_PAIR + 3 * h) % 2
                pe.wait_ge(S("k_sh"), m + 1)
                slab_mm(n, s0, B[0], r1h, r1l).then_inc(S("slab_mm"), 1)
                pe.wait_ge(S(f"wl{h}"), i * 32 + 32)
                pe.wait_ge(S("tw"), m + 1)
                mm(B[1][:], wl[:, h, 0, :], tl[:], start=True, stop=True).then_inc(S("w_mm"), 1)
                pe.wait_ge(S("ta"), m + 1)
                mm(B[2][:], wl[:, h, 1, :], tl[:], start=True, stop=True).then_inc(S("a_mm"), 1)
                pe.wait_ge(S("r_sh"), m + 1)
                slab_mm(n + 1, (s0 + 1) % 2, B[3], r1h, r1l).then_inc(S("slab_mm"), 1)
                pe.wait_ge(S("sq"), m + 2)
                pe.wait_ge(S("ssm"), m + 1)
                mm(B[4][:], bdones[:], tmp["sq"][:], start=True, stop=True).then_inc(S("ss_mm"), 1)
                pe.wait_ge(S("v_sh"), m + 1)
                slab_mm(n + 2, s0, B[5], r1h, r1l).then_inc(S("slab_mm"), 1)
                pe.wait_ge(S("p"), m + 2)
                pe.wait_ge(S("bv"), m + 1)
                mm(B[6][:], bdones[:], tmp["p"][:], start=True, stop=True).then_inc(S("bon_mm"), 1)


        pe.wait_ge(S("bv"), 9)
        pe.wait_ge(S("st_zero"), 2)
        with pe.Fori(0, NCH) as c:
            tk = bass.ds(c * CH, CH)
            tr = nc.tensor.transpose

            def each(h, body):
                for m in range(4):
                    r = body(m)
                return r

            def out4(bank, m):
                return v4(bank)[:, m, :]

            pe.wait_ge(S("tile_ev"), 2 * c + E_GATE)
            slab_mm(2 * c + N_GATE, N_GATE % 2, B[6], r1h, r1l).then_inc(S("slab_mm"), 1)
            for h in range(2):
                b = B[3 * h:3 * h + 3]
                pe.wait_ge(S(f"bd{h}"), c * 5 + 5)
                pe.wait_ge(S(f"y_read{h}"), c + 1)
                for n, k in (("BDb", 0), ("BDk", 1)):
                    for m in range(4):
                        r = mm(v4(b[k])[:, m, :].rearrange("p (x t) -> p x t", x=2), U2[n][h][:, m, :],
                               ar[:, :, 4 * h + m, tk], start=True, stop=True)
                    r.then_inc(S(f"sc_mm{h}"), 1)
            slab_mm(2 * c + (N_GATE + 1), (N_GATE + 1) % 2, B[7], r1h, r1l).then_inc(S("slab_mm"), 1)
            for h in range(2):
                b = B[3 * h:3 * h + 3]
                pe.wait_ge(S(f"sc_ev{h}"), c * 5 + 5)
                each(h, lambda m: tr(out4(b[2], m), U2["AI"][h][:, m, :], ident[:])).then_inc(S(f"ai_mm{h}"), 1)
                each(h, lambda m: tr(out4(b[0], m), U2["BDb"][h][:, m, :], ident[:])).then_inc(S(f"tok_mm{h}"), 1)
                each(h, lambda m: tr(out4(b[1], m), U2["BDk"][h][:, m, :], ident[:])).then_inc(S(f"tok_mm{h}"), 1)
            for h in range(2):
                b = B[3 * h:3 * h + 3]
                pe.wait_ge(S(f"tok_ev{h}"), c * 4 + 1)
                each(h, lambda m: tr(out4(b[0], m), U2["VD"][h][:, m, :], ident[:])).then_inc(S(f"tok_mm{h}"), 1)
            for k in range(len(LEVELS)):
                for h in range(2):
                    b = B[3 * h:3 * h + 3]
                    pe.wait_ge(S(f"x_ready{h}"), c * 5 + (k + 1))
                    each(h, lambda m: mm(out4(b[2], m), U2["aab"][h][:, m, :], U2["X"][h][:, m, :],
                                         start=True, stop=True)).then_inc(S(f"q_mm{h}"), 1)
                for h in range(2):
                    b = B[3 * h:3 * h + 3]
                    pe.wait_ge(S(f"q_ev{h}"), c * 5 + (k + 1))
                    pe.wait_ge(S(f"xt_ready{h}"), c * 5 + (k + 1))
                    if k == 0:
                        pe.wait_ge(S(f"tok_ev{h}"), c * 4 + 4)
                    if k < len(LEVELS) - 1:
                        each(h, lambda m: mm(out4(b[1], m), U2["XT"][h][:, m, :], U2["Qs"][h][:, m, :],
                                             start=True, stop=True)).then_inc(S(f"d_mm{h}"), 1)
                    else:
                        each(h, lambda m: mm(out4(b[1], m), U2["Qs"][h][:, m, :], U2["XT"][h][:, m, :],
                                             start=True, stop=True)).then_inc(S(f"d_mm{h}"), 1)
                if k < len(LEVELS) - 1:
                    for h in range(2):
                        b = B[3 * h:3 * h + 3]
                        pe.wait_ge(S(f"x_ready{h}"), c * 5 + (k + 2))
                        each(h, lambda m: tr(out4(b[0], m), U2["X"][h][:, m, :], ident[:])) \
                            .then_inc(S(f"xt_mm{h}"), 1)

            def o64(bank, m):
                return bank[:].rearrange("p (m n) -> p m n", n=CH)[:, m, :]

            for h in range(2):
                b = B[3 * h:3 * h + 3]
                pe.wait_ge(S(f"st{h}"), c + 1)
                for m in range(4):
                    mm(o64(b[0], m), U2["BDa"][h][:, m, :], U2["St"][h][:, m, :], start=True, stop=False)
                    r = mm(o64(b[0], m), U2["aak"][h][:, m, :], U2["Vc"][h][:, m, :], start=False, stop=True)
                r.then_inc(S(f"g_mm{h}"), 1)
            for h in range(2):
                b = B[3 * h:3 * h + 3]
                pe.wait_ge(S(f"g_ev{h}"), c + 1)
                pe.wait_ge(S(f"xt_last{h}"), c + 1)
                for m in range(4):
                    r = mm(o64(b[2], m), U2["XT"][h][:, m, :], U2["G"][h][:, m, :], start=True, stop=True)
                r.then_inc(S(f"u_mm{h}"), 1)
            for h in range(2):
                b = B[3 * h:3 * h + 3]
                pe.wait_ge(S(f"u_ev{h}"), c + 1)
                for m in range(4):
                    mm(o64(b[1], m), U2["BDr"][h][:, m, :], U2["St"][h][:, m, :], start=True, stop=False)
                    mm(o64(b[1], m), U2["arb"][h][:, m, :], U2["U"][h][:, m, :], start=False, stop=False)
                    r = mm(o64(b[1], m), U2["ark"][h][:, m, :], U2["Vc"][h][:, m, :], start=False, stop=True)
                r.then_inc(S(f"y_mm{h}"), 1)
                for m in range(4):
                    mm(o64(b[0], m), U2["btok"][h][:, m, :], U2["U"][h][:, m, :], start=True, stop=False)
                    r = mm(o64(b[0], m), U2["ktok"][h][:, m, :], U2["Vc"][h][:, m, :], start=False, stop=True)
                r.then_inc(S(f"dS_mm{h}"), 1)
            for h in range(2):
                pe.wait_ge(S(f"yn{h}"), c + 1)
                for m in range(4):
                    for e in range(2):
                        r = mm(B[3 * h + 2][64 * e:64 * e + 64, CH * m:CH * m + CH], U2["Y"][h][:, m, :],
                               ident[:, 64 * e:64 * e + 64], start=True, stop=True)
                r.then_inc(S(f"yt_mm{h}"), 1)

        pe.wait_ge(S("y_read0"), 9)
        pe.wait_ge(S("y_read1"), 9)
        pe.wait_ge(S("back_in"), 64)
        for m in range(KC):
            if m >= 2:
                pe.wait_ge(S("x_f"), SP_Y + m - 1)
            mm(B[m % 2][:], wg[:, 0, P * m:P * m + P], sgb[:, 0, :], start=True, stop=False)
            mm(B[m % 2][:], wg[0:32, 1, P * m:P * m + P], sgb[0:32, 1, :], start=False, stop=True) \
                .then_inc(S("g_mm"), 1)
        pe.wait_ge(S("x_lo"), SP_Y + 8)
        tiles(N_B1, r1h, r1l, E_B1)
        pe.wait_ge(S("x_lo"), SP_M + 8)
        tiles(N_OUT, r2h, r2l, E_OUT)
        rms(N2, B[7])
        rms(N3, B[6])
        pe.wait_ge(S("x_lo"), SP_F + 8)
        with pe.Fori(0, 16) as i:
            for h in range(2):
                pe.wait_ge(S("tile_ev"), 2 * i + (E_UP + h - 1))
                slab_mm(2 * i + (N_UP + h), (N_UP + h) % 2, B[h], r1h, r1l).then_inc(S("slab_mm"), 1)
        pe.wait_ge(S("f_lo"), 32)
        with pe.Fori(0, 4) as i:
            for h in range(2):
                pe.wait_ge(S("tile_ev"), 2 * i + (E_DOWN + h - 1))
                for b in range(KB):
                    slab_mm(8 * i + (N_DOWN + 4 * h + b), (N_DOWN + b) % 2, B[2 + h], fh, fl,
                            first=(b == 0), last=(b == KB - 1), kc0=KC * b).then_inc(S("slab_mm"), 1)
        rms(N4, B[7])

    @block.scalar
    def _(act):
        A = nc.scalar.activation

        act.sem_inc(S("gate_out0"), 16)
        act.sem_inc(S("gate_out1"), 16)
        for n_ in ("k_sc", "tw", "ta", "sq", "eW", "eWi", "eWx", "r_sc", "nrm", "v_sc"):
            act.sem_inc(S(n_), 1)

        def rms_sq(norm, src, ready):
            for kc in range(KC):
                if ready:
                    act.wait_ge(S(ready), kc + 1)
                if kc >= 2:
                    act.wait_ge(S("rms_mm"), norm + kc - 1)
                A(sqt[:, kc % 2, :], src[:, kc, :], ACT.Square).then_inc(S("rms_sq"), 1)

        def rms_root(norm):
            act.wait_ge(S("rms_rec"), norm // 8 + 1)
            A(rst[:, 1, :], rst[:, 0, :], ACT.Sqrt).then_inc(S("rms_root"), 1)

        def split_hi(sp_, hi):
            for kc in range(KC):
                act.wait_ge(S("x_f"), sp_ + kc + 1)
                A(hi[:, kc, :], hx[:, kc % 2, :], ACT.Copy).then_inc(S("x_hi"), 1)

        def w_hi(n, slot, count):
            act.wait_ge(S(f"w_raw{slot}"), count)
            A(whi[:, slot, :, :], raw[:, slot, :, :], ACT.Copy).then_inc(S("w_hi"), 1)

        def after(n0, i, k, per):
            act.wait_ge(S("slab_mm"), per * i + (n0 + k + 1))
            w_hi(None, (n0 + k) % 2, i * (8 * per) + 16 * ((n0 + k + 2) // 2 + 1))

        act.wait_ge(S("x_in"), 16)
        rms_sq(N1, xs, None)
        rms_root(N1)
        split_hi(SP_H, r1h)
        w_hi(0, 0, 16)
        w_hi(1, 1, 16)
        act.wait_ge(S("beta_ev"), 1)
        act.dma_start(beta_d, beta[0:16, :].unsqueeze(1).to_broadcast([16, CH, BETA])).then_inc(S("beta_out"), 16)
        act.wait_ge(S("beta_out"), 16)
        for e in range(2):
            for p in range(2):
                hstep = CH * BETA
                for lo_, dst0 in ((0, 0), (1, 128)):
                    n = 128 if lo_ == 0 else 64
                    src = bass.AP(tensor=beta_t, offset=(2 * e + p) * hstep + CH - 1,
                                  ap=[[BETA - 1, CH], [4 * hstep, 4], [1, n]])
                    act.dma_start(bias[64 * e:64 * e + 64, p:8:2, dst0:dst0 + n], src).then_inc(S("bias_in"), 16)

        for n in range(13):
            act.wait_ge(S("slab_mm"), n + 1)
            w_hi(n + 2, n % 2, 16 * ((n + 2) // 2 + 1))
            b = B[n % 2]
            if n < 3:
                M = 32 if n == 2 else P
                dst = (tl, sg[:, 0, :], sg[:, 1, :])[n]
                dst = dst[0:M, :]
                A(dst, b[0:M, :], ACT.Copy, scale=par[0:M, OM_L + n:OM_L + n + 1]).then_inc(S("lo_sc"), 1)
                act.wait_ge(S("lo_sh"), n + 1)
                if n == 0:
                    A(tl[0:64, :], tl[0:64, :], ACT.Tanh).then_inc(S("lo_th"), 1)
                else:
                    A(dst, dst, ACT.Tanh, scale=0.5).then_inc(S("lo_th"), 1)
            elif n == 3:
                A(kT[:], b[:], ACT.Copy).then_inc(S("tile_ev"), 1)
                act.wait_ge(S("tile_ev"), 1)
                act.wait_ge(S("kb_zero"), 1)
                for o in range(2):
                    for g in range(2):
                        for p in range(2):
                            ksrc = kT[64 * g:64 * g + 64, :].rearrange("d (t x) -> d t x", x=P)
                            kdst = kb[64 * p:64 * p + 64, o, g, p, :, :]
                            if o == 1:
                                act.dma_start(kdst, ksrc).then_inc(S("kb_in"), 16)
                            else:
                                act.dma_start(kdst[:, :, 0:64], ksrc[:, :, 0:64]).then_inc(S("kb_in"), 16)
                                act.dma_start(kdst[:, 1:4, 64:128], ksrc[:, 0:3, 64:128]).then_inc(S("kb_in"), 16)
            elif n == 4:
                A(vT[:], b[:], ACT.Copy).then_inc(S("vT"), 1)
                act.wait_ge(S("vT"), 1)
                act.sem_inc(S("tile_ev"), 1)
            else:
                A(q[:, (n - 5) // 2, :, (n - 5) % 2, :], b[:].rearrange("p (c t) -> p c t", c=NCH), ACT.Copy) \
                    .then_inc(S("tile_ev"), 1)

        for c in range(NCH):
            act.wait_ge(S("at_sub"), c + 1)
            A(lg[:, c % 2, :, :], lg[:, c % 2, :, :], ACT.Exp).then_inc(S("at_exp"), 1)
            A(asm[:, c % 2, 1, :], asm[:, c % 2, 1, :], ACT.Exp).then_inc(S("at_exs"), 1)
            act.wait_ge(S("at_tr"), c + 1)
            for k in range(2):
                A(pT[:, c % 2, 4 * k:4 * k + 4, :], v4(B[6 + k]), ACT.Copy).then_inc(S("at_pT"), 1)
            act.wait_ge(S("at_o"), c + 1)
            A(r2h[:, :, CH * c:CH * c + CH], B[0][:].rearrange("p (m t) -> p m t", m=KC), ACT.Copy) \
                .then_inc(S("at_hi"), 1)
        with act.Fori(0, 4) as i:
            for h in range(2):
                after(N_B0, i, h, 2)
        act.wait_ge(S("tile_ev"), E_GATE)
        act.dma_start(b0_d, b0[:]).then_inc(S("spilled"), 16)
        act.dma_start(sg_d[:, 0:T], sg[:, 0, :]).then_inc(S("spilled"), 16)
        act.dma_start(sg_d[0:32, T:2 * T], sg[0:32, 1, :]).then_inc(S("spilled"), 16)
        act.wait_ge(S("spilled"), 48)

        with act.Fori(0, 4) as i:
            for h in range(2):
                m = 2 * i + h
                n = 6 * i + (N_PAIR + 3 * h)
                after(N_PAIR, i, 3 * h, 6)
                act.wait_ge(S("ax"), m + 1)
                A(tmp["kS"][:], B[0][:], ACT.Copy, scale=pcol(OM_K, m)).then_inc(S("k_sc"), 1)
                act.wait_ge(S("w_mm"), m + 2)
                act.wait_ge(S("ld"), m + 1)
                A(tmp["tw"][:], B[1][:], ACT.Tanh, scale=0.5, bias=pcol(H_W0, m)).then_inc(S("tw"), 1)
                act.wait_ge(S("a_mm"), m + 2)
                act.wait_ge(S("aa"), m + 1)
                A(tmp["ta"][:], B[2][:], ACT.Tanh, scale=0.5, bias=pcol(H_A0, m)).then_inc(S("ta"), 1)
                act.wait_ge(S("k_sh"), m + 2)
                act.wait_ge(S("ss_mm"), m + 1)
                A(tmp["sq"][:], tmp["kS"][:], ACT.Square, scale=pcol(COL["k_k"], m)).then_inc(S("sq"), 1)
                act.wait_ge(S("cum"), m + 2)
                act.wait_ge(S("wc"), m + 1)
                A(tmp["eW"][:], tmp["cum"][:], ACT.Exp).then_inc(S("eW"), 1)
                act.wait_ge(S("bt"), m + 1)
                A(tmp["eWi"][:], tmp["cum"][:], ACT.Exp, scale=-1.0).then_inc(S("eWi"), 1)
                act.wait_ge(S("cx"), m + 2)
                act.wait_ge(S("at"), m + 1)
                A(tmp["eWx"][:], tmp["cx"][:], ACT.Exp).then_inc(S("eWx"), 1)
                after(N_PAIR, i, 3 * h + 1, 6)
                act.wait_ge(S("p"), m + 1)
                A(tmp["rS"][:], B[3][:], ACT.Copy, scale=pcol(OM_R, m)).then_inc(S("r_sc"), 1)
                act.wait_ge(S("ssm"), m + 2)
                act.wait_ge(S("inv"), m + 1)
                A(tmp["nrm"][:], tmp["ssm"][:], ACT.Sqrt).then_inc(S("nrm"), 1)
                after(N_PAIR, i, 3 * h + 2, 6)
                A(vb[:, m, :], B[5][:], ACT.Copy, scale=pcol(OM_V, m)).then_inc(S("v_sc"), 1)

        act.wait_ge(S("bv"), 9)
        act.dma_start(bv_d, bv[:]).then_inc(S("spilled"), 16)
        act.wait_ge(S("spilled"), 64)

        with act.Fori(0, NCH) as c:
            def gate_out(h, dst):
                act.wait_ge(S("tile_ev"), 2 * c + (E_GATE + h + 1))
                act.dma_start(dst[:, bass.ds(c, 1), :].rearrange("p a t -> p (a t)"), gs[:, h, :]) \
                    .then_inc(S(f"gate_out{h}"), 16)

            for h, hgb in ((0, H_GB0), (1, H_GB1)):
                after(N_GATE, c, h, 2)
                act.wait_ge(S(f"gate_out{h}"), c * 16 + 16)
                A(gs[:, h, :], B[6 + h][:], ACT.Tanh, scale=0.5, bias=pcol(hgb, c)).then_inc(S("tile_ev"), 1)
                if h == 0:
                    gate_out(0, t0_d)
            for h in range(2):
                b = B[3 * h:3 * h + 3]
                act.wait_ge(S(f"tok_mm{h}"), c * 3 + 1)
                A(U2["btok"][h][:], v4(b[0]), ACT.Copy).then_inc(S(f"tok_ev{h}"), 1)
                act.wait_ge(S(f"tok_mm{h}"), c * 3 + 2)
                A(U2["ktok"][h][:], v4(b[1]), ACT.Copy).then_inc(S(f"tok_ev{h}"), 1)
            for h in range(2):
                b = B[3 * h:3 * h + 3]
                act.wait_ge(S(f"tok_mm{h}"), c * 3 + 3)
                for e in range(2):
                    A(U2["Vc"][h][64 * e:64 * e + 64, :, :], v4(b[0])[64 * e:64 * e + 64, :, 64 * e:64 * e + 64],
                      ACT.Copy).then_inc(S(f"tok_ev{h}"), 1)
            gate_out(1, t1_d)
            for k in range(len(LEVELS) - 1):
                for h in range(2):
                    act.wait_ge(S(f"xt_mm{h}"), c * 4 + (k + 1))
                    A(U2["XT"][h][:], v4(B[3 * h]), ACT.Copy).then_inc(S(f"xt_ready{h}"), 1)
            for h in range(2):
                act.wait_ge(S(f"g_mm{h}"), c + 1)
                A(U2["G"][h][:], B[3 * h][:, 0:256].rearrange("p (m i) -> p m i", m=4), ACT.Copy) \
                    .then_inc(S(f"g_ev{h}"), 1)
            for h in range(2):
                act.wait_ge(S(f"u_mm{h}"), c + 1)
                A(U2["U"][h][:], B[3 * h + 2][:, 0:256].rearrange("p (m i) -> p m i", m=4), ACT.Copy) \
                    .then_inc(S(f"u_ev{h}"), 1)
            for h in range(2):
                act.wait_ge(S(f"yc{h}"), c + 1)
                A(U2["Yt"][h][:], U2["Y"][h][:], ACT.Square).then_inc(S(f"ysq{h}"), 1)
            for h in range(2):
                act.wait_ge(S(f"yv{h}"), c + 1)
                A(gn[:, h, 3, :], gn[:, h, 2, :], ACT.Sqrt).then_inc(S(f"yr{h}"), 1)

        act.wait_ge(S("y_read0"), 9)
        act.wait_ge(S("y_read1"), 9)
        act.dma_start(wg[:, 0, :], wgate[0:P, :]).then_inc(S("back_in"), 16)
        act.dma_start(wg[0:32, 1, :], wgate[P:P + 32, :]).then_inc(S("back_in"), 16)
        act.dma_start(sgb[:].rearrange("p a t -> p (a t)")[:, 0:T], sg_d[:, 0:T]).then_inc(S("back_in"), 16)
        act.dma_start(sgb[0:32, 1, :], sg_d[0:32, T:2 * T]).then_inc(S("back_in"), 16)
        act.dma_start(bvb[:], bv_d).then_inc(S("bv_in"), 16)
        act.wait_ge(S("gate_out0"), 16 * 9)
        act.wait_ge(S("gate_out1"), 16 * 9)
        act.dma_start(b0b[:], b0_d).then_inc(S("gates_in"), 16)
        act.dma_start(t0b[:], t0_d).then_inc(S("gates_in"), 16)
        act.dma_start(t1b[:], t1_d).then_inc(S("gates_in"), 16)
        split_hi(SP_Y, r1h)
        with act.Fori(0, 4) as i:
            for h in range(2):
                after(N_B1, i, h, 2)
                act.wait_ge(S("x_f"), 2 * i + (SP_M + h + 1))
                A(r2h[:, 2 * i + h, :], hx[:, h, :], ACT.Copy).then_inc(S("x_hi"), 1)
        act.wait_ge(S("x_f"), SP_Y + 8)
        act.dma_start(xr[:], xT).then_inc(S("x_in"), 16)
        with act.Fori(0, 4) as i:
            for h in range(2):
                after(N_OUT, i, h, 2)
                A(mix[:, 2 * i + h, :], B[h][:], ACT.Copy, scale=0.5).then_inc(S("tile_ev"), 1)
        act.wait_ge(S("tile_ev"), E_UP)
        rms_sq(N2, mix, None)
        rms_root(N2)
        rms_sq(N3, xr, "x1_f")
        act.dma_start(x1_d, flat(xr)).then_inc(S("spilled"), 16)
        rms_root(N3)
        split_hi(SP_F, r1h)
        act.wait_ge(S("spilled"), 80)
        with act.Fori(0, 16) as i:
            for h in range(2):
                j = 2 * i + h
                after(N_UP, i, h, 2)
                act.wait_ge(S(f"f_lo{h}"), i + 1)
                A(sqt[:, h, :], B[h][:], ACT.Relu).then_inc(S(f"f_relu{h}"), 1)
                act.wait_ge(S("tile_ev"), 2 * i + (E_UP + h + 1))
                A(fh[:, j, :], hx[:, h, :], ACT.Copy).then_inc(S(f"f_hi{h}"), 1)
        act.wait_ge(S("slab_mm"), N_DOWN)
        act.dma_start(flat(x1), x1_d).then_inc(S("x_in"), 16)
        with act.Fori(0, 3) as i:
            for h in range(2):
                for b in range(KB):
                    after(N_DOWN, i, 4 * h + b, 8)
                A(ob[:, 2 * i + h, :], B[2 + h][:], ACT.Copy).then_inc(S("tile_ev"), 1)
        for h in range(2):
            for b in range(KB):
                if 4 * h + b < 6:
                    after(N_DOWN + 24, 0, 4 * h + b, 8)
            act.wait_ge(S("slab_mm"), N_DOWN + 24 + 4 * h + 4)
            A(ob[:, 6 + h, :], B[2 + h][:], ACT.Copy).then_inc(S("tile_ev"), 1)
        act.wait_ge(S("tile_ev"), E_ALL)
        rms_sq(N4, ob, None)
        rms_root(N4)

    @block.vector
    def _(dve):
        TT = nc.vector.tensor_tensor
        TS = nc.vector.tensor_scalar
        STT = nc.vector.scalar_tensor_tensor
        A_, M_, SUB = ALU.add, ALU.mult, ALU.subtract

        for n_ in ("k_sh", "ld", "cum", "cx", "aa", "kp", "r_sh", "wc", "p", "ssm", "inv", "ax", "be", "at", "bt", "v_sh", "bv", "y_read0", "y_read1", "f_lo0", "f_lo1"):
            dve.sem_inc(S(n_), 1)

        def rms_rec(norm, bank):
            dve.wait_ge(S("rms_mm"), norm + KC)
            TS(rst[:, 0, :], bank[:], 1.0 / D, EPS, M_, A_).then_inc(S("rms_ms"), 1)
            dve.wait_ge(S("rms_ms"), norm // 8 + 1)
            nc.vector.reciprocal(rst[:, 0, :], rst[:, 0, :]).then_inc(S("rms_rec"), 1)
            dve.wait_ge(S("rms_root"), norm // 8 + 1)

        def norm_split(src, gain, sp_, hi, lo):
            for kc in range(KC + 1):
                if kc < KC:
                    if kc >= 2:
                        dve.wait_ge(S("x_lo"), sp_ + kc - 1)
                    STT(hx[:, kc % 2, :], src[:, kc, :], col(gain, kc), rst[:, 1, :], M_, M_).then_inc(S("x_f"), 1)
                if kc >= 1:
                    remainder(kc - 1, sp_, hi, lo)

        def remainder(kc, sp_, hi, lo):
            dve.wait_ge(S("x_f"), sp_ + kc + 1)
            dve.wait_ge(S("x_hi"), sp_ + kc + 1)
            TT(lo[:, kc, :], hx[:, kc % 2, :], hi[:, kc, :].bitcast(F32), SUB).then_inc(S("x_lo"), 1)

        dve.wait_ge(S("par_in"), 16)
        for n_, (o, s_, w_, a, b) in enumerate((
                (OM_R, COL["mu_r"], 24, -1.0, 1.0), (OM_L, MU_L, 3, -1.0, 1.0), (H_W0, COL["w0"], 16, 0.5, 0.0),
                (H_KA, COL["k_a"], 8, 0.5, 0.0), (OH_KA, COL["k_a"], 8, -0.5, 1.0),
                (N_KK, COL["k_k"], 8, -1.0, 0.0), (H_GB0, COL["gb0"], 16, 0.5, 0.0))):
            TS(par[:, o:o + w_], par[:, s_:s_ + w_], a, b, M_, A_).then_inc(S("par_done"), 1)
        dve.wait_ge(S("par_done"), 7)

        nc.vector.memset(kb[:].rearrange("p a b c d e -> p (a b c d e)"), 0.0).then_inc(S("kb_zero"), 1)
        nc.vector.memset(v2[:], 0.0).then_inc(S("kb_zero"), 1)
        rms_rec(N1, B[7])
        norm_split(xs, "pre_mix", SP_H, r1h, r1l)
        dve.wait_ge(S("small_mm"), 1)
        nc.vector.tensor_copy(beta[0:16, :], B[6][0:16, 0:BETA]).then_inc(S("beta_ev"), 1)

        for n in range(3):
            M = 32 if n == 2 else P
            dst = (tl[:], sg[:, 0, :], sg[:, 1, :])[n][0:M]
            dve.wait_ge(S("lo_sc"), n + 1)
            STT(dst[:, 1:T], B[n % 2][0:M, 0:T - 1], par[0:M, MU_L + n:MU_L + n + 1], dst[:, 1:T], M_, A_) \
                .then_inc(S("lo_sh"), 1)
        for n in (1, 2):
            M = 32 if n == 2 else P
            dve.wait_ge(S("lo_th"), n + 1)
            TS(sg[0:M, n - 1, :], sg[0:M, n - 1, :], 0.5, 0.5, M_, A_)
        dve.wait_ge(S("small_mm"), 2)
        dve.wait_ge(S("kb_zero"), 2)
        nc.vector.tensor_copy(v1[:], v4(B[2])).then_inc(S("v_ready"), 1)
        nc.vector.tensor_copy(v2[0:64], v4(B[2])[0:64]).then_inc(S("v_ready"), 1)
        nc.vector.tensor_copy(v2[64:128, 1:4, :], v4(B[2])[64:128, 0:3, :]).then_inc(S("v_ready"), 1)

        dve.wait_ge(S("bias_in"), 16 * 8)
        dve.wait_ge(S("tab_in"), 48)

        def logits(c):
            dve.wait_ge(S("at_sc"), c + 1)
            if c >= 2:
                dve.wait_ge(S("at_tr"), c - 1)
            L = lg[:, c % 2].rearrange("p (k g) n -> p k g n", k=2)
            bs = bias[:, :, 0:128] if c % 2 else bias[:, :, 64:192]
            bs = bs.rearrange("p (k g) n -> p k g n", k=2)
            for k in range(2):
                ps = v4(B[2 + 2 * (c % 2) + k])
                if c == 0:
                    STT(L[:, k, :, 0:64], ps[:, :, 0:64], HD ** -0.5, bs[:, k, :, 0:64], M_, A_) \
                        .then_inc(S("at_lg"), 1)
                    nc.vector.memset(L[:, k, :, 64:128], -1e30).then_inc(S("at_no"), 1)
                else:
                    STT(L[:, k], ps, HD ** -0.5, bs[:, k], M_, A_).then_inc(S("at_lg"), 1)
            if c == 0:
                dve.wait_ge(S("at_no"), 2)
            dve.wait_ge(S("at_lg"), 2 * c + 2)
            a = asm[:, c % 2]
            L = lg[:, c % 2]
            nc.vector.tensor_reduce(a[:, 0, :], L, AX, ALU.max).then_inc(S("at_soft"), 1)
            dve.wait_ge(S("at_soft"), 6 * c + 1)
            TT(a[:, 0, :], a[:, 0, :], sinkT[:], ALU.max).then_inc(S("at_soft"), 1)
            dve.wait_ge(S("at_soft"), 6 * c + 2)
            TT(a[:, 1, :], sinkT[:], a[:, 0, :], SUB).then_inc(S("at_soft"), 1)
            dve.wait_ge(S("at_soft"), 6 * c + 3)
            TT(L, L, a[:, 0, :].unsqueeze(2).to_broadcast([P, 8, P]), SUB).then_inc(S("at_sub"), 1)

        def normalise(c):
            a = asm[:, c % 2]
            L = lg[:, c % 2]
            dve.wait_ge(S("at_exp"), c + 1)
            nc.vector.tensor_reduce(a[:, 2, :], L, AX, A_).then_inc(S("at_soft"), 1)
            dve.wait_ge(S("at_soft"), 6 * c + 4)
            dve.wait_ge(S("at_exs"), c + 1)
            TT(a[:, 3, :], a[:, 2, :], a[:, 1, :], A_).then_inc(S("at_soft"), 1)
            dve.wait_ge(S("at_soft"), 6 * c + 5)
            nc.vector.reciprocal(a[:, 4, :], a[:, 3, :]).then_inc(S("at_soft"), 1)
            dve.wait_ge(S("at_soft"), 6 * c + 6)
            TT(L, L, a[:, 4, :].unsqueeze(2).to_broadcast([P, 8, P]), M_).then_inc(S("at_p"), 1)

        def attn_lo(c):
            dve.wait_ge(S("at_hi"), c + 1)
            cs = slice(CH * c, CH * c + CH)
            TT(r2l[:, :, cs], B[0][:].rearrange("p (m t) -> p m t", m=KC), r2h[:, :, cs].bitcast(F32), SUB) \
                .then_inc(S("at_lo"), 1)

        logits(0)
        for c in range(NCH):
            normalise(c)
            if c + 1 < NCH:
                logits(c + 1)
            attn_lo(c)

        with dve.Fori(0, 4) as i:
            for h in range(2):
                dve.wait_ge(S("slab_mm"), 2 * i + (N_B0 + h + 1))
                nc.vector.tensor_copy(b0[:, 2 * i + h, :], B[h][:]).then_inc(S("tile_ev"), 1)
        nc.vector.memset(wl[:].rearrange("p a b c -> p (a b c)"), 0.0).then_inc(S("wl_zero"), 1)

        dve.wait_ge(S("masks"), 1 + 2 + 3 + 3 + 3 + 3 + 4 * len(LEVELS))
        dve.wait_ge(S("spilled"), 48)
        with dve.Fori(0, 4) as i:
            for h in range(2):
                m = 2 * i + h
                t = {k_: v_[:] for k_, v_ in tmp.items()}

                def need(*names):
                    for n_ in names:
                        dve.wait_ge(S(n_), m + 2)

                def read(*names):
                    for n_ in names:
                        dve.wait_ge(S(n_), m + 1)

                need("k_sc")
                STT(t["kS"][:, 1:T], B[0][:, 0:T - 1], col("mu_k", m), t["kS"][:, 1:T], M_, A_) \
                    .then_inc(S("k_sh"), 1)
                need("tw")
                TS(t["ld"], t["tw"], -C_DEC, -C_DEC, M_, A_).then_inc(S("ld"), 1)
                need("ld")
                read("eWi")
                nc.vector.tensor_tensor_scan(t["cum"], scanm[:], t["ld"], 0.0, M_, A_).then_inc(S("cum"), 1)
                need("cum")
                read("eWx")
                TT(t["cx"], t["cum"], t["ld"], SUB).then_inc(S("cx"), 1)
                need("ta")
                TS(t["t"], t["ta"], pcol(H_KA, m), pcol(OH_KA, m), M_, A_)
                TS(t["aa"], t["ta"], 0.5, 0.5, M_, A_).then_inc(S("aa"), 1)
                need("aa", "k_sh")
                TT(t["kp"], t["kS"], t["t"], M_).then_inc(S("kp"), 1)
                STT(t["b0"], t["kS"], col("k_k", m), t["aa"], M_, M_)
                need("kp", "eWi")
                TT(kt[:, m, :], t["kp"], t["eWi"], M_)
                need("r_sc")
                STT(t["rS"][:, 1:T], B[3][:, 0:T - 1], col("mu_r", m), t["rS"][:, 1:T], M_, A_) \
                    .then_inc(S("r_sh"), 1)
                need("r_sh", "eW")
                TT(ar[:, 1, m, :], t["rS"], t["eW"], M_)
                nc.vector.tensor_copy(wc[:, m, :], t["eW"][:, CH - 1:T:CH]).then_inc(S("wc"), 1)
                read("bon_mm")
                STT(t["p"], t["rS"], col("r_k", m), t["kp"], M_, M_).then_inc(S("p"), 1)
                need("ss_mm")
                read("nrm")
                TS(t["ssm"], B[4][:], 1e-24, None, ALU.max).then_inc(S("ssm"), 1)
                need("nrm")
                nc.vector.reciprocal(t["inv"], t["nrm"]).then_inc(S("inv"), 1)
                need("inv")
                STT(t["ssm"], t["kS"], pcol(N_KK, m), t["inv"], M_, M_).then_inc(S("ax"), 1)
                TT(t["b0"], t["b0"], t["inv"], M_).then_inc(S("be"), 1)
                need("ax", "eWx")
                TT(ar[:, 0, m, :], t["ssm"], t["eWx"], M_).then_inc(S("at"), 1)
                need("be")
                TT(bt[:, m, :], t["b0"], t["eWi"], M_).then_inc(S("bt"), 1)
                need("v_sc")
                STT(vb[:, m, 1:T], B[5][:, 0:T - 1], col("mu_v", m), vb[:, m, 1:T], M_, A_) \
                    .then_inc(S("v_sh"), 1)
                need("v_sh", "bon_mm")
                TT(bv[:, m, :], B[6][:], vb[:, m, :], M_).then_inc(S("bv"), 1)

        dve.wait_ge(S("spilled"), 64)
        for h in range(2):
            nc.vector.memset(U2["St"][h][:], 0.0).then_inc(S("st_zero"), 1)
        dve.wait_ge(S("st_zero"), 2)
        for h in range(2):
            dve.sem_inc(S(f"st{h}"), 1)
        with dve.Fori(0, NCH) as c:
            def m2(t_):
                return t_[:].rearrange("p m (e t) -> p m e t", e=2)

            for h in range(2):
                b = B[3 * h:3 * h + 3]
                dve.wait_ge(S(f"sc_mm{h}"), c * 2 + 1)
                TT(m2(U2["aab"][h]), bc2(v4(b[0])[:, :, 0:64]), mask4(m_strict), M_).then_inc(S(f"sc_ev{h}"), 1)
                TT(m2(U2["arb"][h]), bc2(v4(b[0])[:, :, 64:128]), mask4(m_incl), M_).then_inc(S(f"sc_ev{h}"), 1)
                dve.wait_ge(S(f"sc_mm{h}"), c * 2 + 2)
                TT(m2(U2["aak"][h]), bc2(v4(b[1])[:, :, 0:64]), mask4(m_strict), M_).then_inc(S(f"sc_ev{h}"), 1)
                TT(m2(U2["ark"][h]), bc2(v4(b[1])[:, :, 64:128]), mask4(m_incl), M_).then_inc(S(f"sc_ev{h}"), 1)
                dve.wait_ge(S(f"sc_ev{h}"), c * 5 + 1)
                TT(U2["AI"][h][:], U2["aab"][h][:], mask4f(ident), A_).then_inc(S(f"sc_ev{h}"), 1)
            for h in range(2):
                b = B[3 * h:3 * h + 3]
                dve.wait_ge(S(f"sc_ev{h}"), c * 5 + 5)
                TT(U2["XT"][h][:], U2["AI"][h][:], mask4f(m_1t), M_).then_inc(S(f"xt_ready{h}"), 1)
                dve.wait_ge(S(f"ai_mm{h}"), c + 1)
                TT(U2["X"][h][:], v4(b[2]), mask4f(m_1), M_).then_inc(S(f"x_ready{h}"), 1)
            for k in range(len(LEVELS)):
                for h in range(2):
                    dve.wait_ge(S(f"q_mm{h}"), c * 5 + (k + 1))
                    TT(U2["Qs"][h][:], v4(B[3 * h + 2]), mask4f(m_lev[k]), M_).then_inc(S(f"q_ev{h}"), 1)
                for h in range(2):
                    dve.wait_ge(S(f"d_mm{h}"), c * 5 + (k + 1))
                    if k < len(LEVELS) - 1:
                        TT(U2["X"][h][:], v4(B[3 * h + 1]), U2["X"][h][:], A_).then_inc(S(f"x_ready{h}"), 1)
                    else:
                        TT(U2["XT"][h][:], v4(B[3 * h + 1]), U2["XT"][h][:], A_).then_inc(S(f"xt_last{h}"), 1)

            def r4(t_):
                return t_.unsqueeze(2).to_broadcast([P, 4, CH])

            for h in range(2):
                ps = B[3 * h + 1][:, 0:256].rearrange("p (m i) -> p m i", m=4)
                dve.wait_ge(S(f"y_mm{h}"), c + 1)
                nc.vector.tensor_reduce(gn[:, h, 0, :], ps, AX, A_).then_inc(S(f"gn{h}"), 1)
                dve.wait_ge(S(f"gn{h}"), c * 5 + 1)
                TS(gn[:, h, 1, :], gn[:, h, 0, :], 1.0 / HD, None, M_).then_inc(S(f"gn{h}"), 1)
                dve.wait_ge(S(f"gn{h}"), c * 5 + 2)
                TT(U2["Y"][h][:], ps, r4(gn[:, h, 1, :]), SUB).then_inc(S(f"yc{h}"), 1)
                ds = B[3 * h][:, 0:256].rearrange("p (m i) -> p m i", m=4)
                dve.wait_ge(S(f"dS_mm{h}"), c + 2)
                TT(U2["St"][h][:], ds, U2["St"][h][:], A_).then_inc(S(f"gn{h}"), 1)
                dve.wait_ge(S(f"gn{h}"), c * 5 + 3)
                TT(U2["St"][h][:], U2["St"][h][:],
                   wc[:, 4 * h:4 * h + 4, bass.ds(c, 1)].to_broadcast([P, 4, CH]), M_).then_inc(S(f"st{h}"), 1)
            for h in range(2):
                dve.wait_ge(S(f"ysq{h}"), c + 1)
                nc.vector.tensor_reduce(gn[:, h, 0, :], U2["Yt"][h][:], AX, A_).then_inc(S(f"gn{h}"), 1)
                dve.wait_ge(S(f"gn{h}"), c * 5 + 4)
                TS(gn[:, h, 1, :], gn[:, h, 0, :], 1.0 / HD, GN_EPS, M_, A_).then_inc(S(f"gn{h}"), 1)
                dve.wait_ge(S(f"gn{h}"), c * 5 + 5)
                nc.vector.reciprocal(gn[:, h, 2, :], gn[:, h, 1, :]).then_inc(S(f"yv{h}"), 1)
            for h in range(2):
                dve.wait_ge(S(f"yr{h}"), c + 1)
                TT(U2["Y"][h][:], U2["Y"][h][:], r4(gn[:, h, 3, :]), M_).then_inc(S(f"yn{h}"), 1)
            for h in range(2):
                tk = bass.ds(c * CH, CH)
                dve.wait_ge(S(f"yt_mm{h}"), c + 1)
                TT(vb[:, 4 * h:4 * h + 4, tk], B[3 * h + 2][:, 0:256].rearrange("p (m i) -> p m i", m=4),
                   r4(par[:, COL["ln_w"] + 4 * h:COL["ln_w"] + 4 * h + 4]), M_).then_inc(S(f"y_read{h}"), 1)

        dve.wait_ge(S("y_read0"), 9)
        dve.wait_ge(S("y_read1"), 9)
        dve.wait_ge(S("bv_in"), 16)
        for m in range(KC):
            TT(vb[:, m, :], vb[:, m, :], bvb[:, m, :], A_).then_inc(S("y_sum"), 1)
        for m in range(KC + 1):
            if m < KC:
                dve.wait_ge(S("y_sum"), m + 1)
                dve.wait_ge(S("g_mm"), m + 1)
                if m >= 2:
                    dve.wait_ge(S("x_lo"), SP_Y + m - 1)
                STT(hx[:, m % 2, :], vb[:, m, :], col("ln_b", m), B[m % 2][:], A_, M_).then_inc(S("x_f"), 1)
            if m >= 1:
                remainder(m - 1, SP_Y, r1h, r1l)
        dve.wait_ge(S("gates_in"), 48)
        for m in range(KC):
            STT(t0b[:, m, :], t0b[:, m, :], 1.0, b0b[:, m, :], A_, M_).then_inc(S("m0"), 1)
        for m in range(KC):
            dve.wait_ge(S("slab_mm"), N_B1 + m + 1)
            STT(t1b[:, m, :], t1b[:, m, :], 1.0, B[m % 2][:], A_, M_).then_inc(S("tile_ev"), 1)
            dve.wait_ge(S("tile_ev"), E_B1 + m + 1)
            if m >= 2:
                dve.wait_ge(S("x_lo"), SP_M + m - 1)
            TT(hx[:, m % 2, :], t1b[:, m, :], t0b[:, m, :], A_).then_inc(S("x_f"), 1)
            remainder(m, SP_M, r2h, r2l)

        rms_rec(N2, B[7])
        dve.wait_ge(S("x_in"), 32)
        for kc in range(KC):
            STT(mix[:, kc, :], mix[:, kc, :], col("post_mix", kc), rst[:, 1, :], M_, M_).then_inc(S("scaled"), 1)
            dve.wait_ge(S("scaled"), kc + 1)
            TT(xr[:, kc, :], xr[:, kc, :], mix[:, kc, :], A_).then_inc(S("x1_f"), 1)
        dve.wait_ge(S("x1_f"), 8)
        rms_rec(N3, B[6])
        norm_split(xr, "pre_ffn", SP_F, r1h, r1l)
        dve.wait_ge(S("spilled"), 80)
        with dve.Fori(0, 16) as i:
            for h in range(2):
                j = 2 * i + h
                dve.wait_ge(S(f"f_relu{h}"), i + 1)
                STT(hx[:, h, :], B[h][:], 0.0, sqt[:, h, :], ALU.max, M_).then_inc(S("tile_ev"), 1)
                dve.wait_ge(S("tile_ev"), 2 * i + (E_UP + h + 1))
                dve.wait_ge(S(f"f_hi{h}"), i + 1)
                TT(fl[:, j, :], hx[:, h, :], fh[:, j, :].bitcast(F32), SUB).then_inc(S(f"f_lo{h}"), 1)
                dve.wait_ge(S(f"f_lo{h}"), i + 2)
                dve.sem_inc(S("f_lo"), 1)
        rms_rec(N4, B[7])
        dve.wait_ge(S("x_in"), 48)
        for kc in range(KC):
            STT(ob[:, kc, :], ob[:, kc, :], col("post_ffn", kc), rst[:, 1, :], M_, M_).then_inc(S("scaled"), 1)
            dve.wait_ge(S("scaled"), KC + kc + 1)
            TT(ob[:, kc, :], ob[:, kc, :], x1[:, kc, :], A_).then_inc(S("o_ready"), 1)

    block.__exit__(None, None, None)


def relative_buckets():
    rel = np.arange(-(CH * 2 - 1), CH)
    nb, max_exact = 16, 8
    ret = (rel > 0).astype(np.int32) * nb
    n = np.abs(rel)
    ratio = np.maximum(n, 1).astype(np.float32) / np.float32(max_exact)
    large = max_exact + (np.log(ratio) / np.float32(np.log(128 / max_exact)) * (nb - max_exact)).astype(np.int32)
    return ret + np.where(n < max_exact, n, np.minimum(large, nb - 1))


def kernel(x, w_in, rwkv_shift, pre_mix_g, post_mix_g, pre_ffn_g, post_ffn_g, attn_sinks, rel_bias, w0,
           w_decay_up, a0, w_aaa_up, w_gate_up, k_k, k_a, r_k, ln_x_w, ln_x_b, gate_bias, w_branch, w_out,
           w_ff_up, w_ff_down):
    import concourse.bacc as bacc
    from concourse.bass_utils import run_bass_kernel_spmd

    def tab(v):
        return np.asarray(v).reshape(KC, P).T

    mu = np.asarray(rwkv_shift)[0]
    lmu = np.zeros((3 * P,), np.float32)
    lmu[:288] = mu[3 * D:]
    gb = np.asarray(gate_bias)[0]
    cols = np.concatenate([tab(v) for v in (
        pre_mix_g[0], post_mix_g[0], pre_ffn_g[0], post_ffn_g[0], mu[0:D], mu[D:2 * D], mu[2 * D:3 * D],
        w0[0], a0[0], k_k[0], k_a[0], r_k[0], ln_x_w[0], ln_x_b[0], gb[0], gb[1])] + [lmu.reshape(3, P).T], axis=1)
    head = np.arange(8)
    hmap = np.stack([4 * (head // 2) + 2 * e + head % 2 for e in range(2)])
    sinks = np.repeat(np.asarray(attn_sinks)[0][hmap], CH, axis=0)
    onehot = np.zeros((32, BETA), np.float32)
    onehot[relative_buckets(), np.arange(BETA - 1)] = 1.0
    arrays = {
        "xT": np.asarray(x)[0].T.reshape(KC, P, T).transpose(1, 0, 2),
        "w_in": w_in[0], "cols": cols, "sinks": sinks, "onehot": onehot, "rel_bias": rel_bias,
        "wdec": w_decay_up[0], "waaa": w_aaa_up[0], "wgate": w_gate_up[0], "w_br": w_branch[0],
        "w_out": w_out[0], "w_up": w_ff_up[0], "w_down": w_ff_down[0],
    }
    arrays = {k: np.ascontiguousarray(v) for k, v in arrays.items()}
    nc = bacc.Bacc("TRN2", target_bir_lowering=False, num_devices=1)
    args = [nc.dram_tensor(k, list(v.shape), F32, kind="ExternalInput").ap() for k, v in arrays.items()]
    out = nc.dram_tensor("out", [P, KC, T], F32, kind="ExternalOutput").ap()
    build(nc, *args, out)
    r = run_bass_kernel_spmd(nc, [arrays], core_ids=[0])
    y = r.results[0]["out"]
    return y.transpose(1, 0, 2).reshape(D, T).T[None]
```

```python
import math

import concourse.bass as bass
import numpy as np
from concourse import mybir
from concourse.alu_op_type import AluOpType as ALU

F32 = mybir.dt.float32
F32R = mybir.dt.float32r
ACT = mybir.ActivationFunctionType
AX = mybir.AxisListType.X

P = 128
T = 512
D = 1024
KC = D // P
CH = 64
NCH = T // CH
HD = 64
DFF = 4 * D
KB = DFF // D
EPS = 1e-6
GN_EPS = 64e-5
BETA = 192
C_DEC = 0.5 * math.exp(-0.5)

Q0, K0, V0 = 0, D, D + P
R0, RK0, RV0 = D + 2 * P, 2 * D + 2 * P, 3 * D + 2 * P
L0 = 4 * D + 2 * P
G0 = L0 + 64 + 64 + 160

NAMES = ["pre_mix", "post_mix", "pre_ffn", "post_ffn", "mu_r", "mu_k", "mu_v", "w0", "a0",
         "k_k", "k_a", "r_k", "ln_w", "ln_b", "gb0", "gb1"]
COL = {n: 8 * i for i, n in enumerate(NAMES)}
MU_L = 8 * len(NAMES)
NCOL = MU_L + 3
OM_R, OM_K, OM_V, OM_L = NCOL, NCOL + 8, NCOL + 16, NCOL + 24
H_W0, H_A0, H_KA, OH_KA, N_KK, H_GB0, H_GB1 = (NCOL + 27 + 8 * i for i in range(7))
NCOLS = NCOL + 27 + 56

N_G0 = 13
N_B0 = 21
N_PAIR = 29
N_GATE = 53
N_B1 = 69
N_OUT = 77
N_UP = 85
N_DOWN = 117
POOL_OUT = 3
LEVELS = [2, 4, 8, 16, 32]
E_G0, E_B0, E_GATE, E_B1, E_OUT, E_UP, E_DOWN, E_ALL = 10, 18, 26, 34, 42, 50, 82, 90
N1, N2, N3, N4 = 0, 8, 16, 24
SP_H, SP_Y, SP_M, SP_F = 0, 8, 16, 24


def build(nc, xT, w_in, cols, sinks, onehot, rel_bias, wdec, waaa, wgate, w_br, w_out, w_up, w_down, out):
    sems = {}

    def S(name):
        if name not in sems:
            sems[name] = nc.alloc_semaphore(name)
        return sems[name]

    base = (nc.sbuf_base + 63) // 64 * 64

    def at(name, shape, kib, dt=F32):
        kib = kib if kib < 10 else kib - 0.5
        return nc.alloc_sbuf_tensor_at(name, [P] + shape, dt, offset=base + int(kib * 1024))

    ident = at("ident", [P], 0)
    ones = at("ones", [P], 0.5)
    bdones = at("bdones", [P], 1)
    m_strict = at("m_strict", [P], 1.5)
    m_incl = at("m_incl", [P], 2)
    m_1 = at("m_1", [P], 2.5)
    m_1t = at("m_1t", [P], 3)
    m_lev = [at(f"m_lev{b}", [P], 3.5 + 0.5 * i) for i, b in enumerate(LEVELS)]
    scanm = at("scanm", [T], 6)
    par = at("par", [NCOLS], 8)
    sinkT = at("sinkT", [8], 9)
    wc = at("wc", [KC, NCH], 9.25)
    raw = at("raw", [2, KC, P], 10)
    whi = at("whi", [2, KC, P], 18, F32R)
    wlo = at("wlo", [2, KC, P], 26, F32R)
    r1h, r1l = at("r1h", [KC, T], 34, F32R), at("r1l", [KC, T], 50, F32R)
    r2h, r2l = at("r2h", [KC, T], 66, F32R), at("r2l", [KC, T], 82, F32R)
    xs = at("xs", [KC, T], 98)
    q = at("q", [4, NCH, 2, CH], 98)
    kb = at("kb", [2, 2, 2, 4, P], 114)
    v1 = at("v1", [4, P], 130)
    v2 = at("v2", [4, P], 132)
    bias = at("bias", [8, 192], 134)
    lg = at("lg", [2, 8, P], 146)
    pT = at("pT", [2, 8, P], 154)
    kT = at("kT", [T], 162)
    vT = at("vT", [T], 164)
    t0 = at("t0", [KC, T], 166)
    beta = at("beta", [BETA], 182)
    oneh = at("oneh", [BETA], 183)
    relb = at("relb", [16], 184)
    asm = at("asm", [2, 5, 8], 185)
    sqt = at("sqt", [2, T], 194)
    hx = at("hx", [2, T], 198)
    rst = at("rst", [2, T], 202)
    tl = at("tl", [T], 202)
    sg = at("sg", [2, T], 204)
    ar = at("ar", [2, KC, T], 66)
    bt = at("bt", [KC, T], 98)
    kt = at("kt", [KC, T], 114)
    vb = at("vb", [KC, T], 130)
    bv = at("bv", [KC, T], 146)
    wl = at("wl", [2, 2, P], 162)
    tmp = {n: at("t_" + n, [T], 164 + 2 * i) for i, n in enumerate(
        ["kS", "rS", "tw", "ld", "cum", "cx", "ta", "t", "kp", "aa", "eW", "eWi", "eWx", "b0",
         "sq", "ssm", "nrm", "inv", "p"])}
    U2 = {}
    for i, n in enumerate(["aab", "aak", "arb", "ark", "X", "XT", "Qs", "BDa", "BDr", "BDb", "BDk", "VD"]):
        U2[n] = [at(f"u_{n}{h}", [4, P], 146 + 2 * (2 * i + h)) for h in range(2)]
    U2["AI"] = U2["Qs"]
    U2["btok"], U2["ktok"] = U2["BDb"], U2["BDk"]
    for i, n in enumerate(["Vc", "Y", "Yt", "St"]):
        U2[n] = [at(f"u_{n}{h}", [4, HD], 194 + 2 * i + h) for h in range(2)]
    for i, n in enumerate(["G", "U"]):
        U2[n] = [at(f"u_{n}{h}", [4, HD], 190 + 2 * h + i) for h in range(2)]
    gs = at("gs", [T], 202)
    gn = at("gn", [2, 4, 4], 206)
    wg = at("wg", [2, D], 98)
    bvb = at("bvb", [KC, T], 106)
    sgb = at("sgb", [2, T], 122)
    m0b, t1b = at("m0b", [KC, T], 146), at("t1b", [KC, T], 162)
    mix = at("mix", [KC, T], 98)
    xr = at("xr", [KC, T], 114)
    fh = at("fh", [KB * KC, T], 66, F32R)
    fl = at("fl", [KB * KC, T], 130, F32R)
    ob = at("ob", [KC, T], 34)
    x1 = at("x1", [KC, T], 50)

    m0_d, bv_d, t1_d = (nc.dram_tensor(n, [P, KC, T], F32, kind="Internal").ap()
                        for n in ("m0_d", "bv_d", "t1_d"))
    sg_d = nc.dram_tensor("sg_d", [P, 2 * T], F32, kind="Internal").ap()
    x1_d = nc.dram_tensor("x1_d", [P, KC * T], F32, kind="Internal").ap()
    beta_t = nc.dram_tensor("beta_d", [16, CH, BETA], F32, kind="Internal")
    beta_d = beta_t.ap()

    B = [nc.alloc_psum_tensor(f"bank{i}", [P, T], F32) for i in range(8)]

    def slabs(w):
        return w.rearrange("(kc p) n -> p kc n", p=P)

    win_s, wout_s, wup_s = slabs(w_in), slabs(w_out), slabs(w_up)
    wbr_s = [slabs(w_br[0]), slabs(w_br[1])]
    wdn_s = [slabs(w_down[D * b:D * (b + 1), :]) for b in range(KB)]

    def col(name, m):
        c = COL[name] if name in COL else name
        return par[:, c + m:c + m + 1] if isinstance(m, int) else par[:, bass.ds(c + m, 1)]

    def pcol(c0, m):
        return par[:, c0 + m:c0 + m + 1] if isinstance(m, int) else par[:, bass.ds(c0 + m, 1)]

    def flat(t):
        return t[:].rearrange("p a b -> p (a b)")

    def bc2(ap):
        return ap.unsqueeze(2).to_broadcast([P, 4, 2, CH])

    def mask4(t):
        return t[:].rearrange("p (e t) -> p e t", e=2).unsqueeze(1).to_broadcast([P, 4, 2, CH])

    def mask4f(t):
        return t[:].unsqueeze(1).to_broadcast([P, 4, P])

    def v4(bank):
        return bank[:].rearrange("p (m n) -> p m n", m=4)

    block = nc.Block()
    block.__enter__()

    @block.sync
    def _(sp):
        def slab(n, slot, src, rows=KC):
            if not isinstance(n, int) or n >= 2:
                sp.wait_ge(S("w_split"), n - 1)
            sp.dma_start(raw[:, slot, 0:rows, :], src).then_inc(S(f"w_raw{slot}"), 16)

        sp.dma_start(xs[:, 0:4, :], xT[:, 0:4, :]).then_inc(S("x_in"), 16)
        sp.dma_start(xs[:, 4:8, :], xT[:, 4:8, :]).then_inc(S("x_in_late"), 16)
        sp.dma_start(par[:, 0:NCOL], cols).then_inc(S("par_in"), 16)
        for n in range(13):
            c0 = ([L0, L0 + P, L0 + 2 * P, K0, V0] + [Q0 + P * j for j in range(8)])[n]
            slab(n, n % 2, win_s[:, :, c0:c0 + P])
            if n == 1:
                sp.dma_start(sinkT[:], sinks).then_inc(S("tab_in"), 16)
                sp.dma_start(oneh[0:32, :], onehot).then_inc(S("tab_in"), 16)
                sp.dma_start(relb[0:32, :], rel_bias).then_inc(S("tab_in"), 16)

        def tiles(n0, src, c0, i0=0):
            with sp.Fori(i0, 4) as i:
                for h in range(2):
                    slab(2 * i + (n0 + h), (n0 + h) % 2, src[:, :, bass.ds(i * (2 * P) + (c0 + P * h), P)])

        tiles(N_G0, win_s, G0)
        tiles(N_B0, wbr_s[0], 0)
        with sp.Fori(0, 4) as i:
            for h in range(2):
                slab(6 * i + (N_PAIR + 3 * h), (N_PAIR + 3 * h) % 2,
                     win_s[:, :, bass.ds(i * (2 * P) + (RK0 + P * h), P)])
                sp.wait_ge(S("a_mm"), 2 * i + (h + 1))
                sp.sem_inc(S("wl_free"), 1)
                sp.wait_ge(S("wl_zero"), 1)
                sp.dma_start(wl[0:64, h, 0, :], wdec[:, bass.ds(i * (2 * P) + P * h, P)]).then_inc(S(f"wl{h}"), 16)
                sp.dma_start(wl[64:128, h, 1, :], waaa[:, bass.ds(i * (2 * P) + P * h, P)]).then_inc(S(f"wl{h}"), 16)
                for j, c0 in ((1, R0), (2, RV0)):
                    slab(6 * i + (N_PAIR + 3 * h + j), (N_PAIR + 3 * h + j) % 2,
                         win_s[:, :, bass.ds(i * (2 * P) + (c0 + P * h), P)])
        with sp.Fori(0, NCH) as c:
            for h in range(2):
                slab(2 * c + (N_GATE + h), (N_GATE + h) % 2,
                     win_s[:, 4 * h:4 * h + 4, bass.ds(c * P + (G0 + D), P)], rows=KC // 2)
        for h in range(2):
            slab(N_B1 + h, (N_B1 + h) % 2, wbr_s[1][:, :, P * h:P * h + P])
        for h in range(2):
            sp.wait_ge(S(f"bd{h}"), 5 * NCH)
        sp.dma_start(wg[:, 0, :], wgate[0:P, :]).then_inc(S("back_in"), 16)
        sp.dma_start(wg[0:32, 1, :], wgate[P:P + 32, :]).then_inc(S("back_in"), 16)
        sp.dma_start(sgb[:].rearrange("p a t -> p (a t)")[:, 0:T], sg_d[:, 0:T]).then_inc(S("back_in"), 16)
        sp.dma_start(sgb[0:32, 1, :], sg_d[0:32, T:2 * T]).then_inc(S("back_in"), 16)
        sp.dma_start(bvb[:], bv_d).then_inc(S("bv_in"), 16)
        tiles(N_B1, wbr_s[1], 0, i0=1)
        tiles(N_OUT, wout_s, 0)
        with sp.Fori(0, 16) as i:
            for h in range(2):
                slab(2 * i + (N_UP + h), (N_UP + h) % 2, wup_s[:, :, bass.ds(i * (2 * P) + P * h, P)])
        with sp.Fori(0, 8) as j:
            for b in range(KB):
                slab(4 * j + (N_DOWN + b), (N_DOWN + b) % 2, wdn_s[b][:, :, bass.ds(j * P, P)])
        for kc in range(KC):
            if kc < KC - POOL_OUT:
                sp.wait_ge(S("o_ready"), kc + 1)
            else:
                sp.wait_ge(S("p_ready"), 2 * (kc - (KC - POOL_OUT)) + 2)
            sp.dma_start(out[:, kc, :], ob[:, kc, :]).then_inc(S("out_done"), 16)
        sp.wait_ge(S("out_done"), 16 * KC)

    @block.gpsimd
    def _(pool):
        ms = nc.gpsimd.memset
        for t, v in ((ident, 0.0), (ones, 1.0), (bdones, 1.0), (m_strict, 1.0), (m_incl, 1.0), (scanm, 1.0),
                     (m_1, 1.0), (m_1t, 1.0), *((m, 1.0) for m in m_lev)):
            ms(t[:], v).then_inc(S("set"), 1)
        pool.wait_ge(S("set"), 8 + len(LEVELS))

        def split(n, slot):
            pool.wait_ge(S("w_hi"), n + 1)
            nc.gpsimd.tensor_tensor(wlo[:, slot, :, :], raw[:, slot, :, :], whi[:, slot, :, :].bitcast(F32),
                                    ALU.subtract).then_inc(S("w_split"), 1)

        sel = nc.gpsimd.affine_select

        def keep(view, base_, pattern, mult, op=ALU.is_ge, fill=0.0):
            return sel(out=view, in_=view, compare_op=op, fill=fill, base=base_, pattern=pattern,
                       channel_multiplier=mult)

        keep(ident[:], 0, [[-1, P]], 1, ALU.not_equal, 1.0).then_inc(S("ident"), 1)
        keep(scanm[:].rearrange("p (c t) -> p c t", c=NCH), 0, [[0, NCH], [1, CH]], 0,
             ALU.not_equal, 0.0).then_inc(S("masks"), 1)
        nm = [1]

        def step(ins):
            ins.then_inc(S("masks"), 1)
            nm[0] += 1
            pool.wait_ge(S("masks"), nm[0])

        def blocks(m, b):
            v = m[:].rearrange("p (n r) -> p n r", r=b)
            step(keep(v, 0, [[-b, P // b], [0, b]], 1))
            step(keep(v, b - 1, [[b, P // b], [0, b]], -1))

        blocks(bdones, CH)
        blocks(m_strict, CH)
        step(keep(m_strict[:], -1, [[1, P]], -1))
        blocks(m_incl, CH)
        step(keep(m_incl[:], 0, [[1, P]], -1))
        blocks(m_1, 2)
        step(keep(m_1[:], 0, [[-1, P]], 1))
        blocks(m_1t, 2)
        step(keep(m_1t[:], 0, [[1, P]], -1))
        for m, b in zip(m_lev, LEVELS):
            blocks(m, 2 * b)
            v = m[:].rearrange("p (n r) -> p n r", r=2 * b)
            step(keep(v, -b, [[-2 * b, P // (2 * b)], [0, 2 * b]], 1))
            step(keep(v, b - 1, [[0, P // (2 * b)], [-1, 2 * b]], 0))

        split(0, 0)
        split(1, 1)
        with pool.Fori(0, 26) as i:
            for h in range(2):
                split(2 * i + (2 + h), h)

        pool.wait_ge(S("wc"), 9)
        with pool.Fori(0, NCH) as c:
            tk = bass.ds(c * CH, CH)

            def operands(h, *which):
                for n, src in which:
                    nc.gpsimd.tensor_tensor(U2[n][h][:].rearrange("p m (e t) -> p m e t", e=2),
                                            bc2(src[:, 4 * h:4 * h + 4, tk]), mask4(bdones), ALU.mult) \
                        .then_inc(S(f"bd{h}"), 1)

            for h in range(2):
                pool.wait_ge(S(f"dS_mm{h}"), c + 1)
                pool.sem_inc(S("bd_go"), 1)
                operands(h, ("BDb", bt), ("BDk", kt))
            pool.wait_ge(S("bv"), 9)
            for h in range(2):
                nc.gpsimd.tensor_copy(U2["VD"][h][:].rearrange("p m (e t) -> p m e t", e=2),
                                      bc2(vb[:, 4 * h:4 * h + 4, tk])).then_inc(S(f"bd{h}"), 1)
            for h in range(2):
                operands(h, ("BDa", ar[:, 0]), ("BDr", ar[:, 1]))
            for h in range(2):
                split(2 * c + (N_GATE + 1 + h), (N_GATE + 1 + h) % 2)
        split(N_B1 + 1, (N_B1 + 1) % 2)
        pool.wait_ge(S("y_read0"), 9)
        pool.wait_ge(S("y_read1"), 9)
        pool.wait_ge(S("bv_in"), 16)
        for m in range(KC):
            nc.gpsimd.tensor_tensor(vb[:, m, :], vb[:, m, :], bvb[:, m, :], ALU.add).then_inc(S("y_sum"), 1)
        with pool.Fori(0, 39) as i:
            for h in range(2):
                split(2 * i + (71 + h), (71 + h) % 2)
        pool.wait_ge(S("x_in"), 48)
        pool.wait_ge(S("rms_root"), 4)
        pool.wait_ge(S("tile_ev"), E_ALL)
        for kc in range(KC - POOL_OUT, KC):
            nc.gpsimd.tensor_tensor(ob[:, kc, :], ob[:, kc, :], rst[:, 1, :], ALU.mult).then_inc(S("p_ready"), 1)
            pool.wait_ge(S("p_ready"), 2 * (kc - (KC - POOL_OUT)) + 1)
            nc.gpsimd.tensor_tensor(ob[:, kc, :], ob[:, kc, :], x1[:, kc, :], ALU.add).then_inc(S("p_ready"), 1)

    @block.tensor
    def _(pe):
        mm = nc.tensor.matmul

        for n_ in ("w_mm", "a_mm", "ss_mm", "bon_mm", "dS_mm0", "dS_mm1"):
            pe.sem_inc(S(n_), 1)

        def slab_mm(n, slot, bank, hi, lo, M=P, first=True, last=True, kc0=0, fresh=None, part=(0, KC), rows=KC):
            pe.wait_ge(S("w_split"), n + 1)
            for kc in range(*part):
                if fresh is not None:
                    pe.wait_ge(S("x_lo"), fresh + kc + 1)
                for k, (w, x) in enumerate(((whi, hi), (whi, lo), (wlo, hi))):
                    r = mm(bank[0:M, :], w[:, slot, kc, 0:M], x[:, kc0 + kc, :],
                           start=(first and kc == 0 and k == 0), stop=(last and kc == rows - 1 and k == 2))
            return r

        def rms(norm, bank):
            for kc in range(KC):
                pe.wait_ge(S("rms_sq"), norm + kc + 1)
                mm(bank[:], ones[:], sqt[:, kc % 2, :], start=(kc == 0), stop=(kc == KC - 1)) \
                    .then_inc(S("rms_mm"), 1)

        pe.wait_ge(S("set"), 8 + len(LEVELS))
        rms(N1, B[7])

        pe.wait_ge(S("tab_in"), 48)
        mm(B[6][0:16, 0:BETA], relb[0:32, :], oneh[0:32, :], start=True, stop=True).then_inc(S("small_mm"), 1)
        for n in range(13):
            if 2 <= n < 5:
                pe.wait_ge(S("lo_sh"), n - 1)
            elif n >= 5:
                pe.wait_ge(S("tile_ev"), n - 4)
            slab_mm(n, n % 2, B[n % 2], r1h, r1l, M=32 if n == 2 else P,
                    fresh=SP_H if n == 0 else None).then_inc(S("slab_mm"), 1)
            if n == 5:
                pe.wait_ge(S("vT"), 1)
                pe.wait_ge(S("ident"), 1)
                for t in range(4):
                    r = nc.tensor.transpose(B[2][:, P * t:P * t + P], vT[:, P * t:P * t + P], ident[:])
                r.then_inc(S("small_mm"), 1)

        def tiles(n0, hi, lo, ev, fresh=None):
            if fresh is not None:
                for h in range(2):
                    pe.wait_ge(S("tile_ev"), ev + h - 1)
                    slab_mm(n0 + h, (n0 + h) % 2, B[h], hi, lo,
                            fresh=fresh if h == 0 else None).then_inc(S("slab_mm"), 1)
            with pe.Fori(0 if fresh is None else 1, 4) as i:
                for h in range(2):
                    pe.wait_ge(S("tile_ev"), 2 * i + (ev + h - 1))
                    slab_mm(2 * i + (n0 + h), (n0 + h) % 2, B[h], hi, lo).then_inc(S("slab_mm"), 1)

        pe.wait_ge(S("tile_ev"), 10)

        def scores(c):
            o, t = c % 2, c // 2
            if c == 0:
                pe.wait_ge(S("kb_in"), 16 * 12)
                pe.wait_ge(S("tile_ev"), 10)
            b0 = 2 + 2 * (c % 2)
            if c >= 2:
                pe.wait_ge(S("at_lg"), 2 * c)
            for j in range(4):
                r = mm(B[b0 + j // 2][:].rearrange("p (a n) -> p a n", a=2)[:, j % 2, :],
                       q[:, j, c, :, :].rearrange("p e t -> p (e t)"),
                       kb[:, o, j // 2, :, t, :], start=True, stop=True)
            r.then_inc(S("at_sc"), 1)

        def gate_part(c, k0, k1):
            if k0 == k1:
                return
            if k0 == 0 and c >= 1:
                pe.wait_ge(S("tile_ev"), E_G0 + c)
            r = slab_mm(N_G0 + c, (N_G0 + c) % 2, B[1], r1h, r1l, part=(k0, k1))
            if k1 == KC:
                r.then_inc(S("slab_mm"), 1)

        def probs_values(c):
            k1, k2 = (KC, KC) if c == 0 else (3, KC) if c == NCH - 1 else (3, 6)
            gate_part(c, 0, k1)
            pe.wait_ge(S("at_p"), c + 1)
            for g in range(8):
                r = nc.tensor.transpose(B[6 + g // 4][:, P * (g % 4):P * (g % 4) + P], lg[:, c % 2, g, :], ident[:])
            r.then_inc(S("at_tr"), 1)
            gate_part(c, k1, k2)
            pe.wait_ge(S("at_pT"), 2 * c + 2)
            if c >= 1:
                pe.wait_ge(S("at_lo"), c)
            vv = (v2, v1)[c % 2]
            for g in range(2):
                for p in range(2):
                    r = mm(B[0][64 * p:64 * p + 64, 256 * g:256 * g + 256],
                           vv[:, c // 2, 64 * g:64 * g + 64],
                           pT[:, c % 2, :, :].rearrange("k (j p) q -> k j p q", p=2)[:, 2 * g:2 * g + 2, p, :],
                           start=True, stop=True)
            r.then_inc(S("at_o"), 1)
            gate_part(c, k2, KC)

        pe.wait_ge(S("v_ready"), 3)
        pe.wait_ge(S("beta_ev"), 1)
        scores(0)
        for c in range(NCH):
            if c + 1 < NCH:
                scores(c + 1)
            probs_values(c)
        pe.wait_ge(S("at_lo"), NCH)
        pe.wait_ge(S("tile_ev"), E_B0)
        tiles(N_B0, r2h, r2l, E_B0)

        pe.wait_ge(S("tile_ev"), E_GATE)
        pe.wait_ge(S("masks"), 1 + 2 + 3 + 3 + 3 + 3 + 4 * len(LEVELS))
        with pe.Fori(0, 4) as i:
            for h in range(2):
                m = 2 * i + h
                n = 6 * i + (N_PAIR + 3 * h)
                s0 = (N_PAIR + 3 * h) % 2
                pe.wait_ge(S("k_sh"), m + 1)
                slab_mm(n, s0, B[0], r1h, r1l).then_inc(S("slab_mm"), 1)
                pe.wait_ge(S(f"wl{h}"), i * 32 + 32)
                pe.wait_ge(S("tw"), m + 1)
                mm(B[1][:], wl[:, h, 0, :], tl[:], start=True, stop=True).then_inc(S("w_mm"), 1)
                pe.wait_ge(S("ta"), m + 1)
                mm(B[2][:], wl[:, h, 1, :], tl[:], start=True, stop=True).then_inc(S("a_mm"), 1)
                pe.wait_ge(S("r_sh"), m + 1)
                slab_mm(n + 1, (s0 + 1) % 2, B[3], r1h, r1l, part=(0, 4))
                pe.wait_ge(S("sq"), m + 2)
                pe.wait_ge(S("ssm"), m + 1)
                mm(B[4][:], bdones[:], tmp["sq"][:], start=True, stop=True).then_inc(S("ss_mm"), 1)
                slab_mm(n + 1, (s0 + 1) % 2, B[3], r1h, r1l, part=(4, KC)).then_inc(S("slab_mm"), 1)
                pe.wait_ge(S("v_sh"), m + 1)
                slab_mm(n + 2, s0, B[5], r1h, r1l).then_inc(S("slab_mm"), 1)
                pe.wait_ge(S("p"), m + 2)
                pe.wait_ge(S("bv"), m + 1)
                mm(B[6][:], bdones[:], tmp["p"][:], start=True, stop=True).then_inc(S("bon_mm"), 1)

        pe.wait_ge(S("wc"), 9)
        with pe.Fori(0, NCH) as c:
            tk = bass.ds(c * CH, CH)
            tr = nc.tensor.transpose

            def each(h, body):
                for m in range(4):
                    r = body(m)
                return r

            def out4(bank, m):
                return v4(bank)[:, m, :]

            def gate_half(h):
                if h == 0:
                    pe.wait_ge(S("bv"), 9)
                    pe.wait_ge(S("tile_ev"), c + E_GATE)
                slab_mm(2 * c + (N_GATE + h), (N_GATE + h) % 2, B[6], r1h, r1l, first=(h == 0), last=(h == 1),
                        kc0=4 * h, part=(0, KC // 2), rows=KC // 2).then_inc(S("slab_mm"), 1)

            for h in range(2):
                b = B[3 * h:3 * h + 3]
                pe.wait_ge(S(f"bd{h}"), c * 5 + 2)
                pe.wait_ge(S(f"y_read{h}"), c + 1)
                for n, k in (("BDb", 0), ("BDk", 1)):
                    for m in range(4):
                        r = mm(v4(b[k])[:, m, :].rearrange("p (x t) -> p x t", x=2), U2[n][h][:, m, :],
                               ar[:, :, 4 * h + m, tk], start=True, stop=True)
                    r.then_inc(S(f"sc_mm{h}"), 1)
            gate_half(0)
            for h in range(2):
                b = B[3 * h:3 * h + 3]
                pe.wait_ge(S(f"sc_ev{h}"), c * 5 + 5)
                each(h, lambda m: tr(out4(b[2], m), U2["AI"][h][:, m, :], ident[:])).then_inc(S(f"ai_mm{h}"), 1)
                each(h, lambda m: tr(out4(b[0], m), U2["BDb"][h][:, m, :], ident[:])).then_inc(S(f"tok_mm{h}"), 1)
                each(h, lambda m: tr(out4(b[1], m), U2["BDk"][h][:, m, :], ident[:])).then_inc(S(f"tok_mm{h}"), 1)
            for h in range(2):
                b = B[3 * h:3 * h + 3]
                pe.wait_ge(S(f"bd{h}"), c * 5 + 3)
                pe.wait_ge(S(f"tok_ev{h}"), c * 4 + 1)
                each(h, lambda m: tr(out4(b[0], m), U2["VD"][h][:, m, :], ident[:])).then_inc(S(f"tok_mm{h}"), 1)
            for k in range(len(LEVELS)):
                for h in range(2):
                    b = B[3 * h:3 * h + 3]
                    pe.wait_ge(S(f"x_ready{h}"), c * 5 + (k + 1))
                    each(h, lambda m: mm(out4(b[2], m), U2["aab"][h][:, m, :], U2["X"][h][:, m, :],
                                         start=True, stop=True)).then_inc(S(f"q_mm{h}"), 1)
                    if k > 0:
                        each(h, lambda m: tr(out4(b[0], m), U2["X"][h][:, m, :], ident[:])) \
                            .then_inc(S(f"xt_mm{h}"), 1)
                for h in range(2):
                    b = B[3 * h:3 * h + 3]
                    pe.wait_ge(S(f"q_ev{h}"), c * 5 + (k + 1))
                    pe.wait_ge(S(f"xt_ready{h}"), c * 5 + (k + 1))
                    if k == 0:
                        pe.wait_ge(S(f"tok_ev{h}"), c * 4 + 4)
                    if k < len(LEVELS) - 1:
                        each(h, lambda m: mm(out4(b[1], m), U2["XT"][h][:, m, :], U2["Qs"][h][:, m, :],
                                             start=True, stop=True)).then_inc(S(f"d_mm{h}"), 1)
                    else:
                        each(h, lambda m: mm(out4(b[1], m), U2["Qs"][h][:, m, :], U2["XT"][h][:, m, :],
                                             start=True, stop=True)).then_inc(S(f"d_mm{h}"), 1)

            def o64(bank, m):
                return bank[:].rearrange("p (m n) -> p m n", n=CH)[:, m, :]

            for h in range(2):
                b = B[3 * h:3 * h + 3]
                pe.wait_ge(S(f"bd{h}"), c * 5 + 5)
                pe.wait_ge(S(f"st{h}"), c + 1)
                for m in range(4):
                    mm(o64(b[0], m), U2["BDa"][h][:, m, :], U2["St"][h][:, m, :], start=True, stop=False)
                    r = mm(o64(b[0], m), U2["aak"][h][:, m, :], U2["Vc"][h][:, m, :], start=False, stop=True)
                r.then_inc(S(f"g_mm{h}"), 1)
            for h in range(2):
                b = B[3 * h:3 * h + 3]
                pe.wait_ge(S(f"g_ev{h}"), c + 1)
                pe.wait_ge(S(f"xt_last{h}"), c + 1)
                for m in range(4):
                    r = mm(o64(b[2], m), U2["XT"][h][:, m, :], U2["G"][h][:, m, :], start=True, stop=True)
                r.then_inc(S(f"u_mm{h}"), 1)
            for h in range(2):
                b = B[3 * h:3 * h + 3]
                pe.wait_ge(S(f"u_ev{h}"), c + 1)
                for m in range(4):
                    mm(o64(b[1], m), U2["BDr"][h][:, m, :], U2["St"][h][:, m, :], start=True, stop=False)
                    mm(o64(b[1], m), U2["arb"][h][:, m, :], U2["U"][h][:, m, :], start=False, stop=False)
                    r = mm(o64(b[1], m), U2["ark"][h][:, m, :], U2["Vc"][h][:, m, :], start=False, stop=True)
                r.then_inc(S(f"y_mm{h}"), 1)
                for m in range(4):
                    mm(o64(b[0], m), U2["btok"][h][:, m, :], U2["U"][h][:, m, :], start=True, stop=False)
                    r = mm(o64(b[0], m), U2["ktok"][h][:, m, :], U2["Vc"][h][:, m, :], start=False, stop=True)
                r.then_inc(S(f"dS_mm{h}"), 1)
            gate_half(1)
            for h in range(2):
                pe.wait_ge(S(f"yn{h}"), c + 1)
                for m in range(4):
                    for e in range(2):
                        r = mm(B[3 * h + 2][64 * e:64 * e + 64, CH * m:CH * m + CH], U2["Y"][h][:, m, :],
                               ident[:, 64 * e:64 * e + 64], start=True, stop=True)
                r.then_inc(S(f"yt_mm{h}"), 1)

        pe.wait_ge(S("y_read0"), 9)
        pe.wait_ge(S("y_read1"), 9)
        pe.wait_ge(S("back_in"), 64)
        for m in range(KC):
            if m >= 2:
                pe.wait_ge(S("x_f"), SP_Y + m - 1)
            mm(B[4 + m % 2][:], wg[:, 0, P * m:P * m + P], sgb[:, 0, :], start=True, stop=False)
            mm(B[4 + m % 2][:], wg[0:32, 1, P * m:P * m + P], sgb[0:32, 1, :], start=False, stop=True) \
                .then_inc(S("g_mm"), 1)
        tiles(N_B1, r1h, r1l, E_B1, fresh=SP_Y)

        def square_sum(norm, j, slot, bank, first=False, last=False):
            pe.wait_ge(S("rms_sq"), j + (norm + 1))
            mm(bank[:], ones[:], sqt[:, slot, :], start=first, stop=last).then_inc(S("rms_mm"), 1)

        def out_tile(i, h, first=False):
            pe.wait_ge(S("tile_ev"), 2 * i + (E_OUT + h - 1))
            slab_mm(2 * i + (N_OUT + h), (N_OUT + h) % 2, B[h], r2h, r2l,
                    fresh=SP_M if first else None).then_inc(S("slab_mm"), 1)
            if not first:
                square_sum(N2, 2 * i + (h - 1), 1 - h, B[7], first=isinstance(i, int) and i == 0)

        out_tile(0, 0, first=True)
        out_tile(0, 1)
        with pe.Fori(1, 4) as i:
            for h in range(2):
                out_tile(i, h)
        square_sum(N2, 7, 1, B[7], last=True)
        rms(N3, B[6])
        pe.wait_ge(S("tile_ev"), E_UP)
        slab_mm(N_UP, N_UP % 2, B[0], r1h, r1l, fresh=SP_F).then_inc(S("slab_mm"), 1)
        slab_mm(N_UP + 1, (N_UP + 1) % 2, B[1], r1h, r1l).then_inc(S("slab_mm"), 1)
        with pe.Fori(1, 16) as i:
            for h in range(2):
                pe.wait_ge(S("tile_ev"), 2 * i + (E_UP + h - 1))
                slab_mm(2 * i + (N_UP + h), (N_UP + h) % 2, B[h], r1h, r1l).then_inc(S("slab_mm"), 1)

        def down_tile(i, h, first=False):
            pe.wait_ge(S("tile_ev"), 2 * i + (E_DOWN + h - 1))
            for b in range(KB):
                pe.wait_ge(S("f_lo"), KC * (b + 1))
                slab_mm(8 * i + (N_DOWN + 4 * h + b), (N_DOWN + b) % 2, B[2 + h], fh, fl,
                        first=(b == 0), last=(b == KB - 1), kc0=KC * b).then_inc(S("slab_mm"), 1)
            if not first:
                square_sum(N4, 2 * i + (h - 1), 1 - h, B[7], first=isinstance(i, int) and i == 0)

        down_tile(0, 0, first=True)
        down_tile(0, 1)
        with pe.Fori(1, 4) as i:
            for h in range(2):
                down_tile(i, h)
        square_sum(N4, 7, 1, B[7], last=True)

    @block.scalar
    def _(act):
        A = nc.scalar.activation

        act.sem_inc(S("gate_out"), 16)
        for n_ in ("k_sc", "tw", "ta", "sq", "eW", "eWi", "eWx", "r_sc", "nrm", "v_sc"):
            act.sem_inc(S(n_), 1)

        def rms_sq(norm, src, ready, late=None):
            for kc in range(KC):
                if late and kc == KC // 2:
                    act.wait_ge(S(late), 16)
                if ready:
                    act.wait_ge(S(ready), kc + 1)
                if kc >= 2:
                    act.wait_ge(S("rms_mm"), norm + kc - 1)
                A(sqt[:, kc % 2, :], src[:, kc, :], ACT.Square).then_inc(S("rms_sq"), 1)

        def rms_root(norm):
            act.wait_ge(S("rms_rec"), norm // 4 + 2)
            A(rst[:, 1, :], rst[:, 0, :], ACT.Sqrt).then_inc(S("rms_root"), 1)

        def split_hi(sp_, hi):
            for kc in range(KC):
                act.wait_ge(S("x_f"), sp_ + kc + 1)
                A(hi[:, kc, :], hx[:, kc % 2, :], ACT.Copy).then_inc(S("x_hi"), 1)

        def w_hi(n, slot, count):
            act.wait_ge(S(f"w_raw{slot}"), count)
            A(whi[:, slot, :, :], raw[:, slot, :, :], ACT.Copy).then_inc(S("w_hi"), 1)

        def after(n0, i, k, per):
            act.wait_ge(S("slab_mm"), per * i + (n0 + k + 1))
            w_hi(None, (n0 + k) % 2, i * (8 * per) + 16 * ((n0 + k + 2) // 2 + 1))

        act.wait_ge(S("x_in"), 16)
        rms_sq(N1, xs, None, late="x_in_late")
        w_hi(0, 0, 16)
        w_hi(1, 1, 16)
        rms_root(N1)
        split_hi(SP_H, r1h)
        def bias_out():
            act.wait_ge(S("beta_ev"), 1)
            act.dma_start(beta_d, beta[0:16, :].unsqueeze(1).to_broadcast([16, CH, BETA])).then_inc(S("beta_out"), 16)

        def bias_back():
            act.wait_ge(S("beta_out"), 16)
            for e, p in ((0, 0), (0, 1), (1, 0), (1, 1)):
                hstep = CH * BETA
                for lo_, dst0 in ((0, 0), (1, 128)):
                    n = 128 if lo_ == 0 else 64
                    src = bass.AP(tensor=beta_t, offset=(2 * e + p) * hstep + CH - 1,
                                  ap=[[BETA - 1, CH], [4 * hstep, 4], [1, n]])
                    act.dma_start(bias[64 * e:64 * e + 64, p:8:2, dst0:dst0 + n], src).then_inc(S("bias_in"), 16)

        for n in range(13):
            act.wait_ge(S("slab_mm"), n + 1)
            w_hi(n + 2, n % 2, 16 * ((n + 2) // 2 + 1))
            if n == 6:
                bias_out()
            if n == 8:
                bias_back()
            b = B[n % 2]
            if n < 3:
                M = 32 if n == 2 else P
                dst = (tl, sg[:, 0, :], sg[:, 1, :])[n]
                dst = dst[0:M, :]
                A(dst, b[0:M, :], ACT.Copy, scale=par[0:M, OM_L + n:OM_L + n + 1]).then_inc(S("lo_sc"), 1)
                act.wait_ge(S("lo_sh"), n + 1)
                if n == 0:
                    A(tl[0:64, :], tl[0:64, :], ACT.Tanh).then_inc(S("lo_th"), 1)
                else:
                    A(dst, dst, ACT.Tanh, scale=0.5).then_inc(S("lo_th"), 1)
            elif n == 3:
                A(kT[:], b[:], ACT.Copy).then_inc(S("tile_ev"), 1)
                act.wait_ge(S("tile_ev"), 1)
                act.wait_ge(S("kb_zero"), 1)
                for o in range(2):
                    for g in range(2):
                        for p in range(2):
                            ksrc = kT[64 * g:64 * g + 64, :].rearrange("d (t x) -> d t x", x=P)
                            kdst = kb[64 * p:64 * p + 64, o, g, p, :, :]
                            if o == 1:
                                act.dma_start(kdst, ksrc).then_inc(S("kb_in"), 16)
                            else:
                                act.dma_start(kdst[:, :, 0:64], ksrc[:, :, 0:64]).then_inc(S("kb_in"), 16)
                                act.dma_start(kdst[:, 1:4, 64:128], ksrc[:, 0:3, 64:128]).then_inc(S("kb_in"), 16)
            elif n == 4:
                A(vT[:], b[:], ACT.Copy).then_inc(S("vT"), 1)
                act.wait_ge(S("vT"), 1)
                act.sem_inc(S("tile_ev"), 1)
            else:
                A(q[:, (n - 5) // 2, :, (n - 5) % 2, :], b[:].rearrange("p (c t) -> p c t", c=NCH), ACT.Copy) \
                    .then_inc(S("tile_ev"), 1)

        def gate_tile(c):
            act.wait_ge(S("slab_mm"), N_G0 + c + 1)
            w_hi(N_G0 + c + 2, (N_G0 + c) % 2, 16 * ((N_G0 + c + 2) // 2 + 1))
            A(t0[:, c, :], B[1][:], ACT.Tanh, scale=0.5, bias=pcol(H_GB0, c)).then_inc(S("tile_ev"), 1)

        for c in range(NCH):
            act.wait_ge(S("at_sub"), c + 1)
            A(lg[:, c % 2, :, :], lg[:, c % 2, :, :], ACT.Exp).then_inc(S("at_exp"), 1)
            A(asm[:, c % 2, 1, :], asm[:, c % 2, 1, :], ACT.Exp).then_inc(S("at_exs"), 1)
            if c >= 1:
                gate_tile(c - 1)
            act.wait_ge(S("at_tr"), c + 1)
            for k in range(2):
                A(pT[:, c % 2, 4 * k:4 * k + 4, :], v4(B[6 + k]), ACT.Copy).then_inc(S("at_pT"), 1)
            if c == NCH - 1:
                gate_tile(c)
            act.wait_ge(S("at_o"), c + 1)
            A(r2h[:, :, CH * c:CH * c + CH], B[0][:].rearrange("p (m t) -> p m t", m=KC), ACT.Copy) \
                .then_inc(S("at_hi"), 1)
        with act.Fori(0, 4) as i:
            for h in range(2):
                after(N_B0, i, h, 2)
                act.wait_ge(S("tile_ev"), 2 * i + (E_B0 + h + 1))
                act.dma_start(m0_d[:, bass.ds(2 * i + h, 1), :], t0[:, bass.ds(2 * i + h, 1), :]) \
                    .then_inc(S("spilled"), 16)
        act.dma_start(sg_d[:, 0:T], sg[:, 0, :]).then_inc(S("spilled"), 16)
        act.dma_start(sg_d[0:32, T:2 * T], sg[0:32, 1, :]).then_inc(S("spilled"), 16)
        act.wait_ge(S("spilled"), 160)

        with act.Fori(0, 4) as i:
            for h in range(2):
                m = 2 * i + h
                n = 6 * i + (N_PAIR + 3 * h)
                act.wait_ge(S("slab_mm"), n + 1)
                act.wait_ge(S("ax"), m + 1)
                A(tmp["kS"][:], B[0][:], ACT.Copy, scale=pcol(OM_K, m)).then_inc(S("k_sc"), 1)
                after(N_PAIR, i, 3 * h, 6)
                act.wait_ge(S("k_sh"), m + 2)
                act.wait_ge(S("ss_mm"), m + 1)
                A(tmp["sq"][:], tmp["kS"][:], ACT.Square, scale=pcol(COL["k_k"], m)).then_inc(S("sq"), 1)
                act.wait_ge(S("w_mm"), m + 2)
                act.wait_ge(S("ld"), m + 1)
                A(tmp["tw"][:], B[1][:], ACT.Tanh, scale=0.5, bias=pcol(H_W0, m)).then_inc(S("tw"), 1)
                act.wait_ge(S("a_mm"), m + 2)
                act.wait_ge(S("aa"), m + 1)
                A(tmp["ta"][:], B[2][:], ACT.Tanh, scale=0.5, bias=pcol(H_A0, m)).then_inc(S("ta"), 1)
                act.wait_ge(S("cum"), m + 2)
                act.wait_ge(S("wc"), m + 1)
                A(tmp["eW"][:], tmp["cum"][:], ACT.Exp).then_inc(S("eW"), 1)
                act.wait_ge(S("bt"), m + 1)
                A(tmp["eWi"][:], tmp["cum"][:], ACT.Exp, scale=-1.0).then_inc(S("eWi"), 1)
                act.wait_ge(S("cx"), m + 2)
                act.wait_ge(S("at"), m + 1)
                A(tmp["eWx"][:], tmp["cx"][:], ACT.Exp).then_inc(S("eWx"), 1)
                act.wait_ge(S("ssm"), m + 2)
                act.wait_ge(S("inv"), m + 1)
                A(tmp["nrm"][:], tmp["ssm"][:], ACT.Sqrt).then_inc(S("nrm"), 1)
                if h == 1:
                    act.wait_ge(S("bv"), m + 1)
                    act.dma_start(bv_d[:, bass.ds(2 * i, 1), :], bv[:, bass.ds(2 * i, 1), :]) \
                        .then_inc(S("spilled"), 16)
                act.wait_ge(S("slab_mm"), n + 2)
                act.wait_ge(S("p"), m + 1)
                A(tmp["rS"][:], B[3][:], ACT.Copy, scale=pcol(OM_R, m)).then_inc(S("r_sc"), 1)
                after(N_PAIR, i, 3 * h + 1, 6)
                after(N_PAIR, i, 3 * h + 2, 6)
                A(vb[:, m, :], B[5][:], ACT.Copy, scale=pcol(OM_V, m)).then_inc(S("v_sc"), 1)

        act.wait_ge(S("bv"), 9)
        act.dma_start(bv_d[:, 1:KC:2, :], bv[:, 1:KC:2, :]).then_inc(S("spilled"), 16)
        act.wait_ge(S("spilled"), 240)

        with act.Fori(0, NCH) as c:
            after(N_GATE, c, 0, 2)
            for h in range(2):
                b = B[3 * h:3 * h + 3]
                act.wait_ge(S(f"tok_mm{h}"), c * 3 + 1)
                A(U2["btok"][h][:], v4(b[0]), ACT.Copy).then_inc(S(f"tok_ev{h}"), 1)
                act.wait_ge(S(f"tok_mm{h}"), c * 3 + 2)
                A(U2["ktok"][h][:], v4(b[1]), ACT.Copy).then_inc(S(f"tok_ev{h}"), 1)
            for h in range(2):
                b = B[3 * h:3 * h + 3]
                act.wait_ge(S(f"tok_mm{h}"), c * 3 + 3)
                for e in range(2):
                    A(U2["Vc"][h][64 * e:64 * e + 64, :, :], v4(b[0])[64 * e:64 * e + 64, :, 64 * e:64 * e + 64],
                      ACT.Copy).then_inc(S(f"tok_ev{h}"), 1)
            for k in range(len(LEVELS) - 1):
                for h in range(2):
                    act.wait_ge(S(f"xt_mm{h}"), c * 4 + (k + 1))
                    A(U2["XT"][h][:], v4(B[3 * h]), ACT.Copy).then_inc(S(f"xt_ready{h}"), 1)
            for h in range(2):
                act.wait_ge(S(f"g_mm{h}"), c + 1)
                A(U2["G"][h][:], B[3 * h][:, 0:256].rearrange("p (m i) -> p m i", m=4), ACT.Copy) \
                    .then_inc(S(f"g_ev{h}"), 1)
            for h in range(2):
                act.wait_ge(S(f"u_mm{h}"), c + 1)
                A(U2["U"][h][:], B[3 * h + 2][:, 0:256].rearrange("p (m i) -> p m i", m=4), ACT.Copy) \
                    .then_inc(S(f"u_ev{h}"), 1)
            for h in range(2):
                act.wait_ge(S(f"yc{h}"), c + 1)
                A(U2["Yt"][h][:], U2["Y"][h][:], ACT.Square).then_inc(S(f"ysq{h}"), 1)
            for h in range(2):
                act.wait_ge(S(f"yv{h}"), c + 1)
                A(gn[:, h, 3, :], gn[:, h, 2, :], ACT.Sqrt).then_inc(S(f"yr{h}"), 1)
            after(N_GATE, c, 1, 2)
            act.wait_ge(S("gate_out"), c * 16 + 16)
            A(gs[:], B[6][:], ACT.Tanh, scale=0.5, bias=pcol(H_GB1, c)).then_inc(S("tile_ev"), 1)
            act.wait_ge(S("tile_ev"), c + (E_GATE + 1))
            act.dma_start(t1_d[:, bass.ds(c, 1), :].rearrange("p a t -> p (a t)"), gs[:]) \
                .then_inc(S("gate_out"), 16)

        act.wait_ge(S("y_read0"), 9)
        act.wait_ge(S("y_read1"), 9)
        act.wait_ge(S("gate_out"), 16 * 9)
        act.dma_start(m0b[:], m0_d).then_inc(S("gates_in"), 16)
        act.dma_start(t1b[:], t1_d).then_inc(S("gates_in"), 16)
        split_hi(SP_Y, r1h)
        with act.Fori(0, 4) as i:
            for h in range(2):
                after(N_B1, i, h, 2)
                act.wait_ge(S("x_f"), 2 * i + (SP_M + h + 1))
                A(r2h[:, 2 * i + h, :], hx[:, h, :], ACT.Copy).then_inc(S("x_hi"), 1)
        act.wait_ge(S("x_f"), SP_Y + 8)
        act.dma_start(xr[:], xT).then_inc(S("x_in"), 16)
        with act.Fori(0, 4) as i:
            for h in range(2):
                after(N_OUT, i, h, 2)
                act.wait_ge(S("rms_mm"), 2 * i + (N2 + h - 1))
                A(sqt[:, h, :], B[h][:], ACT.Square, scale=0.5).then_inc(S("rms_sq"), 1)
                A(mix[:, 2 * i + h, :], B[h][:], ACT.Copy, scale=0.5).then_inc(S("tile_ev"), 1)
        rms_root(N2)
        rms_sq(N3, xr, "x1_f")
        act.dma_start(x1_d, flat(xr)).then_inc(S("spilled"), 16)
        rms_root(N3)
        split_hi(SP_F, r1h)
        act.wait_ge(S("spilled"), 256)
        with act.Fori(0, 16) as i:
            for h in range(2):
                j = 2 * i + h
                after(N_UP, i, h, 2)
                act.wait_ge(S(f"f_lo{h}"), i + 1)
                A(sqt[:, h, :], B[h][:], ACT.Relu).then_inc(S(f"f_relu{h}"), 1)
                act.wait_ge(S("tile_ev"), 2 * i + (E_UP + h + 1))
                A(fh[:, j, :], hx[:, h, :], ACT.Copy).then_inc(S(f"f_hi{h}"), 1)
        act.wait_ge(S("slab_mm"), N_DOWN)
        act.dma_start(flat(x1), x1_d).then_inc(S("x_in"), 16)

        def down_out(i, h):
            act.wait_ge(S("rms_mm"), 2 * i + (N4 + h - 1))
            A(sqt[:, h, :], B[2 + h][:], ACT.Square).then_inc(S("rms_sq"), 1)
            j = 2 * i + h
            gain = col("post_ffn", j) if isinstance(i, int) else pcol(COL["post_ffn"], j)
            A(ob[:, j, :], B[2 + h][:], ACT.Copy, scale=gain).then_inc(S("tile_ev"), 1)

        with act.Fori(0, 3) as i:
            for h in range(2):
                for b in range(KB):
                    after(N_DOWN, i, 4 * h + b, 8)
                down_out(i, h)
        for h in range(2):
            for b in range(KB):
                if 4 * h + b < 6:
                    after(N_DOWN + 24, 0, 4 * h + b, 8)
            act.wait_ge(S("slab_mm"), N_DOWN + 24 + 4 * h + 4)
            down_out(3, h)
        rms_root(N4)

    @block.vector
    def _(dve):
        TT = nc.vector.tensor_tensor
        TS = nc.vector.tensor_scalar
        STT = nc.vector.scalar_tensor_tensor
        A_, M_, SUB = ALU.add, ALU.mult, ALU.subtract

        for n_ in ("k_sh", "ld", "cum", "cx", "aa", "kp", "r_sh", "wc", "p", "ssm", "inv", "ax", "be", "at", "bt", "v_sh", "bv", "y_read0", "y_read1", "f_lo0", "f_lo1"):
            dve.sem_inc(S(n_), 1)

        def rms_rec(norm, bank):
            dve.wait_ge(S("rms_mm"), norm + KC)
            TS(rst[:, 0, :], bank[:], 1.0 / D, EPS, M_, A_).then_inc(S("rms_rec"), 1)
            dve.wait_ge(S("rms_rec"), norm // 4 + 1)
            nc.vector.reciprocal(rst[:, 0, :], rst[:, 0, :]).then_inc(S("rms_rec"), 1)
            dve.wait_ge(S("rms_root"), norm // 8 + 1)

        def norm_split(src, gain, sp_, hi, lo):
            for kc in range(KC + 1):
                if kc < KC:
                    if kc >= 2:
                        dve.wait_ge(S("x_lo"), sp_ + kc - 1)
                    STT(hx[:, kc % 2, :], src[:, kc, :], col(gain, kc), rst[:, 1, :], M_, M_).then_inc(S("x_f"), 1)
                if kc >= 1:
                    remainder(kc - 1, sp_, hi, lo)

        def remainder(kc, sp_, hi, lo):
            dve.wait_ge(S("x_f"), sp_ + kc + 1)
            dve.wait_ge(S("x_hi"), sp_ + kc + 1)
            TT(lo[:, kc, :], hx[:, kc % 2, :], hi[:, kc, :].bitcast(F32), SUB).then_inc(S("x_lo"), 1)

        dve.wait_ge(S("par_in"), 16)
        for n_, (o, s_, w_, a, b) in enumerate((
                (OM_R, COL["mu_r"], 24, -1.0, 1.0), (OM_L, MU_L, 3, -1.0, 1.0), (H_W0, COL["w0"], 16, 0.5, 0.0),
                (H_KA, COL["k_a"], 8, 0.5, 0.0), (OH_KA, COL["k_a"], 8, -0.5, 1.0),
                (N_KK, COL["k_k"], 8, -1.0, 0.0), (H_GB0, COL["gb0"], 16, 0.5, 0.0))):
            TS(par[:, o:o + w_], par[:, s_:s_ + w_], a, b, M_, A_).then_inc(S("par_done"), 1)
        dve.wait_ge(S("par_done"), 7)

        nc.vector.memset(kb[:].rearrange("p a b c d e -> p (a b c d e)"), 0.0).then_inc(S("kb_zero"), 1)
        nc.vector.memset(v2[:], 0.0).then_inc(S("kb_zero"), 1)
        rms_rec(N1, B[7])
        norm_split(xs, "pre_mix", SP_H, r1h, r1l)
        dve.wait_ge(S("small_mm"), 1)
        nc.vector.tensor_copy(beta[0:16, :], B[6][0:16, 0:BETA]).then_inc(S("beta_ev"), 1)

        for n in range(3):
            M = 32 if n == 2 else P
            dst = (tl[:], sg[:, 0, :], sg[:, 1, :])[n][0:M]
            dve.wait_ge(S("lo_sc"), n + 1)
            STT(dst[:, 1:T], B[n % 2][0:M, 0:T - 1], par[0:M, MU_L + n:MU_L + n + 1], dst[:, 1:T], M_, A_) \
                .then_inc(S("lo_sh"), 1)
        for n in (1, 2):
            M = 32 if n == 2 else P
            dve.wait_ge(S("lo_th"), n + 1)
            TS(sg[0:M, n - 1, :], sg[0:M, n - 1, :], 0.5, 0.5, M_, A_)
        dve.wait_ge(S("small_mm"), 2)
        dve.wait_ge(S("kb_zero"), 2)
        nc.vector.tensor_copy(v1[:], v4(B[2])).then_inc(S("v_ready"), 1)
        nc.vector.tensor_copy(v2[0:64], v4(B[2])[0:64]).then_inc(S("v_ready"), 1)
        nc.vector.tensor_copy(v2[64:128, 1:4, :], v4(B[2])[64:128, 0:3, :]).then_inc(S("v_ready"), 1)

        dve.wait_ge(S("bias_in"), 16 * 8)
        dve.wait_ge(S("tab_in"), 48)

        def logits(c):
            dve.wait_ge(S("at_sc"), c + 1)
            if c >= 2:
                dve.wait_ge(S("at_tr"), c - 1)
            L = lg[:, c % 2].rearrange("p (k g) n -> p k g n", k=2)
            bs = bias[:, :, 0:128] if c % 2 else bias[:, :, 64:192]
            bs = bs.rearrange("p (k g) n -> p k g n", k=2)
            for k in range(2):
                ps = v4(B[2 + 2 * (c % 2) + k])
                if c == 0:
                    STT(L[:, k, :, 0:64], ps[:, :, 0:64], HD ** -0.5, bs[:, k, :, 0:64], M_, A_) \
                        .then_inc(S("at_lg"), 1)
                    nc.vector.memset(L[:, k, :, 64:128], -1e30).then_inc(S("at_lg"), 1)
                else:
                    STT(L[:, k], ps, HD ** -0.5, bs[:, k], M_, A_).then_inc(S("at_lg"), 1)
            dve.wait_ge(S("at_lg"), 2 * c + 4)
            a = asm[:, c % 2]
            L = lg[:, c % 2]
            nc.vector.tensor_reduce(a[:, 0, :], L, AX, ALU.max).then_inc(S("at_soft"), 1)
            dve.wait_ge(S("at_soft"), 6 * c + 1)
            TT(a[:, 0, :], a[:, 0, :], sinkT[:], ALU.max).then_inc(S("at_soft"), 1)
            dve.wait_ge(S("at_soft"), 6 * c + 2)
            TT(a[:, 1, :], sinkT[:], a[:, 0, :], SUB).then_inc(S("at_soft"), 1)
            dve.wait_ge(S("at_soft"), 6 * c + 3)
            TT(L, L, a[:, 0, :].unsqueeze(2).to_broadcast([P, 8, P]), SUB).then_inc(S("at_sub"), 1)

        def normalise(c):
            a = asm[:, c % 2]
            L = lg[:, c % 2]
            dve.wait_ge(S("at_exp"), c + 1)
            nc.vector.tensor_reduce(a[:, 2, :], L, AX, A_).then_inc(S("at_soft"), 1)
            dve.wait_ge(S("at_soft"), 6 * c + 4)
            dve.wait_ge(S("at_exs"), c + 1)
            TT(a[:, 3, :], a[:, 2, :], a[:, 1, :], A_).then_inc(S("at_soft"), 1)
            dve.wait_ge(S("at_soft"), 6 * c + 5)
            nc.vector.reciprocal(a[:, 4, :], a[:, 3, :]).then_inc(S("at_soft"), 1)
            dve.wait_ge(S("at_soft"), 6 * c + 6)
            TT(L, L, a[:, 4, :].unsqueeze(2).to_broadcast([P, 8, P]), M_).then_inc(S("at_p"), 1)

        def attn_lo(c):
            dve.wait_ge(S("at_hi"), c + 1)
            cs = slice(CH * c, CH * c + CH)
            TT(r2l[:, :, cs], B[0][:].rearrange("p (m t) -> p m t", m=KC), r2h[:, :, cs].bitcast(F32), SUB) \
                .then_inc(S("at_lo"), 1)

        dve.wait_ge(S("kb_in"), 16 * 12)
        nc.vector.memset(wl[:].rearrange("p a b c -> p (a b c)"), 0.0).then_inc(S("wl_zero"), 1)

        logits(0)
        for c in range(NCH):
            normalise(c)
            if c + 1 < NCH:
                logits(c + 1)
            attn_lo(c)

        with dve.Fori(0, 4) as i:
            for h in range(2):
                dve.wait_ge(S("slab_mm"), 2 * i + (N_B0 + h + 1))
                tile = t0[:, bass.ds(2 * i + h, 1), :].rearrange("p a t -> p (a t)")
                STT(tile, tile, 1.0, B[h][:], A_, M_).then_inc(S("tile_ev"), 1)
        dve.wait_ge(S("masks"), 1 + 2 + 3 + 3 + 3 + 3 + 4 * len(LEVELS))
        dve.wait_ge(S("spilled"), 160)
        with dve.Fori(0, 4) as i:
            for h in range(2):
                m = 2 * i + h
                t = {k_: v_[:] for k_, v_ in tmp.items()}

                def need(*names):
                    for n_ in names:
                        dve.wait_ge(S(n_), m + 2)

                def read(*names):
                    for n_ in names:
                        dve.wait_ge(S(n_), m + 1)

                need("k_sc")
                STT(t["kS"][:, 1:T], B[0][:, 0:T - 1], col("mu_k", m), t["kS"][:, 1:T], M_, A_) \
                    .then_inc(S("k_sh"), 1)
                need("tw")
                TS(t["ld"], t["tw"], -C_DEC, -C_DEC, M_, A_).then_inc(S("ld"), 1)
                need("ld")
                read("eWi")
                nc.vector.tensor_tensor_scan(t["cum"], scanm[:], t["ld"], 0.0, M_, A_).then_inc(S("cum"), 1)
                need("cum")
                read("eWx")
                TT(t["cx"], t["cum"], t["ld"], SUB).then_inc(S("cx"), 1)
                need("ta")
                TS(t["t"], t["ta"], pcol(H_KA, m), pcol(OH_KA, m), M_, A_)
                TS(t["aa"], t["ta"], 0.5, 0.5, M_, A_).then_inc(S("aa"), 1)
                need("aa", "k_sh")
                TT(t["kp"], t["kS"], t["t"], M_).then_inc(S("kp"), 1)
                STT(t["b0"], t["kS"], col("k_k", m), t["aa"], M_, M_)
                need("kp", "eWi")
                TT(kt[:, m, :], t["kp"], t["eWi"], M_)
                need("ss_mm")
                read("nrm")
                TS(t["ssm"], B[4][:], 1e-24, None, ALU.max).then_inc(S("ssm"), 1)
                need("r_sc")
                STT(t["rS"][:, 1:T], B[3][:, 0:T - 1], col("mu_r", m), t["rS"][:, 1:T], M_, A_) \
                    .then_inc(S("r_sh"), 1)
                need("r_sh")
                read("bon_mm")
                STT(t["p"], t["rS"], col("r_k", m), t["kp"], M_, M_).then_inc(S("p"), 1)
                need("nrm")
                nc.vector.reciprocal(t["inv"], t["nrm"]).then_inc(S("inv"), 1)
                need("inv")
                STT(t["ssm"], t["kS"], pcol(N_KK, m), t["inv"], M_, M_).then_inc(S("ax"), 1)
                TT(t["b0"], t["b0"], t["inv"], M_).then_inc(S("be"), 1)
                need("ax", "eWx")
                TT(ar[:, 0, m, :], t["ssm"], t["eWx"], M_).then_inc(S("at"), 1)
                need("be")
                TT(bt[:, m, :], t["b0"], t["eWi"], M_).then_inc(S("bt"), 1)
                need("r_sh", "eW")
                TT(ar[:, 1, m, :], t["rS"], t["eW"], M_)
                nc.vector.tensor_copy(wc[:, m, :], t["eW"][:, CH - 1:T:CH]).then_inc(S("wc"), 1)
                need("v_sc")
                STT(vb[:, m, 1:T], B[5][:, 0:T - 1], col("mu_v", m), vb[:, m, 1:T], M_, A_) \
                    .then_inc(S("v_sh"), 1)
                need("v_sh", "bon_mm")
                TT(bv[:, m, :], B[6][:], vb[:, m, :], M_).then_inc(S("bv"), 1)

        dve.wait_ge(S("spilled"), 240)
        for h in range(2):
            nc.vector.memset(U2["St"][h][:], 0.0).then_inc(S("st_zero"), 1)
        dve.wait_ge(S("st_zero"), 2)
        for h in range(2):
            dve.sem_inc(S(f"st{h}"), 1)
        with dve.Fori(0, NCH) as c:
            def m2(t_):
                return t_[:].rearrange("p m (e t) -> p m e t", e=2)

            for h in range(2):
                b = B[3 * h:3 * h + 3]
                dve.wait_ge(S(f"sc_mm{h}"), c * 2 + 1)
                TT(m2(U2["aab"][h]), bc2(v4(b[0])[:, :, 0:64]), mask4(m_strict), M_).then_inc(S(f"sc_ev{h}"), 1)
                TT(m2(U2["arb"][h]), bc2(v4(b[0])[:, :, 64:128]), mask4(m_incl), M_).then_inc(S(f"sc_ev{h}"), 1)
                dve.wait_ge(S(f"sc_mm{h}"), c * 2 + 2)
                TT(m2(U2["aak"][h]), bc2(v4(b[1])[:, :, 0:64]), mask4(m_strict), M_).then_inc(S(f"sc_ev{h}"), 1)
                TT(m2(U2["ark"][h]), bc2(v4(b[1])[:, :, 64:128]), mask4(m_incl), M_).then_inc(S(f"sc_ev{h}"), 1)
                dve.wait_ge(S(f"sc_ev{h}"), c * 5 + 1)
                TT(U2["AI"][h][:], U2["aab"][h][:], mask4f(ident), A_).then_inc(S(f"sc_ev{h}"), 1)
            for h in range(2):
                b = B[3 * h:3 * h + 3]
                dve.wait_ge(S(f"sc_ev{h}"), c * 5 + 5)
                TT(U2["XT"][h][:], U2["AI"][h][:], mask4f(m_1t), M_).then_inc(S(f"xt_ready{h}"), 1)
                dve.wait_ge(S(f"ai_mm{h}"), c + 1)
                TT(U2["X"][h][:], v4(b[2]), mask4f(m_1), M_).then_inc(S(f"x_ready{h}"), 1)
            for k in range(len(LEVELS)):
                for h in range(2):
                    dve.wait_ge(S(f"q_mm{h}"), c * 5 + (k + 1))
                    TT(U2["Qs"][h][:], v4(B[3 * h + 2]), mask4f(m_lev[k]), M_).then_inc(S(f"q_ev{h}"), 1)
                for h in range(2):
                    dve.wait_ge(S(f"d_mm{h}"), c * 5 + (k + 1))
                    if k < len(LEVELS) - 1:
                        TT(U2["X"][h][:], v4(B[3 * h + 1]), U2["X"][h][:], A_).then_inc(S(f"x_ready{h}"), 1)
                    else:
                        TT(U2["XT"][h][:], v4(B[3 * h + 1]), U2["XT"][h][:], A_).then_inc(S(f"xt_last{h}"), 1)

            def r4(t_):
                return t_.unsqueeze(2).to_broadcast([P, 4, CH])

            for h in range(2):
                ps = B[3 * h + 1][:, 0:256].rearrange("p (m i) -> p m i", m=4)
                dve.wait_ge(S(f"y_mm{h}"), c + 1)
                nc.vector.tensor_reduce(gn[:, h, 0, :], ps, AX, A_).then_inc(S(f"gn{h}"), 1)
                dve.wait_ge(S(f"gn{h}"), c * 5 + 1)
                TS(gn[:, h, 1, :], gn[:, h, 0, :], 1.0 / HD, None, M_).then_inc(S(f"gn{h}"), 1)
                dve.wait_ge(S(f"gn{h}"), c * 5 + 2)
                TT(U2["Y"][h][:], ps, r4(gn[:, h, 1, :]), SUB).then_inc(S(f"yc{h}"), 1)
                ds = B[3 * h][:, 0:256].rearrange("p (m i) -> p m i", m=4)
                dve.wait_ge(S(f"dS_mm{h}"), c + 2)
                TT(U2["St"][h][:], ds, U2["St"][h][:], A_).then_inc(S(f"gn{h}"), 1)
                dve.wait_ge(S(f"gn{h}"), c * 5 + 3)
                TT(U2["St"][h][:], U2["St"][h][:],
                   wc[:, 4 * h:4 * h + 4, bass.ds(c, 1)].to_broadcast([P, 4, CH]), M_).then_inc(S(f"st{h}"), 1)
            for h in range(2):
                dve.wait_ge(S(f"ysq{h}"), c + 1)
                nc.vector.tensor_reduce(gn[:, h, 0, :], U2["Yt"][h][:], AX, A_).then_inc(S(f"gn{h}"), 1)
                dve.wait_ge(S(f"gn{h}"), c * 5 + 4)
                TS(gn[:, h, 1, :], gn[:, h, 0, :], 1.0 / HD, GN_EPS, M_, A_).then_inc(S(f"gn{h}"), 1)
                dve.wait_ge(S(f"gn{h}"), c * 5 + 5)
                nc.vector.reciprocal(gn[:, h, 2, :], gn[:, h, 1, :]).then_inc(S(f"yv{h}"), 1)
            for h in range(2):
                dve.wait_ge(S(f"yr{h}"), c + 1)
                TT(U2["Y"][h][:], U2["Y"][h][:], r4(gn[:, h, 3, :]), M_).then_inc(S(f"yn{h}"), 1)
            for h in range(2):
                tk = bass.ds(c * CH, CH)
                dve.wait_ge(S(f"yt_mm{h}"), c + 1)
                TT(vb[:, 4 * h:4 * h + 4, tk], B[3 * h + 2][:, 0:256].rearrange("p (m i) -> p m i", m=4),
                   r4(par[:, COL["ln_w"] + 4 * h:COL["ln_w"] + 4 * h + 4]), M_).then_inc(S(f"y_read{h}"), 1)

        dve.wait_ge(S("y_read0"), 9)
        dve.wait_ge(S("y_read1"), 9)
        for m in range(KC + 1):
            if m < KC:
                dve.wait_ge(S("y_sum"), m + 1)
                dve.wait_ge(S("g_mm"), m + 1)
                if m >= 2:
                    dve.wait_ge(S("x_lo"), SP_Y + m - 1)
                STT(hx[:, m % 2, :], vb[:, m, :], col("ln_b", m), B[4 + m % 2][:], A_, M_).then_inc(S("x_f"), 1)
            if m >= 1:
                remainder(m - 1, SP_Y, r1h, r1l)
        dve.wait_ge(S("gates_in"), 32)
        for m in range(KC):
            dve.wait_ge(S("slab_mm"), N_B1 + m + 1)
            STT(t1b[:, m, :], t1b[:, m, :], 1.0, B[m % 2][:], A_, M_).then_inc(S("tile_ev"), 1)
            dve.wait_ge(S("tile_ev"), E_B1 + m + 1)
            if m >= 2:
                dve.wait_ge(S("x_lo"), SP_M + m - 1)
            TT(hx[:, m % 2, :], t1b[:, m, :], m0b[:, m, :], A_).then_inc(S("x_f"), 1)
            remainder(m, SP_M, r2h, r2l)

        rms_rec(N2, B[7])
        dve.wait_ge(S("x_in"), 32)
        for kc in range(KC):
            STT(mix[:, kc, :], mix[:, kc, :], col("post_mix", kc), rst[:, 1, :], M_, M_).then_inc(S("step1"), 1)
            dve.wait_ge(S("step1"), kc + 1)
            TT(xr[:, kc, :], xr[:, kc, :], mix[:, kc, :], A_).then_inc(S("x1_f"), 1)
        dve.wait_ge(S("x1_f"), 8)
        rms_rec(N3, B[6])
        norm_split(xr, "pre_ffn", SP_F, r1h, r1l)
        dve.wait_ge(S("spilled"), 256)
        with dve.Fori(0, 16) as i:
            for h in range(2):
                j = 2 * i + h
                dve.wait_ge(S(f"f_relu{h}"), i + 1)
                STT(hx[:, h, :], B[h][:], 0.0, sqt[:, h, :], ALU.max, M_).then_inc(S("tile_ev"), 1)
                dve.wait_ge(S("tile_ev"), 2 * i + (E_UP + h + 1))
                dve.wait_ge(S(f"f_hi{h}"), i + 1)
                TT(fl[:, j, :], hx[:, h, :], fh[:, j, :].bitcast(F32), SUB).then_inc(S(f"f_lo{h}"), 1)
                dve.wait_ge(S(f"f_lo{h}"), i + 2)
                dve.sem_inc(S("f_lo"), 1)
        rms_rec(N4, B[7])
        dve.wait_ge(S("x_in"), 48)
        dve.wait_ge(S("tile_ev"), E_ALL)
        for kc in range(KC - POOL_OUT):
            TT(ob[:, kc, :], ob[:, kc, :], rst[:, 1, :], M_).then_inc(S("step1"), 1)
            dve.wait_ge(S("step1"), KC + kc + 1)
            TT(ob[:, kc, :], ob[:, kc, :], x1[:, kc, :], A_).then_inc(S("o_ready"), 1)

    block.__exit__(None, None, None)


def relative_buckets():
    rel = np.arange(-(CH * 2 - 1), CH)
    nb, max_exact = 16, 8
    ret = (rel > 0).astype(np.int32) * nb
    n = np.abs(rel)
    ratio = np.maximum(n, 1).astype(np.float32) / np.float32(max_exact)
    large = max_exact + (np.log(ratio) / np.float32(np.log(128 / max_exact)) * (nb - max_exact)).astype(np.int32)
    return ret + np.where(n < max_exact, n, np.minimum(large, nb - 1))


def kernel(x, w_in, rwkv_shift, pre_mix_g, post_mix_g, pre_ffn_g, post_ffn_g, attn_sinks, rel_bias, w0,
           w_decay_up, a0, w_aaa_up, w_gate_up, k_k, k_a, r_k, ln_x_w, ln_x_b, gate_bias, w_branch, w_out,
           w_ff_up, w_ff_down):
    import concourse.bacc as bacc
    from concourse.bass_utils import run_bass_kernel_spmd

    def tab(v):
        return np.asarray(v).reshape(KC, P).T

    mu = np.asarray(rwkv_shift)[0]
    lmu = np.zeros((3 * P,), np.float32)
    lmu[:288] = mu[3 * D:]
    gb = np.asarray(gate_bias)[0]
    cols = np.concatenate([tab(v) for v in (
        pre_mix_g[0], post_mix_g[0], pre_ffn_g[0], post_ffn_g[0], mu[0:D], mu[D:2 * D], mu[2 * D:3 * D],
        w0[0], a0[0], k_k[0], k_a[0], r_k[0], ln_x_w[0], ln_x_b[0], gb[0], gb[1])] + [lmu.reshape(3, P).T], axis=1)
    head = np.arange(8)
    hmap = np.stack([4 * (head // 2) + 2 * e + head % 2 for e in range(2)])
    sinks = np.repeat(np.asarray(attn_sinks)[0][hmap], CH, axis=0)
    onehot = np.zeros((32, BETA), np.float32)
    onehot[relative_buckets(), np.arange(BETA - 1)] = 1.0
    arrays = {
        "xT": np.asarray(x)[0].T.reshape(KC, P, T).transpose(1, 0, 2),
        "w_in": w_in[0], "cols": cols, "sinks": sinks, "onehot": onehot, "rel_bias": rel_bias,
        "wdec": w_decay_up[0], "waaa": w_aaa_up[0], "wgate": w_gate_up[0], "w_br": w_branch[0],
        "w_out": w_out[0], "w_up": w_ff_up[0], "w_down": w_ff_down[0],
    }
    arrays = {k: np.ascontiguousarray(v) for k, v in arrays.items()}
    nc = bacc.Bacc("TRN2", target_bir_lowering=False, num_devices=1)
    args = [nc.dram_tensor(k, list(v.shape), F32, kind="ExternalInput").ap() for k, v in arrays.items()]
    out = nc.dram_tensor("out", [P, KC, T], F32, kind="ExternalOutput").ap()
    build(nc, *args, out)
    r = run_bass_kernel_spmd(nc, [arrays], core_ids=[0])
    y = r.results[0]["out"]
    return y.transpose(1, 0, 2).reshape(D, T).T[None]
```
